# Optimizing a Trainium2 kernel written in Bass

```python
import math
import jax, jax.numpy as jnp
from jax import lax
import numpy as np

D_MODEL = 1024
BATCH = 1
SEQ = 1024
DEPTH = 1

CHUNK = 64
Q_BLOCK = 128
ROPE_THETA = 500000.0
D_MIX = D_MODEL
MLA_HEADS = 8
MLA_NOPE_DIM = 64
MLA_ROPE_DIM = 32
MLA_V_DIM = 64
MLA_QK_DIM = MLA_NOPE_DIM + MLA_ROPE_DIM
Q_RANK = 384
KV_RANK = 256
DIFF_HEADS = 4
DIFF_HEAD_DIM = 64
DIFF_ROPE_DIM = DIFF_HEAD_DIM // 4
IN_WIDTHS = (Q_RANK, KV_RANK, MLA_ROPE_DIM,
             DIFF_HEADS * 2 * DIFF_HEAD_DIM, DIFF_HEADS * 2 * DIFF_HEAD_DIM, DIFF_HEADS * 2 * DIFF_HEAD_DIM)
IN_COLS = sum(IN_WIDTHS)
N_EXPERTS = 32
TOP_K = 4
EXPERT_DFF = D_MODEL
SWIGLU_LIMIT = 7.0
SWIGLU_ALPHA = 1.702
MOE_BLOCK = 128
N_MOD = 6

kernel_name = "hybrid_mla_diffattn_moe_adaln_block"

def rms_norm(x, g, eps=1e-6):
    xf = x.astype(jnp.float32)
    y = xf * lax.rsqrt(jnp.mean(xf * xf, axis=-1, keepdims=True) + eps)
    return (y * g.astype(jnp.float32)).astype(x.dtype)

def apply_rope(x, positions, rot_dim):
    half = rot_dim // 2
    inv_freq = ROPE_THETA ** (-jnp.arange(half, dtype=jnp.float32) / half)
    ang = positions.astype(jnp.float32)[:, :, None] * inv_freq
    ang = ang.reshape(ang.shape[:2] + (1,) * (x.ndim - 3) + (half,))
    cos, sin = jnp.cos(ang), jnp.sin(ang)
    xr = x[..., :rot_dim].astype(jnp.float32)
    x1, x2 = xr[..., :half], xr[..., half:]
    rot = jnp.concatenate([x1 * cos - x2 * sin, x2 * cos + x1 * sin], axis=-1).astype(x.dtype)
    return jnp.concatenate([rot, x[..., rot_dim:]], axis=-1)

def _split_query_blocks(q):
    *lead, s, d = q.shape
    return jnp.moveaxis(q.reshape(*lead, s // Q_BLOCK, Q_BLOCK, d), -3, 0)

def _merge_query_blocks(o):
    o = jnp.moveaxis(o, 0, -3)
    *lead, nb, qb, d = o.shape
    return o.reshape(*lead, nb * qb, d)

def _chunk_causal_mask(blk, s):
    q_idx = blk * Q_BLOCK + jnp.arange(Q_BLOCK)
    k_idx = jnp.arange(s)
    return (k_idx[None, :] // CHUNK) <= (q_idx[:, None] // CHUNK)

def mla_attention(q, k, v):
    s = q.shape[-2]
    scale = MLA_QK_DIM ** -0.5

    def one_block(args):
        qb, blk = args
        sc = jnp.einsum('bhqd,bhkd->bhqk', qb, k).astype(jnp.float32) * scale
        sc = jnp.where(_chunk_causal_mask(blk, s), sc, -jnp.inf)
        p = jax.nn.softmax(sc, axis=-1).astype(v.dtype)
        return jnp.einsum('bhqk,bhkd->bhqd', p, v)

    out = lax.map(one_block, (_split_query_blocks(q), jnp.arange(s // Q_BLOCK)))
    return _merge_query_blocks(out)

def diff_attention(q, k, v, lam):
    s = q.shape[-2]
    scale = DIFF_HEAD_DIM ** -0.5

    def one_block(args):
        qb, blk = args
        sc = jnp.einsum('bhcqd,bhckd->bhcqk', qb, k).astype(jnp.float32) * scale
        sc = jnp.where(_chunk_causal_mask(blk, s), sc, -jnp.inf)
        p = jax.nn.softmax(sc, axis=-1)
        w = (p[:, :, 0] - lam * p[:, :, 1]).astype(v.dtype)
        return jnp.einsum('bhqk,bhkd->bhqd', w, v)

    out = lax.map(one_block, (_split_query_blocks(q), jnp.arange(s // Q_BLOCK)))
    return _merge_query_blocks(out)

def hybrid_mixer(h, positions, w_in, g_q_norm, w_uq, g_kv_norm, w_ukv,
                 lambda_q1, lambda_k1, lambda_q2, lambda_k2, g_subln, w_out, lambda_init):
    b, s, _ = h.shape
    proj = h @ w_in
    cuts = list(np.cumsum(IN_WIDTHS)[:-1])
    c_q, c_kv, k_pe, dq, dk, dv = jnp.split(proj, cuts, axis=-1)

    q = (rms_norm(c_q, g_q_norm) @ w_uq).reshape(b, s, MLA_HEADS, MLA_QK_DIM)
    q = jnp.concatenate([q[..., :MLA_NOPE_DIM],
                         apply_rope(q[..., MLA_NOPE_DIM:], positions, MLA_ROPE_DIM)], axis=-1)
    kv = (rms_norm(c_kv, g_kv_norm) @ w_ukv).reshape(b, s, MLA_HEADS, MLA_NOPE_DIM + MLA_V_DIM)
    k_nope, v_m = kv[..., :MLA_NOPE_DIM], kv[..., MLA_NOPE_DIM:]
    k_pe = apply_rope(k_pe[:, :, None, :], positions, MLA_ROPE_DIM)
    k = jnp.concatenate([k_nope, jnp.broadcast_to(k_pe, (b, s, MLA_HEADS, MLA_ROPE_DIM))], axis=-1)
    o_mla = mla_attention(q.transpose(0, 2, 1, 3), k.transpose(0, 2, 1, 3), v_m.transpose(0, 2, 1, 3))
    o_mla = o_mla.transpose(0, 2, 1, 3).reshape(b, s, MLA_HEADS * MLA_V_DIM)

    dq = apply_rope(dq.reshape(b, s, DIFF_HEADS, 2, DIFF_HEAD_DIM), positions, DIFF_ROPE_DIM)
    dk = apply_rope(dk.reshape(b, s, DIFF_HEADS, 2, DIFF_HEAD_DIM), positions, DIFF_ROPE_DIM)
    dv = dv.reshape(b, s, DIFF_HEADS, 2 * DIFF_HEAD_DIM).transpose(0, 2, 1, 3)
    lam = (jnp.exp(jnp.sum(lambda_q1.astype(jnp.float32) * lambda_k1.astype(jnp.float32)))
           - jnp.exp(jnp.sum(lambda_q2.astype(jnp.float32) * lambda_k2.astype(jnp.float32)))
           + lambda_init)
    o_diff = diff_attention(dq.transpose(0, 2, 3, 1, 4), dk.transpose(0, 2, 3, 1, 4), dv, lam)
    o_diff = rms_norm(o_diff, g_subln, eps=1e-5) * (1.0 - lambda_init)
    o_diff = o_diff.transpose(0, 2, 1, 3).reshape(b, s, DIFF_HEADS * 2 * DIFF_HEAD_DIM)

    return jnp.concatenate([o_mla, o_diff], axis=-1) @ w_out

def clamped_swiglu(gu):
    gate, up = gu[..., ::2], gu[..., 1::2]
    gate = jnp.minimum(gate, SWIGLU_LIMIT)
    up = jnp.clip(up, -SWIGLU_LIMIT, SWIGLU_LIMIT)
    return gate * jax.nn.sigmoid(SWIGLU_ALPHA * gate) * (up + 1.0)

def moe_ffn(t, w_router, b_router, w_gate_up, b_gate_up, w_down, b_down):
    n, d = t.shape
    logits = (t @ w_router + b_router).astype(jnp.float32)
    top_val, top_idx = lax.top_k(logits, TOP_K)
    top_w = jax.nn.softmax(top_val, axis=-1)
    a = n * TOP_K
    flat_e = top_idx.reshape(a)
    flat_tok = jnp.arange(a, dtype=jnp.int32) // TOP_K
    flat_w = top_w.reshape(a)
    order = jnp.argsort(flat_e)
    sorted_e = flat_e[order]
    counts = jnp.bincount(flat_e, length=N_EXPERTS)
    padded = (counts + MOE_BLOCK - 1) // MOE_BLOCK * MOE_BLOCK
    start_sorted = jnp.cumsum(counts) - counts
    end_padded = jnp.cumsum(padded)
    start_padded = end_padded - padded
    slot = start_padded[sorted_e] + jnp.arange(a) - start_sorted[sorted_e]
    p = a + N_EXPERTS * MOE_BLOCK
    slot_tok = jnp.zeros((p,), jnp.int32).at[slot].set(flat_tok[order])
    slot_w = jnp.zeros((p,), jnp.float32).at[slot].set(flat_w[order])
    nblk = p // MOE_BLOCK
    blk_expert = jnp.minimum(
        jnp.searchsorted(end_padded, jnp.arange(nblk) * MOE_BLOCK, side='right'), N_EXPERTS - 1)

    def one_block(args):
        tok, wgt, e = args
        xb = t[tok]
        act = clamped_swiglu(xb @ w_gate_up[e] + b_gate_up[e])
        y = act @ w_down[e] + b_down[e]
        return y * wgt[:, None].astype(y.dtype)

    y = lax.map(one_block, (slot_tok.reshape(nblk, MOE_BLOCK),
                            slot_w.reshape(nblk, MOE_BLOCK), blk_expert))
    return jnp.zeros_like(t).at[slot_tok].add(y.reshape(p, d))

def setup_inputs(seed: int = 0) -> dict:
    key = jax.random.key(seed)
    ks = jax.random.split(key, 32)
    f32 = jnp.float32
    nrm = lambda k, shape, scale: jax.random.normal(k, shape, f32) * scale
    gain = lambda k, shape: 1.0 + 0.02 * jax.random.normal(k, shape, f32)
    L = DEPTH
    offset = jax.random.randint(ks[2], (BATCH, 1), 0, 4096, dtype=jnp.int32)
    positions = offset + jnp.arange(SEQ, dtype=jnp.int32)[None, :]
    return {
        "x": nrm(ks[0], (BATCH, SEQ, D_MODEL), 1.0),
        "c": nrm(ks[1], (BATCH, D_MODEL), 1.0),
        "positions": positions,
        "w_ada": nrm(ks[3], (L, D_MODEL, N_MOD * D_MODEL), 0.5 * D_MODEL ** -0.5),
        "b_ada": nrm(ks[4], (L, N_MOD * D_MODEL), 0.01),
        "g_norm1": gain(ks[5], (L, D_MODEL)),
        "w_in": nrm(ks[6], (L, D_MODEL, IN_COLS), D_MODEL ** -0.5),
        "g_q_norm": gain(ks[7], (L, Q_RANK)),
        "w_uq": nrm(ks[8], (L, Q_RANK, MLA_HEADS * MLA_QK_DIM), Q_RANK ** -0.5),
        "g_kv_norm": gain(ks[9], (L, KV_RANK)),
        "w_ukv": nrm(ks[10], (L, KV_RANK, MLA_HEADS * (MLA_NOPE_DIM + MLA_V_DIM)), KV_RANK ** -0.5),
        "lambda_q1": nrm(ks[11], (L, DIFF_HEAD_DIM), 0.1),
        "lambda_k1": nrm(ks[12], (L, DIFF_HEAD_DIM), 0.1),
        "lambda_q2": nrm(ks[13], (L, DIFF_HEAD_DIM), 0.1),
        "lambda_k2": nrm(ks[14], (L, DIFF_HEAD_DIM), 0.1),
        "g_subln": gain(ks[15], (L, 2 * DIFF_HEAD_DIM)),
        "w_out": nrm(ks[16], (L, D_MIX, D_MODEL), D_MIX ** -0.5),
        "g_norm2": gain(ks[17], (L, D_MODEL)),
        "w_router": nrm(ks[18], (L, D_MODEL, N_EXPERTS), D_MODEL ** -0.5),
        "b_router": nrm(ks[19], (L, N_EXPERTS), 0.01),
        "w_gate_up": nrm(ks[20], (L, N_EXPERTS, D_MODEL, 2 * EXPERT_DFF), D_MODEL ** -0.5),
        "b_gate_up": nrm(ks[21], (L, N_EXPERTS, 2 * EXPERT_DFF), 0.01),
        "w_down": nrm(ks[22], (L, N_EXPERTS, EXPERT_DFF, D_MODEL), EXPERT_DFF ** -0.5),
        "b_down": nrm(ks[23], (L, N_EXPERTS, D_MODEL), 0.01),
        "g_final": gain(ks[24], (D_MODEL,)),
    }

def reference(x, c, positions, w_ada, b_ada, g_norm1, w_in, g_q_norm, w_uq, g_kv_norm, w_ukv,
              lambda_q1, lambda_k1, lambda_q2, lambda_k2, g_subln, w_out, g_norm2,
              w_router, b_router, w_gate_up, b_gate_up, w_down, b_down, g_final):
    b, s, d = x.shape
    for l in range(DEPTH):
        lambda_init = 0.8 - 0.6 * math.exp(-0.3 * l)
        mod = jax.nn.silu(c) @ w_ada[l] + b_ada[l]
        sh1, sc1, gt1, sh2, sc2, gt2 = jnp.split(mod[:, None, :], N_MOD, axis=-1)
        h = rms_norm(x, g_norm1[l]) * (1.0 + sc1) + sh1
        mix = hybrid_mixer(h, positions, w_in[l], g_q_norm[l], w_uq[l], g_kv_norm[l], w_ukv[l],
                           lambda_q1[l], lambda_k1[l], lambda_q2[l], lambda_k2[l], g_subln[l],
                           w_out[l], lambda_init)
        x = x + gt1 * mix
        h = rms_norm(x, g_norm2[l]) * (1.0 + sc2) + sh2
        y = moe_ffn(h.reshape(b * s, d), w_router[l], b_router[l], w_gate_up[l], b_gate_up[l],
                    w_down[l], b_down[l]).reshape(b, s, d)
        x = x + gt2 * y
    return rms_norm(x, g_final)


_drawn_inputs = setup_inputs


def setup_inputs(seed=0):
    import zlib

    import numpy as np

    out = dict(_drawn_inputs(seed))
    spreads = {}
    factors = {'b_ada': 3.186,
     'g_norm1': 6.866,
     'g_q_norm': 8.0,
     'g_kv_norm': 8.0,
     'lambda_k1': 5.608,
     'lambda_q2': 5.886,
     'lambda_k2': 7.379,
     'g_subln': 7.796,
     'g_norm2': 3.646,
     'b_router': 4.73,
     'b_gate_up': 22.617,
     'b_down': 64.0,
     'g_final': 8.46}
    for name, (base, spread) in spreads.items():
        noise = np.random.default_rng([zlib.crc32(name.encode()), seed]).standard_normal(out[name].shape)
        drawn = base * np.exp(spread * noise) if base else spread * noise
        out[name] = __import__('jax').numpy.asarray(drawn.astype(out[name].dtype))
    for name, factor in factors.items():
        out[name] = (out[name] * factor).astype(out[name].dtype)
    return out
```

```python
from contextlib import ExitStack

import numpy as np
import concourse.bass as bass
from concourse import mybir

F32 = mybir.dt.float32
I32 = mybir.dt.int32
U32 = mybir.dt.uint32
ALU = mybir.AluOpType
ACT = mybir.ActivationFunctionType
AX_X = mybir.AxisListType.X

P = 128
D = 1024
KD = D // P
S = 1024
NT = S // P
HM, NOPE, ROPE, DV_M = 8, 64, 32, 64
QK = NOPE + ROPE
QR, KVR = 384, 256
KQ, KKV = QR // P, KVR // P
HD, DH = 4, 64
DROPE = DH // 4
FM, FD = ROPE // 2, DROPE // 2
THETA = 500000.0
CHUNK = 64
NCOL = QR + KVR + ROPE + 3 * HD * 2 * DH
C_DQ = QR + KVR + ROPE
NE, TOPK = 32, 4
LIMIT, SWISH = 7.0, 1.702
LAMBDA_INIT = 0.8 - 0.6
CAP = 256
SIZES = (112, 128, 144, 160, 176, 256)
MAXPASS = NE + S * TOPK // CAP
NPASS_ROWS = 128
DUMMY = S
NROW = S + CAP
SCALE_M = float(QK) ** -0.5
SCALE_D = float(DH) ** -0.5
MASKED = -1.0e30
MAGIC = 12582912.0
TWO_PI = 2 * np.pi
PI_1 = 6.28125
PI_2 = float(np.float32(round((TWO_PI - PI_1) * 2 ** 21) / 2 ** 21))
PI_3 = float(TWO_PI - PI_1 - PI_2)
PI_IN = 3.1415925

R_C, R_BADA, R_G1, R_G2, R_GQ, R_GKV, R_SUB = 0, 8, 56, 64, 72, 75, 77
NR = 78


def carve(arena, at, *shape):
    n = int(np.prod(shape))
    view = arena[:, at:at + n]
    if len(shape) == 2:
        view = view.rearrange("p (a b) -> p a b", a=shape[0])
    elif len(shape) == 3:
        view = view.rearrange("p (a b c) -> p a b c", a=shape[0], b=shape[1])
    return view, at + n


class Chain:

    def __init__(self, eng, sem, base):
        self.eng, self.sem, self.base, self.done = eng, sem, base, 0

    def __call__(self, ins):
        self.done += 1
        ins.then_inc(self.sem, 1)
        self.eng.wait_ge(self.sem, self.base + self.done)


def attention_plan():
    units = [(i, u) for i in range(NT) for u in range(HM + HD)]
    tail = {1: "oT", 3: "mix0", 5: "mix1", 7: "xT", 9: "router", 11: "rank"}
    steps, group = [], 0

    def put(kind, i, u):
        nonlocal group
        steps.append((kind, i, u, group))
        if kind == "T":
            group += i // 4 + 1
        elif kind in ("oT", "xT"):
            group += 2

    put("S", 0, 0)
    for n, (i, u) in enumerate(units):
        if n + 1 < len(units):
            put("S", *units[n + 1])
        put("T", i, u)
        if n:
            put("PV", *units[n - 1])
        if i and u in tail:
            put(tail[u], i - 1, 0)
    put("PV", *units[-1])
    for kind in ("oT", "mix0", "mix1", "xT", "router", "rank"):
        put(kind, NT - 1, 0)
    return steps


def item(i, u):
    return 16 * i + (u if u < HM else HM + 2 * (u - HM))


def unit_of(n):
    i, r = divmod(n, 16)
    return i, (r if r < HM else HM + (r - HM) // 2)


def hybrid_block(nc, x, c, positions, w_ada, b_ada, g_norm1, w_in, g_q_norm, w_uq, g_kv_norm, w_ukv,
                 lambda_q1, lambda_k1, lambda_q2, lambda_k2, g_subln, w_out, g_norm2,
                 w_router, b_router, w_gate_up, b_gate_up, w_down, b_down, g_final, out):
    x2d = x.rearrange("b s d -> (b s) d")
    out2d = out.rearrange("b s d -> (b s) d")
    w_ada_v = w_ada[0].rearrange("(k p) n -> p k n", p=P)
    w_in_v = w_in[0].rearrange("(k p) n -> p k n", p=P)
    w_gu_v = w_gate_up.rearrange("l e (k p) n -> p (l e) k n", p=P)
    w_dn_v = w_down.rearrange("l e (k p) n -> p (l e) k n", p=P)

    q_scr = nc.dram_tensor("q_scr", (NT, P, HM * P), F32).ap()
    dq_scr = nc.dram_tensor("dq_scr", (NT, P, HD * P), F32).ap()
    x_hat = nc.dram_tensor("x_hat", (NROW, D), F32).ap()
    x_acc = nc.dram_tensor("x_acc", (NROW, D), F32).ap()
    table = nc.dram_tensor("table", (NE * S, 2), I32).ap()
    gt1_scr = nc.dram_tensor("gt1_scr", (P, D), F32).ap()
    bias_scr = nc.dram_tensor("bias_scr", (P, 3 * NE * KD), F32).ap()
    passes = nc.dram_tensor("passes", (NPASS_ROWS, 4), I32).ap()

    with ExitStack() as ctx:
        def sem(name):
            return ctx.enter_context(nc.semaphore(name))

        arena = ctx.enter_context(nc.sbuf_tensor("arena", [P, 53100], F32))
        bank = [ctx.enter_context(nc.psum_tensor(f"bank{b}", [P, 512], F32)) for b in range(8)]

        at = 0
        ident, at = carve(arena, at, P)
        ones, at = carve(arena, at, P)
        before, at = carve(arena, at, P)
        iota_e, at = carve(arena, at, NE)
        iota_p, at = carve(arena, at, 1)
        cols, at = carve(arena, at, 80)
        mods, at = carve(arena, at, 48)
        a1, at = carve(arena, at, KD)
        a2, at = carve(arena, at, KD)
        gsub, at = carve(arena, at, 1)
        neg_lam, at = carve(arena, at, 1)
        cos_t, at = carve(arena, at, NT, FM + FD)
        sin_t, at = carve(arena, at, NT, FM + FD)
        small, at = carve(arena, at, 32)
        mhalf, at = carve(arena, at, TOPK)
        base = at
        sh1, sh2, gt2 = mods[:, 0:8], mods[:, 24:32], mods[:, 40:48]

        kT, at = carve(arena, base, HM, S)
        v_m, at = carve(arena, at, NT, HM * DV_M)
        dkT, at = carve(arena, at, HD, S)
        v_d, at = carve(arena, at, NT, HD * 2 * DH)
        work = at
        NRING = 5
        ada = [carve(arena, base + r * KD * 512, KD, 512)[0] for r in range(NRING)]

        win, at = carve(arena, work, KD, NCOL)
        wuq, at = carve(arena, at, KQ, HM * QK)
        wukv, at = carve(arena, at, KKV, HM * (NOPE + DV_M))
        p1 = at
        rows, at = carve(arena, p1, P)
        posi, at = carve(arena, at, P)
        posf, at = carve(arena, at, P)
        pos_c, at = carve(arena, at, NT)
        freq, at = carve(arena, at, FM + FD)
        ang, at = carve(arena, at, NT, FM + FD)
        turns, at = carve(arena, at, NT, FM + FD)
        wide, at = carve(arena, at, NT, FM + FD)
        lam4, at = carve(arena, at, 4, DH)
        brow, at = carve(arena, at, 2, 256)
        drow, at = carve(arena, at, 2, P)
        scb, at = carve(arena, at, KD, P)
        bada_b, at = carve(arena, at, D)
        tinit, at = carve(arena, at, 256, 2)
        zero, at = carve(arena, at, D)
        gt1b, at = carve(arena, at, D)
        bias_e, at = carve(arena, at, 3, NE * KD)
        posi = posi.bitcast(I32)
        tinit = tinit.bitcast(I32)
        sig = small[:, 0:8]
        silu = small[:, 8:16]
        lam_s = small[:, 16:24]
        assert at <= 53100

        s_cst, s_rows, s_pos, s_lamld, s_brow, s_bada = map(sem, ("s_cst", "s_rows", "s_pos", "s_lamld", "s_brow", "s_bada"))
        s_ada = [sem(f"s_ada{r}") for r in range(NRING)]
        s_win, s_colT, s_cols, s_sig, s_silu, s_posf, s_posT = map(
            sem, ("s_win", "s_colT", "s_cols", "s_sig", "s_silu", "s_posf", "s_posT"))
        s_adau, s_gt1, s_bT, s_lam, s_lame, s_ang, s_sin, s_v0, s_tab, s_zero = map(
            sem, ("s_adau", "s_gt1", "s_bT", "s_lam", "s_lame", "s_ang", "s_sin", "s_v0", "s_tab", "s_zero"))
        s_keep = sem("s_keep")
        NADA = 12

        with nc.Block() as block:
            @block.sync
            def _(sp):
                for row, src, n in ((R_C, c[0], KD), (R_BADA, b_ada[0], 48), (R_G1, g_norm1[0], KD),
                                    (R_G2, g_norm2[0], KD), (R_GQ, g_q_norm[0], KQ), (R_GKV, g_kv_norm[0], KKV),
                                    (R_SUB, g_subln[0], 1)):
                    sp.dma_start(rows[row:row + n, :], src.rearrange("(r p) -> r p", p=P)).then_inc(s_rows, 16)
                sp.dma_start(posi[0:NT, :], positions.rearrange("b (t p) -> (b t) p", p=P)).then_inc(s_pos, 16)
                for q in range(4):
                    sp.dma_start(ada[q], w_ada_v[:, :, q * 512:(q + 1) * 512]).then_inc(s_ada[q], 16)
                for q, src in enumerate((lambda_q1, lambda_k1, lambda_q2, lambda_k2)):
                    sp.dma_start(lam4[:, q, :], src.broadcast_to((P, DH))).then_inc(s_lamld, 16)
                sp.dma_start(bada_b, b_ada[0:1, 2 * D:3 * D].broadcast_to((P, D))).then_inc(s_bada, 16)
                for h in range(2):
                    sp.dma_start(brow[:, h, :], b_gate_up[0, 16 * h:16 * h + 16].rearrange(
                        "e (j n) -> (e j) n", j=KD)).then_inc(s_brow, 16)
                    sp.dma_start(drow[:, h, :], b_down[0, 16 * h:16 * h + 16].rearrange(
                        "e (j n) -> (e j) n", j=KD)).then_inc(s_brow, 16)
                sp.dma_start(win, w_in_v).then_inc(s_win, 16)
                sp.dma_start(wuq, w_uq[0].rearrange("(k p) n -> p k n", p=P)).then_inc(s_win, 16)
                sp.dma_start(wukv, w_ukv[0].rearrange("(k p) n -> p k n", p=P)).then_inc(s_win, 16)
                for q in range(4, NADA):
                    if q >= NRING:
                        sp.wait_ge(s_adau, q - NRING + 1)
                    sp.dma_start(ada[q % NRING], w_ada_v[:, :, q * 512:(q + 1) * 512]).then_inc(s_ada[q % NRING], 16)
                sp.wait_ge(s_cst, 7)
                sp.dma_start(table.rearrange("(p j) w -> p j w", p=P), tinit).then_inc(s_tab, 16)
                for r in range(S, NROW, P):
                    sp.dma_start(x_hat[r:r + P, :], zero).then_inc(s_tab, 16)
                    sp.dma_start(x_acc[r:r + P, :], zero).then_inc(s_tab, 16)
                sp.wait_ge(s_keep, 2)
                sp.dma_start(gt1_scr, gt1b).then_inc(s_tab, 16)
                sp.dma_start(bias_scr, bias_e.rearrange("p a n -> p (a n)")).then_inc(s_tab, 16)
                sp.wait_ge(s_tab, 16 * (3 + 2 * CAP // P))
                sp.wait_ge(s_win, 48)

            @block.gpsimd
            def _(pool):
                pool.memset(ident, 0.0).then_inc(s_cst, 1)
                pool.memset(ones, 1.0).then_inc(s_cst, 1)
                pool.wait_ge(s_cst, 2)
                pool.affine_select(out=ident, in_=ident, compare_op=ALU.not_equal, fill=1.0, base=0,
                                   pattern=[[-1, P]], channel_multiplier=1).then_inc(s_cst, 1)
                pool.affine_select(out=before, in_=ones, compare_op=ALU.is_gt, fill=0.0, base=0,
                                   pattern=[[1, P]], channel_multiplier=-1).then_inc(s_cst, 1)
                for f in range(FM + FD):
                    n, half = (f, FM) if f < FM else (f - FM, FD)
                    pool.memset(freq[:, f:f + 1], float(np.float32(THETA ** (-n / half))))
                pool.memset(mhalf, -0.5)
                pool.iota(iota_e, [[1, NE]], 0, 0, allow_small_or_imprecise_dtypes=True)
                pool.iota(iota_p, [[1, 1]], 0, 1, allow_small_or_imprecise_dtypes=True).then_inc(s_cst, 1)
                pool.iota(tinit[:, :, 0], [[1, CAP]], DUMMY, 0).then_inc(s_cst, 1)
                pool.memset(zero, 0.0)
                pool.memset(tinit[:, :, 1], 0).then_inc(s_cst, 1)

            @block.tensor
            def _(pe):
                pe.wait_ge(s_cst, 4)
                pe.wait_ge(s_rows, 16 * 7)
                pe.transpose(bank[0][:, 0:NR], rows[0:NR, :], ident[0:NR, 0:NR]).then_inc(s_colT, 1)
                pe.wait_ge(s_posf, 1)
                pe.transpose(bank[0][:, 128:128 + NT], posf[0:NT, :], ident[0:NT, 0:NT]).then_inc(s_posT, 1)
                pe.wait_ge(s_brow, 64)
                for h in range(2):
                    pe.transpose(bank[4][:, h * P:(h + 1) * P], brow[:, h, 0::2], ident)
                    pe.transpose(bank[4][:, (2 + h) * P:(3 + h) * P], brow[:, h, 1::2], ident)
                    pe.transpose(bank[5][:, h * P:(h + 1) * P], drow[:, h, :], ident).then_inc(s_bT, 1)
                pe.wait_ge(s_silu, 2)
                for q in range(NADA):
                    pe.wait_ge(s_ada[q % NRING], 16 * (q // NRING + 1))
                    piece = ada[q % NRING]
                    if q in (4, 5):
                        for k in range(KD):
                            m = pe.matmul(bank[2 + q - 4][:, :], scb[:, k, :], piece[:, k, :],
                                          start=(k == 0), stop=(k == KD - 1))
                    else:
                        for j in range(4):
                            for k in range(KD):
                                m = pe.matmul(bank[1][:, 4 * q + j:4 * q + j + 1], piece[:, k, j * P:(j + 1) * P],
                                              silu[:, k:k + 1], start=(k == 0), stop=(k == KD - 1))
                    m.then_inc(s_adau, 1)

            @block.scalar
            def _(act):
                act.wait_ge(s_cols, 1)
                act.activation(sig, cols[:, R_C:R_C + KD], ACT.Sigmoid).then_inc(s_sig, 1)
                act.wait_ge(s_lam, 2)
                act.activation(lam_s[:, 2:4], lam_s[:, 0:2], ACT.Exp).then_inc(s_lame, 1)
                act.wait_ge(s_ang, 1)
                act.activation(sin_t, ang, ACT.Sin).then_inc(s_sin, 1)
                act.activation(cos_t, wide, ACT.Sin).then_inc(s_sin, 1)

            @block.vector
            def _(v):
                link = Chain(v, s_v0, 0)

                v.wait_ge(s_colT, 1)
                v.tensor_copy(cols[:, 0:NR], bank[0][:, 0:NR]).then_inc(s_cols, 1)
                v.wait_ge(s_pos, 16)
                v.tensor_copy(posf[0:NT, :], posi[0:NT, :]).then_inc(s_posf, 1)
                v.wait_ge(s_sig, 1)
                v.wait_ge(s_cols, 1)
                v.tensor_tensor(silu, cols[:, R_C:R_C + KD], sig, ALU.mult).then_inc(s_silu, 1)
                v.wait_ge(s_silu, 1)
                v.tensor_copy(scb, silu.rearrange("p (k o) -> p k o", o=1).broadcast_to((P, KD, P))).then_inc(s_silu, 1)
                v.wait_ge(s_lamld, 64)
                for q in range(2):
                    v.tensor_tensor_reduce(lam4[:, 2 * q, :], lam4[:, 2 * q, :], lam4[:, 2 * q + 1, :], 1.0, 0.0,
                                           ALU.mult, ALU.add, lam_s[:, q:q + 1]).then_inc(s_lam, 1)
                v.wait_ge(s_lame, 1)
                link(v.tensor_tensor(lam_s[:, 4:5], lam_s[:, 3:4], lam_s[:, 2:3], ALU.subtract))
                link(v.tensor_scalar(neg_lam, lam_s[:, 4:5], -LAMBDA_INIT, None, ALU.add))
                link(v.tensor_scalar(gsub, cols[:, R_SUB:R_SUB + 1], 1.0 - LAMBDA_INIT, None, ALU.mult))
                v.wait_ge(s_posT, 1)
                link(v.tensor_copy(pos_c, bank[0][:, 128:128 + NT]))
                v.wait_ge(s_cst, 5)
                link(v.tensor_tensor(ang, pos_c.rearrange("p (t o) -> p t o", o=1).broadcast_to((P, NT, FM + FD)),
                                     freq.rearrange("p (o f) -> p o f", o=1).broadcast_to((P, NT, FM + FD)), ALU.mult))
                link(v.tensor_scalar(turns, ang, 1.0 / TWO_PI, MAGIC, ALU.mult, ALU.add))
                link(v.tensor_scalar(turns, turns, MAGIC, None, ALU.subtract))
                for part in (PI_1, PI_2, PI_3):
                    link(v.scalar_tensor_tensor(ang, turns, -part, ang, ALU.mult, ALU.add))
                link(v.tensor_scalar(turns, ang, float(np.pi / 2), -TWO_PI, ALU.is_gt, ALU.mult))
                link(v.scalar_tensor_tensor(wide, ang, float(np.pi / 2), turns, ALU.add, ALU.add))
                link(v.tensor_scalar(wide, wide, PI_IN, -PI_IN, ALU.min, ALU.max))
                v.tensor_scalar(ang, ang, PI_IN, -PI_IN, ALU.min, ALU.max).then_inc(s_ang, 1)
                v.wait_ge(s_bT, 2)
                link(v.tensor_copy(bias_e[:, 0, :], bank[4][:, 0:256]))
                link(v.tensor_scalar(bias_e[:, 1, :], bank[4][:, 256:512], 1.0, None, ALU.add))
                v.tensor_copy(bias_e[:, 2, :], bank[5][:, 0:256]).then_inc(s_keep, 1)
                v.wait_ge(s_adau, 6)
                v.wait_ge(s_bada, 16)
                link(v.tensor_tensor(gt1b[:, 0:512], bank[2][:, :], bada_b[:, 0:512], ALU.add))
                v.tensor_tensor(gt1b[:, 512:D], bank[3][:, :], bada_b[:, 512:D], ALU.add).then_inc(s_keep, 1)
                v.wait_ge(s_adau, NADA)
                link(v.tensor_tensor(mods[:, 0:16], bank[1][:, 0:16], cols[:, R_BADA:R_BADA + 16], ALU.add))
                link(v.tensor_tensor(mods[:, 24:48], bank[1][:, 24:48], cols[:, R_BADA + 24:R_BADA + 48], ALU.add))
                v.scalar_tensor_tensor(a1, mods[:, 8:16], 1.0, cols[:, R_G1:R_G1 + 8], ALU.add, ALU.mult)
                v.scalar_tensor_tensor(a2, mods[:, 32:40], 1.0, cols[:, R_G2:R_G2 + 8], ALU.add, ALU.mult)

        at = p1
        hT, at = carve(arena, at, KD, P)
        xt, at = carve(arena, at, D)
        cqn, at = carve(arena, at, QR)
        ckn, at = carve(arena, at, KVR)
        kpe, at = carve(arena, at, ROPE)
        cT, at = carve(arena, at, KQ + KKV, P)
        qf, at = carve(arena, at, HM, QK)
        kf, at = carve(arena, at, HM, QK)
        dqk_at = at
        dqk, at = carve(arena, at, 16, DH)
        qT_o, at = carve(arena, at, HM, P)
        dqT_o, at = carve(arena, at, HD, P)
        rot, at = carve(arena, at, 512)
        rot_a, rot_b = rot[:, 0:256], rot[:, 256:512]
        cs, at = carve(arena, at, 2, FM + FD)
        st1, at = carve(arena, at, 8)
        assert at <= 53100, at
        junk = carve(arena, dqk_at, QR)[0]

        names = ("pKV pQ pDQ pDK pDV tKV tQ up0 up1 uq0 uq1 tDQ tDK tK0 tK1 tN0 tN1 "
                 "ssKV ssQ eDQ eDK cTk cTq qup0 qup1 dqTo qTo "
                 "ckn cqn vd drot kv0 kv1 qfin dkT kT0 kT1 stored").split()
        ahead = "xn tX0 tX1 hT".split()
        ev = {n: sem("l_" + n) for n in names + ahead}
        s_x, s_qst, s_v1, s_var, s_rstd = map(sem, ("s_x", "s_qst", "s_v1", "s_var", "s_rstd"))

        def now(t):
            return t + 2

        def prev(t):
            return t + 1

        with nc.Block() as block:
            @block.sync
            def _(sp):
                sp.dma_start(xt, x2d[0:P, :]).then_inc(s_x, 16)
                with sp.Fori(0, NT) as t:
                    sp.wait_ge(ev["tX1"], prev(t))
                    sp.dma_start(xt, x2d.rearrange("(t p) d -> t p d", p=P)[bass.ds((t + 1) % NT, 1)]
                                 .rearrange("o p d -> p (o d)")).then_inc(s_x, 16)
                    sp.wait_ge(ev["dqTo"], now(t))
                    sp.dma_start(dq_scr[bass.ds(t, 1)].rearrange("o p n -> p (o n)"),
                                 dqT_o.rearrange("p h n -> p (h n)")).then_inc(s_qst, 16)
                    sp.wait_ge(ev["qTo"], now(t))
                    sp.dma_start(q_scr[bass.ds(t, 1), 0:QK].rearrange("o p n -> p (o n)"),
                                 qT_o[0:QK].rearrange("p h n -> p (h n)")).then_inc(s_qst, 16)
                    sp.wait_ge(s_qst, t * 32 + 32)
                    sp.sem_inc(ev["stored"], 1)
                sp.wait_ge(s_x, 16 * (NT + 1))

            @block.gpsimd
            def _(pool):
                for n in names:
                    pool.sem_inc(ev[n], 1)

                def root(count, col):
                    pool.wait_ge(s_var, count)
                    pool.tensor_tensor(st1[:, col:col + 1], st1[:, col:col + 1], mhalf[:, 0:1], ALU.pow).then_inc(s_rstd, 1)

                root(1, 3)
                with pool.Fori(0, NT) as t:
                    root(t * 3 + 2, 4)
                    root(t * 3 + 3, 5)
                    root(t * 3 + 4, 3)

            @block.tensor
            def _(pe):
                def turn_x():
                    for g in range(2):
                        for k in range(4 * g, 4 * g + 4):
                            m = pe.transpose(bank[5 + g][:, (k % 4) * P:(k % 4 + 1) * P], xt[:, k * P:(k + 1) * P], ident)
                        m.then_inc(ev[f"tX{g}"], 1)

                pe.wait_ge(ev["xn"], 1)
                turn_x()
                with pe.Fori(0, NT) as t:
                    pe.wait_ge(ev["hT"], prev(t))
                    for name, b, lo, n, free in (("pKV", 0, QR, KVR + ROPE, "dqTo"), ("pQ", 1, 0, QR, "dkT"),
                                                 ("pDQ", 2, C_DQ, 512, "qTo"), ("pDK", 3, C_DQ + 512, 512, "qTo"),
                                                 ("pDV", 4, C_DQ + 1024, 512, "qup0")):
                        pe.wait_ge(ev[free], prev(t))
                        for k in range(KD):
                            m = pe.matmul(bank[b][:, 0:n], hT[:, k, :], win[:, k, lo:lo + n],
                                          start=(k == 0), stop=(k == KD - 1))
                        m.then_inc(ev[name], 1)
                    pe.wait_ge(ev["ckn"], now(t))
                    for k in range(KKV):
                        m = pe.transpose(bank[0][:, k * P:(k + 1) * P], ckn[:, k * P:(k + 1) * P], ident)
                    m.then_inc(ev["tKV"], 1)
                    pe.wait_ge(ev["cqn"], now(t))
                    for k in range(KQ):
                        m = pe.transpose(bank[1][:, k * P:(k + 1) * P], cqn[:, k * P:(k + 1) * P], ident)
                    m.then_inc(ev["tQ"], 1)
                    pe.wait_ge(ev["xn"], now(t))
                    pe.wait_ge(ev["kT0"], prev(t))
                    pe.wait_ge(ev["kT1"], prev(t))
                    turn_x()
                    pe.wait_ge(ev["cTk"], now(t))
                    for g, free in ((0, "eDQ"), (1, "eDK")):
                        pe.wait_ge(ev[free], now(t))
                        for k in range(KKV):
                            m = pe.matmul(bank[2 + g][:, :], cT[:, k, :], wukv[:, k, g * 512:(g + 1) * 512],
                                          start=(k == 0), stop=(k == KKV - 1))
                        m.then_inc(ev[f"up{g}"], 1)
                    pe.wait_ge(ev["cTq"], now(t))
                    pe.wait_ge(ev["vd"], now(t))
                    pe.wait_ge(ev["qup1"], prev(t))
                    for g, b in ((0, 4), (1, 7)):
                        for k in range(KQ):
                            m = pe.matmul(bank[b][:, 0:4 * QK], cT[:, KKV + k, :], wuq[:, k, g * 4 * QK:(g + 1) * 4 * QK],
                                          start=(k == 0), stop=(k == KQ - 1))
                        m.then_inc(ev[f"uq{g}"], 1)
                    pe.wait_ge(ev["drot"], now(t))
                    for g, (name, free) in enumerate((("tDQ", "cTk"), ("tDK", "cTq"))):
                        pe.wait_ge(ev[free], now(t))
                        for h in range(HD):
                            m = pe.transpose(bank[g][:, h * P:(h + 1) * P],
                                             dqk[:, 8 * g + 2 * h:8 * g + 2 * h + 2, :].rearrange("p a d -> p (a d)"), ident)
                        m.then_inc(ev[name], 1)
                    pe.wait_ge(ev["kv1"], now(t))
                    pe.wait_ge(ev["hT"], now(t))
                    for g in range(2):
                        for h in range(4):
                            m = pe.transpose(bank[5 + g][0:QK, h * P:(h + 1) * P], kf[:, 4 * g + h, :], ident)
                        m.then_inc(ev[f"tK{g}"], 1)
                    pe.wait_ge(ev["qfin"], now(t))
                    for g in range(2):
                        for h in range(4):
                            m = pe.transpose(bank[2 + g][0:QK, h * P:(h + 1) * P], qf[:, 4 * g + h, :], ident)
                        m.then_inc(ev[f"tN{g}"], 1)

            @block.scalar
            def _(act):
                def modulate():
                    for k in range(KD):
                        m = act.activation(hT[:, k, :], bank[5 + k // 4][:, (k % 4) * P:(k % 4 + 1) * P], ACT.Identity,
                                           bias=sh1[:, k:k + 1], scale=a1[:, k:k + 1])
                    m.then_inc(ev["hT"], 1)

                act.wait_ge(ev["tX0"], 1)
                act.wait_ge(ev["tX1"], 1)
                modulate()
                with act.Fori(0, NT) as t:
                    act.wait_ge(ev["tDK"], prev(t))
                    act.wait_ge(ev["pKV"], now(t))
                    act.activation(junk[:, 0:KVR], bank[0][:, 0:KVR], ACT.Square, accum_out=st1[:, 0:1]).then_inc(ev["ssKV"], 1)
                    act.wait_ge(ev["pQ"], now(t))
                    act.wait_ge(ev["ssKV"], now(t))
                    act.activation(junk, bank[1][:, 0:QR], ACT.Square, accum_out=st1[:, 1:2]).then_inc(ev["ssQ"], 1)
                    act.wait_ge(ev["pDQ"], now(t))
                    act.wait_ge(ev["ssQ"], now(t))
                    act.activation(dqk[:, 0:8, :].rearrange("p a d -> p (a d)"), bank[2][:, :], ACT.Copy).then_inc(ev["eDQ"], 1)
                    act.wait_ge(ev["pDK"], now(t))
                    act.activation(dqk[:, 8:16, :].rearrange("p a d -> p (a d)"), bank[3][:, :], ACT.Copy).then_inc(ev["eDK"], 1)
                    act.wait_ge(ev["tKV"], now(t))
                    for k in range(KKV):
                        m = act.activation(cT[:, k, :], bank[0][:, k * P:(k + 1) * P], ACT.Copy, scale=cols[:, R_GKV + k:R_GKV + k + 1])
                    m.then_inc(ev["cTk"], 1)
                    act.wait_ge(ev["tQ"], now(t))
                    for k in range(KQ):
                        m = act.activation(cT[:, KKV + k, :], bank[1][:, k * P:(k + 1) * P], ACT.Copy, scale=cols[:, R_GQ + k:R_GQ + k + 1])
                    m.then_inc(ev["cTq"], 1)
                    act.wait_ge(ev["tX0"], now(t))
                    act.wait_ge(ev["tX1"], now(t))
                    modulate()
                    act.wait_ge(ev["uq0"], now(t))
                    act.wait_ge(ev["tN1"], prev(t))
                    act.activation(qf[:, 0:4, :].rearrange("p h d -> p (h d)"), bank[4][:, 0:4 * QK], ACT.Copy).then_inc(ev["qup0"], 1)
                    act.wait_ge(ev["uq1"], now(t))
                    act.activation(qf[:, 4:8, :].rearrange("p h d -> p (h d)"), bank[7][:, 0:4 * QK], ACT.Copy).then_inc(ev["qup1"], 1)
                    act.wait_ge(ev["stored"], prev(t))
                    act.wait_ge(ev["tDQ"], now(t))
                    act.activation(dqT_o.rearrange("p h n -> p (h n)"), bank[0][:, :], ACT.Copy).then_inc(ev["dqTo"], 1)
                    act.wait_ge(ev["tN0"], now(t))
                    act.activation(qT_o[0:QK, 0:4, :].rearrange("p h n -> p (h n)"), bank[2][0:QK, :], ACT.Copy)
                    act.wait_ge(ev["tN1"], now(t))
                    act.activation(qT_o[0:QK, 4:8, :].rearrange("p h n -> p (h n)"), bank[3][0:QK, :], ACT.Copy).then_inc(ev["qTo"], 1)

            @block.vector
            def _(v):
                def rstd(count, out, ss, n, eps):
                    v.tensor_scalar(out, ss, 1.0 / n, eps, ALU.mult, ALU.add).then_inc(s_var, 1)
                    v.wait_ge(s_rstd, count)

                def norm_x(link, count):
                    for h in range(2):
                        link(v.tensor_tensor_reduce(rot, xt[:, h * 512:(h + 1) * 512], xt[:, h * 512:(h + 1) * 512], 1.0, 0.0,
                                                    ALU.mult, ALU.add, st1[:, 6 + h:7 + h]))
                    link(v.tensor_tensor(st1[:, 2:3], st1[:, 6:7], st1[:, 7:8], ALU.add))
                    rstd(count, st1[:, 3:4], st1[:, 2:3], D, 1e-6)
                    v.tensor_scalar(xt, xt, st1[:, 3:4], None, ALU.mult).then_inc(ev["xn"], 1)

                def rotate(link, z, out, n, F, lo):
                    ra = rot_a[:, 0:2 * n * F].rearrange("p (g a f) -> p g a f", g=n, a=2)
                    rb = rot_b[:, 0:2 * n * F].rearrange("p (g a f) -> p g a f", g=n, a=2)
                    cw = cs[:, 0:1, lo:lo + F].rearrange("p (g a) f -> p g a f", g=1).broadcast_to((P, n, 2, F))
                    sw = cs[:, 1:2, lo:lo + F].rearrange("p (g a) f -> p g a f", g=1).broadcast_to((P, n, 2, F))
                    link(v.tensor_tensor(ra, z, cw, ALU.mult))
                    link(v.tensor_tensor(rb, z, sw, ALU.mult))
                    link(v.tensor_tensor(out[:, :, 0, :], ra[:, :, 0, :], rb[:, :, 1, :], ALU.subtract))
                    return v.tensor_tensor(out[:, :, 1, :], ra[:, :, 1, :], rb[:, :, 0, :], ALU.add)

                PRE, PER = 3, 18
                v.wait_ge(s_x, 16)
                link = Chain(v, s_v1, 0)
                norm_x(link, 1)
                assert link.done == PRE
                with v.Fori(0, NT) as t:
                    link = Chain(v, s_v1, t * PER + PRE)
                    link(v.tensor_scalar(cs[:, 0:1, :], cos_t[:, bass.ds(t, 1), :], 1.0, None, ALU.mult))
                    link(v.tensor_scalar(cs[:, 1:2, :], sin_t[:, bass.ds(t, 1), :], 1.0, None, ALU.mult))
                    v.wait_ge(ev["ssKV"], now(t))
                    rstd(t * 3 + 2, st1[:, 4:5], st1[:, 0:1], KVR, 1e-6)
                    link(v.tensor_scalar(ckn, bank[0][:, 0:KVR], st1[:, 4:5], None, ALU.mult))
                    rotate(link, bank[0][:, KVR:KVR + ROPE].rearrange("p (g a f) -> p g a f", g=1, a=2),
                           kpe.rearrange("p (g a f) -> p g a f", g=1, a=2), 1, FM, 0).then_inc(ev["ckn"], 1)
                    v.wait_ge(ev["ssQ"], now(t))
                    rstd(t * 3 + 3, st1[:, 5:6], st1[:, 1:2], QR, 1e-6)
                    v.tensor_scalar(cqn, bank[1][:, 0:QR], st1[:, 5:6], None, ALU.mult).then_inc(ev["cqn"], 1)
                    v.wait_ge(s_x, t * 16 + 32)
                    norm_x(link, t * 3 + 4)
                    v.wait_ge(ev["pDV"], now(t))
                    v.tensor_scalar(v_d[:, bass.ds(t, 1), :].rearrange("p o n -> p (o n)"), bank[4][:, :], 1.0, None,
                                    ALU.mult).then_inc(ev["vd"], 1)
                    v.wait_ge(ev["eDQ"], now(t))
                    v.wait_ge(ev["eDK"], now(t))
                    z = dqk[:, :, 0:DROPE].rearrange("p g (a f) -> p g a f", a=2)
                    rotate(link, z, z, 16, FD, FM).then_inc(ev["drot"], 1)
                    v.wait_ge(ev["tK1"], prev(t))
                    v.wait_ge(ev["ckn"], now(t))
                    link(v.tensor_copy(kf[:, :, NOPE:QK], kpe.rearrange("p (o f) -> p o f", o=1).broadcast_to((P, HM, ROPE))))
                    for g in range(2):
                        v.wait_ge(ev[f"up{g}"], now(t))
                        kv = bank[2 + g][:, :].rearrange("p (h n) -> p h n", h=4)
                        link(v.tensor_copy(kf[:, 4 * g:4 * g + 4, 0:NOPE], kv[:, :, 0:NOPE]))
                        v.tensor_scalar(v_m[:, bass.ds(t, 1), g * 256:(g + 1) * 256].rearrange("p o (h n) -> p (o h) n", h=4),
                                        kv[:, :, NOPE:NOPE + DV_M], 1.0, None, ALU.mult).then_inc(ev[f"kv{g}"], 1)
                    v.wait_ge(ev["qup0"], now(t))
                    v.wait_ge(ev["qup1"], now(t))
                    z = qf[:, :, NOPE:QK].rearrange("p g (a f) -> p g a f", a=2)
                    rotate(link, z, z, HM, FM, 0).then_inc(ev["qfin"], 1)
                    v.wait_ge(ev["tDK"], now(t))
                    v.tensor_scalar(dkT[:, :, bass.ds(t * P, P)], bank[1][:, :].rearrange("p (h n) -> p h n", h=4), 1.0, None,
                                    ALU.mult).then_inc(ev["dkT"], 1)
                    for g in range(2):
                        v.wait_ge(ev[f"tK{g}"], now(t))
                        v.tensor_scalar(kT[0:QK, 4 * g:4 * g + 4, bass.ds(t * P, P)],
                                        bank[5 + g][0:QK, :].rearrange("p (h n) -> p h n", h=4), 1.0, None,
                                        ALU.mult).then_inc(ev[f"kT{g}"], 1)
                    assert link.done == PER, link.done

        at = work
        wout, at = carve(arena, at, KD, D)
        pbuf, at = carve(arena, at, 4, S)
        pT, at = carve(arena, at, 2, KD, P)
        qTb, at = carve(arena, at, 2, HM, P)
        dqTb, at = carve(arena, at, 2, HD, P)
        o_sb, at = carve(arena, at, 2, D)
        oT, at = carve(arena, at, KD, P)
        x2, at = carve(arena, at, D)
        x1, at = carve(arena, at, D)
        xh, at = carve(arena, at, D)
        h2T, at = carve(arena, at, KD, P)
        gt1b, at = carve(arena, at, D)
        wr, at = carve(arena, at, KD, NE)
        br, at = carve(arena, at, NE)
        nmax, at = carve(arena, at, 4)
        psum_p, at = carve(arena, at, 4)
        inv, at = carve(arena, at, 4)
        fac, at = carve(arena, at, 2)
        st2, at = carve(arena, at, 16)
        lg, at = carve(arena, at, NE)
        v8, at = carve(arena, at, 8)
        i8, at = carve(arena, at, 8)
        i8f, at = carve(arena, at, TOPK)
        hot, at = carve(arena, at, TOPK, NE)
        chosen, at = carve(arena, at, NE)
        earlier, at = carve(arena, at, NE)
        slot_f, at = carve(arena, at, NE)
        pick, at = carve(arena, at, TOPK, NE)
        w4, at = carve(arena, at, 8)
        s4f, at = carve(arena, at, TOPK)
        slots, at = carve(arena, at, 2, TOPK)
        entry, at = carve(arena, at, 2, TOPK, 2)
        ptab, at = carve(arena, at, 4)
        pp, at = carve(arena, at, 10, NE)
        ps, at = carve(arena, at, 8)
        assert at <= 53100, at
        i8 = i8.bitcast(U32)
        slots = slots.bitcast(I32)
        entry_i, entry_f = entry.bitcast(I32), entry
        ptab = ptab.bitcast(I32)

        steps = attention_plan()
        PTB = (4, 5)
        (s_w2, s_x2, s_scores, s_max, s_exp, s_mixw, s_T, s_ev4, s_ev5, s_pv, s_oev, s_on, s_m7, s_m7ev, s_x1, s_xh,
         s_st, s_var2, s_rstd2, s_v2, s_top, s_ew, s_chosen, s_slot, s_cnt, s_ptab) = map(sem, (
             "s_w2 s_x2 s_scores s_max s_exp s_mixw s_T s_ev4 s_ev5 s_pv s_oev s_on s_m7 s_m7ev s_x1 s_xh "
             "s_st s_var2 s_rstd2 s_v2 s_top s_ew s_chosen s_slot s_cnt s_ptab").split())
        s_q = [sem("s_q0"), sem("s_q1")]
        s_scat = [sem("s_scat0"), sem("s_scat1")]
        group_of = {(kind, i, u): g for kind, i, u, g in steps}

        def evacuated(eng, g):
            eng.wait_ge((s_ev4, s_ev5)[g % 2], g // 2 + 1)

        with nc.Block() as block:
            @block.sync
            def _(sp):
                sp.dma_start(gt1b, gt1_scr).then_inc(s_w2, 16)
                sp.dma_start(wr, w_router[0].rearrange("(k p) n -> p k n", p=P)).then_inc(s_w2, 16)
                sp.dma_start(br, b_router.broadcast_to((P, NE))).then_inc(s_w2, 16)
                for i in range(NT):
                    if i >= 2:
                        sp.wait_ge(s_scores, item(i - 1, 0))
                    sp.dma_start(qTb[0:QK, i % 2].rearrange("p h n -> p (h n)"), q_scr[i, 0:QK]).then_inc(s_q[i % 2], 16)
                    sp.dma_start(dqTb[:, i % 2].rearrange("p h n -> p (h n)"), dq_scr[i]).then_inc(s_q[i % 2], 16)
                    if i == 0:
                        sp.dma_start(wout, w_out[0].rearrange("(k p) n -> p k n", p=P)).then_inc(s_w2, 16)
                        sp.dma_start(x2, x2d[0:P, :]).then_inc(s_x2, 16)
                    else:
                        sp.wait_ge(s_x1, i)
                        sp.dma_start(x_acc[(i - 1) * P:i * P, :], x1).then_inc(s_st, 16)
                        sp.dma_start(x2, x2d[i * P:(i + 1) * P, :]).then_inc(s_x2, 16)
                        sp.wait_ge(s_xh, i)
                        sp.dma_start(x_hat[(i - 1) * P:i * P, :], xh).then_inc(s_st, 16)
                sp.wait_ge(s_x1, NT)
                sp.dma_start(x_acc[(NT - 1) * P:S, :], x1).then_inc(s_st, 16)
                sp.wait_ge(s_xh, NT)
                sp.dma_start(x_hat[(NT - 1) * P:S, :], xh).then_inc(s_st, 16)
                sp.wait_ge(s_cnt, 1)
                sp.dma_start(passes, ptab).then_inc(s_ptab, 16)
                sp.wait_ge(s_st, 32 * NT)
                sp.wait_ge(s_ptab, 16)

            @block.gpsimd
            def _(pool):
                for i in range(NT):
                    for q, cut in enumerate((slice(10, 14), slice(15, 16))):
                        pool.wait_ge(s_var2, 2 * i + q + 1)
                        pool.tensor_tensor(st2[:, cut], st2[:, cut], mhalf[:, 0:cut.stop - cut.start], ALU.pow).then_inc(s_rstd2, 1)
                    pool.wait_ge(s_slot, i + 1)
                    for k in range(TOPK):
                        pool.indirect_dma_start(table, bass.IndirectOffsetOnAxis(ap=slots[:, i % 2, k:k + 1], axis=0),
                                                entry_i[:, i % 2, k, :], None).then_inc(s_scat[i % 2], 16)
                for par in range(2):
                    pool.wait_ge(s_scat[par], 16 * TOPK * NT // 2)

            @block.tensor
            def _(pe):
                oT_group = group_of["oT", 0, 0]

                def group_bank(g):
                    if g >= 2:
                        evacuated(pe, g - 2)
                    return bank[PTB[g % 2]]

                def turn(src, g0):
                    for g in range(2):
                        b = group_bank(g0 + g)
                        for k in range(4):
                            m = pe.transpose(b[:, k * P:(k + 1) * P], src[:, (4 * g + k) * P:(4 * g + k + 1) * P], ident)
                        m.then_inc(s_T, 1)

                def misc(n):
                    if n:
                        pe.wait_ge(s_m7ev, n)
                    return bank[7]

                for kind, i, u, g0 in steps:
                    kb = i + 1
                    if kind == "S":
                        if u == 0:
                            pe.wait_ge(s_q[i % 2], 32 * (i // 2 + 1))
                        for half in range(1 if u < HM else 2):
                            n = item(i, u) + half
                            if n >= 2:
                                pe.wait_ge(s_exp, n - 1)
                            for w in range(0, kb * P, 512):
                                hi = min(w + 512, kb * P)
                                dst = bank[2 * (n % 2) + w // 512][:, 0:hi - w]
                                if u < HM:
                                    m = pe.matmul(dst, qTb[0:QK, i % 2, u, :], kT[0:QK, u, w:hi], start=True, stop=True)
                                else:
                                    rows_ = slice(half * DH, half * DH + DH)
                                    m = pe.matmul(dst, dqTb[rows_, i % 2, u - HM, :], dkT[rows_, u - HM, w:hi],
                                                  start=True, stop=True)
                            m.then_inc(s_scores, 1)
                    elif kind == "T":
                        n = item(i, u)
                        if u < HM:
                            pe.wait_ge(s_exp, n + 1)
                        else:
                            pe.wait_ge(s_mixw, HD * i + u - HM + 1)
                        for g in range(0, kb, 4):
                            b = group_bank(g0 + g // 4)
                            for k in range(g, min(g + 4, kb)):
                                m = pe.transpose(b[:, (k - g) * P:(k - g + 1) * P], pbuf[:, n % 4, k * P:(k + 1) * P], ident)
                            m.then_inc(s_T, 1)
                    elif kind == "PV":
                        U = (HM + HD) * i + u
                        gs = group_of["T", i, u]
                        for g in range(gs, gs + i // 4 + 1):
                            evacuated(pe, g)
                        if U:
                            pe.wait_ge(s_oev, U)
                        for k in range(kb):
                            if u < HM:
                                m = pe.matmul(bank[6][:, 0:DV_M], pT[:, U % 2, k, :],
                                              v_m[:, k, u * DV_M:(u + 1) * DV_M], start=(k == 0), stop=(k == kb - 1))
                            else:
                                m = pe.matmul(bank[6][:, 0:P], pT[:, U % 2, k, :],
                                              v_d[:, k, (u - HM) * P:(u - HM + 1) * P], start=(k == 0), stop=(k == kb - 1))
                        m.then_inc(s_pv, 1)
                    elif kind == "oT":
                        pe.wait_ge(s_on, i + 1)
                        turn(o_sb[:, i % 2, :], g0)
                    elif kind in ("mix0", "mix1"):
                        h = int(kind[-1])
                        if h == 0:
                            for g in range(2):
                                evacuated(pe, group_of["oT", i, 0] + g)
                            pe.wait_ge(s_w2, 64)
                        b = misc(4 * i + h)
                        for k in range(KD):
                            m = pe.matmul(b[:, :], oT[:, k, :], wout[:, k, h * 512:(h + 1) * 512], start=(k == 0), stop=(k == KD - 1))
                        m.then_inc(s_m7, 1)
                    elif kind == "xT":
                        pe.wait_ge(s_xh, i + 1)
                        turn(xh, g0)
                    elif kind == "router":
                        for g in range(2):
                            evacuated(pe, group_of["xT", i, 0] + g)
                        b = misc(4 * i + 2)
                        for k in range(KD):
                            m = pe.matmul(b[:, 0:NE], h2T[:, k, :], wr[:, k, :], start=(k == 0), stop=(k == KD - 1))
                        m.then_inc(s_m7, 1)
                    elif kind == "rank":
                        pe.wait_ge(s_chosen, i + 1)
                        b = misc(4 * i + 3)
                        m = pe.matmul(b[:, 0:NE], before, chosen, start=True, stop=(i == 0))
                        if i:
                            m = pe.matmul(b[:, 0:NE], ones, earlier, start=False, stop=True)
                        m.then_inc(s_m7, 1)
                pe.wait_ge(s_slot, NT)
                b = misc(4 * NT)
                pe.matmul(b[:, 0:NE], ones, earlier, start=True, stop=True).then_inc(s_m7, 1)

            @block.scalar
            def _(act):
                for kind, i, u, g0 in steps:
                    kw = (i + 1) * P
                    if kind == "S":
                        scale = SCALE_M if u < HM else SCALE_D
                        for n in range(item(i, u), item(i, u) + (1 if u < HM else 2)):
                            act.wait_ge(s_max, n + 1)
                            if n >= 4:
                                un = unit_of(n - 4)
                                act.wait_ge(s_T, group_of["T", un[0], un[1]] + un[0] // 4 + 1)
                            for w in range(0, kw, 512):
                                hi = min(w + 512, kw)
                                m = act.activation(pbuf[:, n % 4, w:hi], bank[2 * (n % 2) + w // 512][:, 0:hi - w], ACT.Exp,
                                                   bias=nmax[:, n % 4:n % 4 + 1], scale=scale,
                                                   accum_out=st2[:, (w // 512) * 4 + n % 4:(w // 512) * 4 + n % 4 + 1])
                            m.then_inc(s_exp, 1)
                    elif kind == "T":
                        U = (HM + HD) * i + u
                        for g in range(g0, g0 + i // 4 + 1):
                            if g % 2 == 0:
                                continue
                            k0, k1 = 4 * (g - g0), min(4 * (g - g0) + 4, i + 1)
                            act.wait_ge(s_T, g + 1)
                            if U >= 2:
                                act.wait_ge(s_pv, U - 1)
                            act.activation(pT[:, U % 2, k0:k1, :].rearrange("p k n -> p (k n)"),
                                           bank[5][:, 0:(k1 - k0) * P], ACT.Copy).then_inc(s_ev5, 1)
                    elif kind in ("oT", "xT"):
                        g = g0 if g0 % 2 else g0 + 1
                        half = g - g0
                        act.wait_ge(s_T, g + 1)
                        for k in range(4 * half, 4 * half + 4):
                            src = bank[5][:, (k % 4) * P:(k % 4 + 1) * P]
                            if kind == "xT":
                                m = act.activation(h2T[:, k, :], src, ACT.Identity, bias=sh2[:, k:k + 1], scale=a2[:, k:k + 1])
                            else:
                                m = act.activation(oT[:, k, :], src, ACT.Copy, scale=gsub if half else 1.0)
                        m.then_inc(s_ev5, 1)
                    elif kind == "router":
                        act.wait_ge(s_top, i + 1)
                        act.activation(w4[:, 0:TOPK], v8[:, 0:TOPK], ACT.Exp, bias=w4[:, 5:6], scale=1.0,
                                       accum_out=w4[:, 4:5]).then_inc(s_ew, 1)

            @block.vector
            def _(v):
                link = Chain(v, s_v2, 0)
                link(v.memset(earlier, 0.0))

                def rstd(count, out, ss, n, eps):
                    v.tensor_scalar(out, ss, 1.0 / n, eps, ALU.mult, ALU.add).then_inc(s_var2, 1)
                    v.wait_ge(s_rstd2, count)

                def total(n, kb):
                    if kb > 4:
                        link(v.tensor_tensor(psum_p[:, n % 4:n % 4 + 1], st2[:, n % 4:n % 4 + 1], st2[:, 4 + n % 4:5 + n % 4], ALU.add))
                        return psum_p[:, n % 4:n % 4 + 1]
                    return st2[:, n % 4:n % 4 + 1]

                for kind, i, u, g0 in steps:
                    kb = i + 1
                    kw = kb * P
                    if kind == "S":
                        scale = SCALE_M if u < HM else SCALE_D
                        for n in range(item(i, u), item(i, u) + (1 if u < HM else 2)):
                            v.wait_ge(s_scores, n + 1)
                            b = 2 * (n % 2)
                            edge = bank[b + (kw - 1) // 512][0:CHUNK, (kw - CHUNK) % 512:(kw - CHUNK) % 512 + CHUNK]
                            link(v.memset(edge, MASKED))
                            for w in range(0, kw, 512):
                                hi = min(w + 512, kw)
                                link(v.reduce_max(st2[:, 8 + w // 512:9 + w // 512], bank[b + w // 512][:, 0:hi - w], AX_X))
                            if n >= 4:
                                v.wait_ge(s_exp, n - 3)
                            if kb > 4:
                                link(v.tensor_tensor(st2[:, 8:9], st2[:, 8:9], st2[:, 9:10], ALU.max))
                            v.tensor_scalar(nmax[:, n % 4:n % 4 + 1], st2[:, 8:9], -scale, None, ALU.mult).then_inc(s_max, 1)
                    elif kind == "T":
                        U = (HM + HD) * i + u
                        n = item(i, u)
                        if u < HM:
                            v.wait_ge(s_exp, n + 1)
                            link(v.reciprocal(inv[:, U % 4:U % 4 + 1], total(n, kb)))
                        else:
                            v.wait_ge(s_exp, n + 2)
                            t1, t2 = total(n, kb), total(n + 1, kb)
                            link(v.reciprocal(inv[:, U % 4:U % 4 + 1], t1))
                            link(v.reciprocal(fac[:, 0:1], t2))
                            link(v.tensor_tensor(fac[:, 1:2], fac[:, 0:1], t1, ALU.mult))
                            link(v.tensor_tensor(fac[:, 0:1], fac[:, 1:2], neg_lam, ALU.mult))
                            v.scalar_tensor_tensor(pbuf[:, n % 4, 0:kw], pbuf[:, (n + 1) % 4, 0:kw], fac[:, 0:1],
                                                   pbuf[:, n % 4, 0:kw], ALU.mult, ALU.add).then_inc(s_mixw, 1)
                        for g in range(g0, g0 + i // 4 + 1):
                            if g % 2:
                                continue
                            k0, k1 = 4 * (g - g0), min(4 * (g - g0) + 4, kb)
                            v.wait_ge(s_T, g + 1)
                            if U >= 2:
                                v.wait_ge(s_pv, U - 1)
                            v.tensor_copy(pT[:, U % 2, k0:k1, :].rearrange("p k n -> p (k n)"),
                                          bank[4][:, 0:(k1 - k0) * P]).then_inc(s_ev4, 1)
                    elif kind == "PV":
                        U = (HM + HD) * i + u
                        v.wait_ge(s_pv, U + 1)
                        if u == 0 and i >= 2:
                            v.wait_ge(s_T, group_of["oT", i - 2, 0] + 2)
                        w = DV_M if u < HM else P
                        lo = u * DV_M if u < HM else HM * DV_M + (u - HM) * P
                        ins = v.tensor_scalar(o_sb[:, i % 2, lo:lo + w], bank[6][:, 0:w],
                                              inv[:, U % 4:U % 4 + 1], None, ALU.mult)
                        ins.then_inc(s_oev, 1)
                        if u == HM + HD - 1:
                            v.wait_ge(s_oev, U + 1)
                            od = o_sb[:, i % 2, HM * DV_M:D].rearrange("p (h n) -> p h n", h=HD)
                            sq = xh[:, 0:P]
                            if i:
                                v.wait_ge(s_st, 32 * i)
                            for h in range(HD):
                                link(v.tensor_tensor_reduce(sq, od[:, h, :], od[:, h, :], 1.0, 0.0, ALU.mult, ALU.add,
                                                            st2[:, 10 + h:11 + h]))
                            rstd(2 * i + 1, st2[:, 10:14], st2[:, 10:14], P, 1e-5)
                            v.tensor_tensor(od, od, st2[:, 10:14].rearrange("p (h o) -> p h o", o=1).broadcast_to((P, HD, P)),
                                            ALU.mult).then_inc(s_on, 1)
                    elif kind in ("oT", "xT"):
                        g = g0 + g0 % 2
                        half = g - g0
                        v.wait_ge(s_T, g + 1)
                        for k in range(4 * half, 4 * half + 4):
                            src = bank[4][:, (k % 4) * P:(k % 4 + 1) * P]
                            if kind == "xT":
                                m = v.tensor_scalar(h2T[:, k, :], src, a2[:, k:k + 1], sh2[:, k:k + 1], ALU.mult, ALU.add)
                            elif half:
                                m = v.tensor_scalar(oT[:, k, :], src, gsub, None, ALU.mult)
                            else:
                                m = v.tensor_copy(oT[:, k, :], src)
                        m.then_inc(s_ev4, 1)
                    elif kind in ("mix0", "mix1"):
                        h = int(kind[-1])
                        cut = slice(h * 512, (h + 1) * 512)
                        v.wait_ge(s_m7, 4 * i + h + 1)
                        if h == 0:
                            v.wait_ge(s_w2, 64)
                            v.wait_ge(s_x2, 16 * (i + 1))
                            if i:
                                v.wait_ge(s_st, 32 * i)
                        v.tensor_tensor(x1[:, cut], bank[7][:, :], gt1b[:, cut], ALU.mult).then_inc(s_m7ev, 1)
                        v.wait_ge(s_m7ev, 4 * i + h + 1)
                        ins = v.tensor_tensor(x1[:, cut], x1[:, cut], x2[:, cut], ALU.add)
                        if h == 0:
                            link(ins)
                        else:
                            ins.then_inc(s_x1, 1)
                            v.wait_ge(s_x1, i + 1)
                            link(v.tensor_tensor_reduce(xh, x1, x1, 1.0, 0.0, ALU.mult, ALU.add, st2[:, 14:15]))
                            rstd(2 * i + 2, st2[:, 15:16], st2[:, 14:15], D, 1e-6)
                            v.tensor_scalar(xh, x1, st2[:, 15:16], None, ALU.mult).then_inc(s_xh, 1)
                    elif kind == "router":
                        v.wait_ge(s_m7, 4 * i + 3)
                        v.tensor_tensor(lg, bank[7][:, 0:NE], br, ALU.add).then_inc(s_m7ev, 1)
                        v.wait_ge(s_m7ev, 4 * i + 3)
                        link(v.max(v8, lg))
                        link(v.max_index(i8, v8, lg))
                        v.tensor_scalar(w4[:, 5:6], v8[:, 0:1], -1.0, None, ALU.mult).then_inc(s_top, 1)
                        link(v.tensor_copy(i8f, i8[:, 0:TOPK]))
                        for k in range(TOPK):
                            link(v.tensor_scalar(hot[:, k, :], iota_e, i8f[:, k:k + 1], None, ALU.is_equal))
                        if i >= 2:
                            v.wait_ge(s_scat[i % 2], 16 * TOPK * (i // 2))
                        link(v.tensor_tensor(pick[:, 0, :], hot[:, 0, :], hot[:, 1, :], ALU.add))
                        link(v.tensor_tensor(pick[:, 1, :], hot[:, 2, :], hot[:, 3, :], ALU.add))
                        v.tensor_tensor(chosen, pick[:, 0, :], pick[:, 1, :], ALU.add).then_inc(s_chosen, 1)
                        v.wait_ge(s_ew, i + 1)
                        link(v.reciprocal(w4[:, 6:7], w4[:, 4:5]))
                        link(v.tensor_scalar(entry_f[:, i % 2, :, 1], w4[:, 0:TOPK], w4[:, 6:7], None, ALU.mult))
                        link(v.tensor_scalar(s4f, iota_p.broadcast_to((P, TOPK)), float(i * P), None, ALU.add))
                        link(v.tensor_copy(entry_i[:, i % 2, :, 0], s4f))
                    elif kind == "rank":
                        v.wait_ge(s_m7, 4 * i + 4)
                        v.scalar_tensor_tensor(slot_f, iota_e, float(S), bank[7][:, 0:NE], ALU.mult, ALU.add).then_inc(s_m7ev, 1)
                        v.wait_ge(s_m7ev, 4 * i + 4)
                        v.wait_ge(s_chosen, i + 1)
                        link(v.tensor_tensor(earlier, earlier, chosen, ALU.add))
                        for k in range(TOPK):
                            link(v.tensor_tensor_reduce(pick[:, k, :], hot[:, k, :], slot_f, 1.0, 0.0, ALU.mult, ALU.add,
                                                        s4f[:, k:k + 1]))
                        v.tensor_copy(slots[:, i % 2, :], s4f).then_inc(s_slot, 1)
                cnt, npass, ends, starts, ge, hot_e, tmp = (pp[:, q, :] for q in range(7))
                v.wait_ge(s_m7, 4 * NT + 1)
                link(v.tensor_copy(cnt, bank[7][:, 0:NE]))
                link(v.tensor_scalar(npass, cnt, float(CAP), 1.0, ALU.is_gt, ALU.add))
                for q in range(2, S // CAP):
                    link(v.scalar_tensor_tensor(npass, cnt, float(q * CAP), npass, ALU.is_gt, ALU.add))
                link(v.tensor_tensor_scan(ends, ones[:, 0:NE], npass, 0.0, ALU.mult, ALU.add))
                link(v.tensor_tensor(starts, ends, npass, ALU.subtract))
                link(v.tensor_scalar(ge, starts, iota_p, None, ALU.is_le))
                link(v.reduce_sum(ps[:, 0:1], ge, AX_X))
                link(v.tensor_scalar(ps[:, 0:1], ps[:, 0:1], -1.0, None, ALU.add))
                link(v.tensor_scalar(hot_e, iota_e, ps[:, 0:1], None, ALU.is_equal))
                link(v.tensor_tensor_reduce(tmp, hot_e, starts, 1.0, 0.0, ALU.mult, ALU.add, ps[:, 1:2]))
                link(v.tensor_tensor_reduce(tmp, hot_e, cnt, 1.0, 0.0, ALU.mult, ALU.add, ps[:, 2:3]))
                link(v.tensor_tensor(ps[:, 3:4], iota_p, ps[:, 1:2], ALU.subtract))
                link(v.tensor_scalar(ps[:, 3:4], ps[:, 3:4], float(S // CAP - 1), float(CAP), ALU.min, ALU.mult))
                link(v.tensor_tensor(ps[:, 4:5], ps[:, 2:3], ps[:, 3:4], ALU.subtract))
                link(v.scalar_tensor_tensor(ps[:, 5:6], ps[:, 0:1], float(S), ps[:, 3:4], ALU.mult, ALU.add))
                link(v.tensor_copy(ptab[:, 0:1], ps[:, 0:1]))
                link(v.tensor_copy(ptab[:, 1:2], ps[:, 5:6]))
                link(v.tensor_copy(ptab[:, 2:3], ps[:, 4:5]))
                v.tensor_copy(ptab[:, 3:4], ends[:, NE - 1:NE]).then_inc(s_cnt, 1)

        NJ = 2 * D // 256
        ND = D // 256
        NW = NJ + ND
        at = base
        w_slot = []
        for q in range(NW):
            sl, at = carve(arena, at, KD, 256)
            w_slot.append(sl)
        xg, at = carve(arena, at, 2, D)
        xT, at = carve(arena, at, KD, CAP)
        actT, at = carve(arena, at, KD, CAP)
        yT, at = carve(arena, at, KD, CAP)
        y, at = carve(arena, at, 2, D)
        bias_e, at = carve(arena, at, 3, NE * KD)
        bc, at = carve(arena, at, 3, KD)
        gate_t, at = carve(arena, at, CAP)
        up_t, at = carve(arena, at, CAP)
        sig_t, at = carve(arena, at, CAP)
        idx_g, at = carve(arena, at, 2, 2)
        idx_s, at = carve(arena, at, 2, 2)
        assert at <= 53100, at
        idx_g, idx_s, wgt = idx_g.bitcast(I32), idx_s.bitcast(I32), idx_s

        (s_gx, s_xte, s_gu, s_gev, s_gate, s_sigd, s_actd, s_yt, s_yev, s_ytr, s_ye, s_yfree,
         s_is, s_ig, s_sc, s_be, s_tr, s_v3, s_go) = map(sem, (
             "s_gx s_xte s_gu s_gev s_gate s_sigd s_actd s_yt s_yev s_ytr s_ye s_yfree "
             "s_is s_ig s_sc s_be s_tr s_v3 s_go").split())
        s_wd = [sem(f"s_wd{q}") for q in range(NW)]

        def pass_value(eng, i, col, hi):
            return eng.value_load(passes[bass.ds(i, 1), col:col + 1] if not isinstance(i, int) else
                                  passes[i:i + 1, col:col + 1], min_val=0, max_val=hi)

        def n_passes(eng):
            return eng.value_load(passes[0:1, 3:4], min_val=NE, max_val=MAXPASS)

        def by_size(eng, tokens, body, sizes=SIZES):
            if len(sizes) == 1:
                body(sizes[0])
                return
            with eng.If(tokens <= sizes[0]):
                body(sizes[0])
            with eng.Else():
                by_size(eng, tokens, body, sizes[1:])

        with nc.Block() as block:
            @block.sync
            def _(sp):
                sp.dma_start(bias_e.rearrange("p a n -> p (a n)"), bias_scr).then_inc(s_be, 16)
                T = n_passes(sp)
                with sp.Fori(0, T) as i:
                    e = pass_value(sp, i, 0, NE - 1)
                    for q in range(NW):
                        if q < NJ:
                            sp.wait_ge(s_gu, i * 8 + q + 1)
                        else:
                            sp.wait_ge(s_yt, i * 8 + 2 * (q - NJ) + 2)
                        src = (w_gu_v[:, bass.ds(e, 1), :, q * 256:(q + 1) * 256] if q < NJ else
                               w_dn_v[:, bass.ds(e, 1), :, (q - NJ) * 256:(q - NJ + 1) * 256])
                        sp.dma_start(w_slot[q], src.rearrange("p o k n -> p (o k) n")).then_inc(s_wd[q], 16)

            @block.gpsimd
            def _(pool):
                def rows_of(i, dst, sem_):
                    r0 = pass_value(pool, i, 1, NE * S - CAP)
                    pool.dma_start(dst, table[bass.ds(r0, CAP), :].rearrange("(b p) w -> p b w", p=P)).then_inc(sem_, 16)

                def gather():
                    for b in range(2):
                        pool.indirect_dma_start(xg[:, b, :], None, x_hat,
                                                bass.IndirectOffsetOnAxis(ap=idx_g[:, b, 0:1], axis=0)).then_inc(s_gx, 16)

                pool.sem_inc(s_gu, 8)
                pool.sem_inc(s_yt, 8)
                pool.sem_inc(s_gev, 8)
                pool.sem_inc(s_yev, 8)
                pool.sem_inc(s_ye, 4)
                pool.sem_inc(s_yfree, 1)
                T = n_passes(pool)
                rows_of(0, idx_g, s_ig)
                pool.wait_ge(s_ig, 16)
                gather()
                with pool.Fori(0, T) as i:
                    rows_of(i, idx_s, s_is)
                    pool.wait_ge(s_gx, i * 32 + 32)
                    pool.sem_inc(s_go, 1)
                    rows_of(i + 1, idx_g, s_ig)
                    pool.wait_ge(s_ig, i * 16 + 32)
                    pool.wait_ge(s_tr, i * 4 + 4)
                    pool.sem_inc(s_go, 1)
                    gather()
                    pool.wait_ge(s_is, i * 16 + 16)
                    pool.wait_ge(s_ye, i * 4 + 8)
                    pool.sem_inc(s_go, 1)
                    for b in range(2):
                        pool.indirect_dma_start(x_acc, bass.IndirectOffsetOnAxis(ap=idx_s[:, b, 0:1], axis=0),
                                                y[:, b, :], None, compute_op=ALU.add).then_inc(s_sc, 16)
                    pool.wait_ge(s_sc, i * 32 + 32)
                    pool.sem_inc(s_yfree, 1)
                pool.wait_ge(s_gx, T * 32 + 32)

            @block.tensor
            def _(pe):
                def turn_x(i, first):
                    pe.wait_ge(s_gx, 32 if first else i * 32 + 32)
                    for g in range(4):
                        if g >= 2:
                            pe.wait_ge(s_xte, g - 1 if first else i * 4 + g - 1)
                        elif not first:
                            pe.wait_ge(s_ye, i * 4 + g - 1)
                        for kk in range(2):
                            for b in range(2):
                                m = pe.transpose(bank[6 + g % 2][:, (2 * kk + b) * P:(2 * kk + b + 1) * P],
                                                 xg[:, b, (2 * g + kk) * P:(2 * g + kk + 1) * P], ident)
                        m.then_inc(s_tr, 1)

                turn_x(0, True)
                T = n_passes(pe)
                with pe.Fori(0, T) as i:
                    tokens = pass_value(pe, i, 2, S)

                    def body(N):
                        pe.wait_ge(s_xte, i * 4 + 4)
                        for j in range(KD):
                            pe.wait_ge(s_wd[j], i * 16 + 16)
                            pe.wait_ge(s_gev, i * 8 + j + 5)
                            for half in range(2):
                                for k in range(KD):
                                    m = pe.matmul(bank[j % 4][:, half * 256:half * 256 + N], w_slot[j][:, k, half::2],
                                                  xT[:, k, 0:N], start=(k == 0), stop=(k == KD - 1))
                            m.then_inc(s_gu, 1)
                        turn_x(i + 1, False)
                        for m_ in range(KD):
                            q = NJ + m_ // 2
                            if m_ == 0:
                                pe.wait_ge(s_actd, i * 8 + 8)
                            pe.wait_ge(s_wd[q], i * 16 + 16)
                            pe.wait_ge(s_yev, i * 8 + m_ + 7)
                            for k in range(KD):
                                m = pe.matmul(bank[4 + m_ % 2][:, 0:N], w_slot[q][:, k, (m_ % 2) * P:(m_ % 2 + 1) * P],
                                              actT[:, k, 0:N], start=(k == 0), stop=(k == KD - 1))
                            m.then_inc(s_yt, 1)
                            if m_ == 5:
                                turn_y(i, 0)
                        turn_y(i, 1)

                    def turn_y(i, half):
                        pe.wait_ge(s_yev, i * 8 + 8 + 4 * half + 4)
                        for b in range(2):
                            g = 2 * half + b
                            if half == 0:
                                pe.wait_ge(s_xte, i * 4 + g + 7)
                            else:
                                pe.wait_ge(s_ye, i * 4 + g + 3)
                            for k in range(4):
                                m = pe.transpose(bank[6 + g % 2][:, k * P:(k + 1) * P],
                                                 yT[:, 4 * half + k, b * P:(b + 1) * P], ident)
                            m.then_inc(s_ytr, 1)

                    by_size(pe, tokens, body)

            @block.scalar
            def _(act):
                def take_x(i, first):
                    for g in range(4):
                        act.wait_ge(s_tr, g + 1 if first else i * 4 + g + 1)
                        for kk in range(2):
                            k = 2 * g + kk
                            m = act.activation(xT[:, k, :], bank[6 + g % 2][:, kk * CAP:(kk + 1) * CAP], ACT.Identity,
                                               bias=sh2[:, k:k + 1], scale=a2[:, k:k + 1])
                        m.then_inc(s_xte, 1)

                take_x(0, True)
                T = n_passes(act)
                with act.Fori(0, T) as i:
                    tokens = pass_value(act, i, 2, S)

                    def body(N):
                        for j in range(KD):
                            act.wait_ge(s_gate, i * 8 + j + 1)
                            act.activation(sig_t[:, 0:N], gate_t[:, 0:N], ACT.Sigmoid, scale=SWISH).then_inc(s_sigd, 1)

                    by_size(act, tokens, body)
                    take_x(i + 1, False)
                    act.wait_ge(s_is, i * 16 + 16)
                    act.wait_ge(s_yfree, i + 1)
                    for g in range(4):
                        half, b = divmod(g, 2)
                        act.wait_ge(s_ytr, i * 4 + g + 1)
                        act.activation(y[:, b, half * 512:(half + 1) * 512], bank[6 + g % 2][:, :], ACT.Copy,
                                       scale=wgt[:, b, 1:2]).then_inc(s_ye, 1)

            @block.vector
            def _(v):
                PER = 1 + KD
                v.memset(yT, 0.0)
                v.wait_ge(s_be, 16)
                T = n_passes(v)
                with v.Fori(0, T) as i:
                    e = pass_value(v, i, 0, NE - 1)
                    tokens = pass_value(v, i, 2, S)
                    link = Chain(v, s_v3, i * PER)
                    v.wait_ge(s_yev, i * 8 + 8)
                    v.tensor_scalar(bc, bias_e[:, :, bass.ds(e * KD, KD)], 1.0, None, ALU.mult).then_inc(s_v3, 1)

                    def body(N):
                        link.done = 1
                        v.wait_ge(s_v3, i * PER + 1)
                        for j in range(KD):
                            v.wait_ge(s_gu, i * 8 + j + 9)
                            b = bank[j % 4]
                            v.tensor_scalar(gate_t[:, 0:N], b[:, 0:N], bc[:, 0, j:j + 1], LIMIT, ALU.add, ALU.min).then_inc(s_gate, 1)
                            v.tensor_scalar(up_t[:, 0:N], b[:, 256:256 + N], bc[:, 1, j:j + 1], 1.0 + LIMIT,
                                            ALU.add, ALU.min).then_inc(s_gev, 1)
                            v.wait_ge(s_gate, i * 8 + j + 1)
                            v.wait_ge(s_gev, i * 8 + j + 9)
                            link(v.scalar_tensor_tensor(up_t[:, 0:N], up_t[:, 0:N], 1.0 - LIMIT, gate_t[:, 0:N], ALU.max, ALU.mult))
                            v.wait_ge(s_sigd, i * 8 + j + 1)
                            v.tensor_tensor(actT[:, j, 0:N], up_t[:, 0:N], sig_t[:, 0:N], ALU.mult).then_inc(s_actd, 1)
                            v.wait_ge(s_actd, i * 8 + j + 1)
                        for m_ in range(KD):
                            v.wait_ge(s_yt, i * 8 + m_ + 9)
                            v.tensor_scalar(yT[:, m_, 0:N], bank[4 + m_ % 2][:, 0:N], bc[:, 2, m_:m_ + 1], gt2[:, m_:m_ + 1],
                                            ALU.add, ALU.mult).then_inc(s_yev, 1)
                        assert link.done == 1 + KD

                    by_size(v, tokens, body)

        at = base
        gfb, at = carve(arena, at, D)
        fin, at = carve(arena, at, NT, D)
        sq, at = carve(arena, at, D)
        fs, at = carve(arena, at, 2, NT)
        s_fin = [sem(f"s_fin{i}") for i in range(NT)]
        s_var4, s_rstd4 = sem("s_var4"), sem("s_rstd4")
        s_gf, s_v4, s_res, s_out = map(sem, ("s_gf", "s_v4", "s_res", "s_out"))

        with nc.Block() as block:
            @block.sync
            def _(sp):
                sp.dma_start(gfb, g_final.rearrange("(o d) -> o d", o=1).broadcast_to((P, D))).then_inc(s_gf, 16)
                for i in range(NT):
                    sp.dma_start(fin[:, i, :], x_acc[i * P:(i + 1) * P, :]).then_inc(s_fin[i], 16)
                for i in range(NT):
                    sp.wait_ge(s_res, i + 1)
                    sp.dma_start(out2d[i * P:(i + 1) * P, :], fin[:, i, :]).then_inc(s_out, 16)
                sp.wait_ge(s_out, 16 * NT)

            @block.gpsimd
            def _(pool):
                for i in range(NT):
                    pool.wait_ge(s_var4, i + 1)
                    pool.tensor_tensor(fs[:, 1, i:i + 1], fs[:, 1, i:i + 1], mhalf[:, 0:1], ALU.pow).then_inc(s_rstd4, 1)

            @block.vector
            def _(v):
                link = Chain(v, s_v4, 0)
                v.wait_ge(s_gf, 16)
                for i in range(NT):
                    v.wait_ge(s_fin[i], 16)
                    link(v.tensor_tensor_reduce(sq, fin[:, i, :], fin[:, i, :], 1.0, 0.0, ALU.mult, ALU.add, fs[:, 0, i:i + 1]))
                    v.tensor_scalar(fs[:, 1, i:i + 1], fs[:, 0, i:i + 1], 1.0 / D, 1e-6, ALU.mult, ALU.add).then_inc(s_var4, 1)
                    v.wait_ge(s_rstd4, i + 1)
                    v.scalar_tensor_tensor(fin[:, i, :], fin[:, i, :], fs[:, 1, i:i + 1], gfb, ALU.mult, ALU.mult).then_inc(s_res, 1)


_INS = ["x", "c", "positions", "w_ada", "b_ada", "g_norm1", "w_in", "g_q_norm", "w_uq", "g_kv_norm", "w_ukv",
        "lambda_q1", "lambda_k1", "lambda_q2", "lambda_k2", "g_subln", "w_out", "g_norm2", "w_router", "b_router",
        "w_gate_up", "b_gate_up", "w_down", "b_down", "g_final"]
_OUTS = [((1, S, D), "float32")]


def kernel(**inputs):
    import numpy as _np
    import concourse.bacc as _bacc
    from concourse import mybir as _mybir
    from concourse.bass_utils import run_bass_kernel_spmd as _run

    nc = _bacc.Bacc("TRN2", target_bir_lowering=False, num_devices=1)
    arrays, args = {}, []
    for name in _INS:
        a = _np.ascontiguousarray(inputs[name])
        arrays[f"in_{name}_dram"] = a
        args.append(nc.dram_tensor(f"in_{name}_dram", a.shape, _mybir.dt.from_np(a.dtype), kind="ExternalInput").ap())
    for i, (shape, dtype) in enumerate(_OUTS):
        dt = _mybir.dt.from_np(_np.dtype(dtype))
        args.append(nc.dram_tensor(f"out_{i}_dram", shape, dt, kind="ExternalOutput").ap())
    hybrid_block(nc, *args)
    r = _run(nc, [arrays], core_ids=[0])
    return r.results[0]["out_0_dram"]
```

```python
from contextlib import ExitStack

import numpy as np
import concourse.bass as bass
from concourse import mybir

F32 = mybir.dt.float32
I32 = mybir.dt.int32
U32 = mybir.dt.uint32
ALU = mybir.AluOpType
ACT = mybir.ActivationFunctionType
AX_X = mybir.AxisListType.X

P = 128
D = 1024
KD = D // P
S = 1024
NT = S // P
HM, NOPE, ROPE, DV_M = 8, 64, 32, 64
QK = NOPE + ROPE
QR, KVR = 384, 256
KQ, KKV = QR // P, KVR // P
HD, DH = 4, 64
DROPE = DH // 4
FM, FD = ROPE // 2, DROPE // 2
THETA = 500000.0
CHUNK = 64
NCOL = QR + KVR + ROPE + 3 * HD * 2 * DH
C_DQ = QR + KVR + ROPE
NE, TOPK = 32, 4
LIMIT, SWISH = 7.0, 1.702
LAMBDA_INIT = 0.8 - 0.6
CAP = 256
SIZES = (128, 136, 144, 152, 160, 168, 176, 256)
MAXPASS = NE + S * TOPK // CAP
NPASS_ROWS = 128
DUMMY = S
NROW = S + CAP
SCALE_M = float(QK) ** -0.5
SCALE_D = float(DH) ** -0.5
WIDE = 512 // P
MASKED = -1.0e30
MAGIC = 12582912.0
TWO_PI = 2 * np.pi
PI_1 = 6.28125
PI_2 = float(np.float32(round((TWO_PI - PI_1) * 2 ** 21) / 2 ** 21))
PI_3 = float(TWO_PI - PI_1 - PI_2)
PI_IN = 3.1415925

R_C, R_BADA, R_G1, R_G2, R_GQ, R_GKV, R_SUB = 0, 8, 56, 64, 72, 75, 77
NR = 78


def carve(arena, at, *shape):
    n = int(np.prod(shape))
    view = arena[:, at:at + n]
    if len(shape) == 2:
        view = view.rearrange("p (a b) -> p a b", a=shape[0])
    elif len(shape) == 3:
        view = view.rearrange("p (a b c) -> p a b c", a=shape[0], b=shape[1])
    return view, at + n


class Chain:

    def __init__(self, eng, sem, base):
        self.eng, self.sem, self.base, self.done = eng, sem, base, 0

    def __call__(self, ins):
        self.done += 1
        ins.then_inc(self.sem, 1)
        self.eng.wait_ge(self.sem, self.base + self.done)


def attention_plan():
    units = [(i, u) for i in range(NT) for u in range(HM + HD)]
    tail = {1: "oT", 3: "mix0", 5: "mix1", 7: "xT", 9: "router", 11: "rank"}
    scored = 0
    steps, group = [], 0

    def put(kind, i, u):
        nonlocal group
        steps.append((kind, i, u, group))
        if kind == "T":
            group += i // 4 + 1
        elif kind in ("oT", "xT"):
            group += 2

    for n, (i, u) in enumerate(units):
        last = item(i, u) + (0 if u < HM else 1)
        while scored <= last:
            put("S", scored // 16, scored)
            scored += 1
        if u >= HM:
            put("W", i, u)
        while scored < item(NT, 0) and scored <= last + (3 if scored // 16 < WIDE else 2):
            put("S", scored // 16, scored)
            scored += 1
        put("T", i, u)
        if n:
            put("PV", *units[n - 1])
        if i and u in tail:
            put(tail[u], i - 1, 0)
    put("PV", *units[-1])
    for kind in ("oT", "mix0", "mix1", "xT", "router", "rank"):
        put(kind, NT - 1, 0)
    return steps


def item(i, u):
    return 16 * i + (u if u < HM else HM + 2 * (u - HM))


def slots_of(n, narrow):
    return {n % narrow} if n // 16 < WIDE else {2 * (n % (narrow // 2)), 2 * (n % (narrow // 2)) + 1}


def last_in_slots(n, narrow):
    return next((m for m in range(n - 1, -1, -1) if slots_of(m, narrow) & slots_of(n, narrow)), None)


def unit_of(n):
    i, r = divmod(n, 16)
    return i, (r if r < HM else HM + (r - HM) // 2)


def hybrid_block(nc, x, c, positions, w_ada, b_ada, g_norm1, w_in, g_q_norm, w_uq, g_kv_norm, w_ukv,
                 lambda_q1, lambda_k1, lambda_q2, lambda_k2, g_subln, w_out, g_norm2,
                 w_router, b_router, w_gate_up, b_gate_up, w_down, b_down, g_final, out):
    x2d = x.rearrange("b s d -> (b s) d")
    out2d = out.rearrange("b s d -> (b s) d")
    w_ada_v = w_ada[0].rearrange("(k p) n -> p k n", p=P)
    w_in_v = w_in[0].rearrange("(k p) n -> p k n", p=P)
    w_gu_v = w_gate_up.rearrange("l e (k p) n -> p (l e) k n", p=P)
    w_dn_v = w_down.rearrange("l e (k p) n -> p (l e) k n", p=P)

    q_scr = nc.dram_tensor("q_scr", (NT, P, HM * P), F32).ap()
    dq_scr = nc.dram_tensor("dq_scr", (NT, P, HD * P), F32).ap()
    x_hat = nc.dram_tensor("x_hat", (NROW, D), F32).ap()
    x_acc = nc.dram_tensor("x_acc", (NROW, D), F32).ap()
    table = nc.dram_tensor("table", (NE * S, 2), I32).ap()
    gt1_scr = nc.dram_tensor("gt1_scr", (P, D), F32).ap()
    bias_scr = nc.dram_tensor("bias_scr", (P, 3 * NE * KD), F32).ap()
    passes = nc.dram_tensor("passes", (NPASS_ROWS, 4), I32).ap()

    with ExitStack() as ctx:
        def sem(name):
            return ctx.enter_context(nc.semaphore(name))

        arena = ctx.enter_context(nc.sbuf_tensor("arena", [P, 53100], F32))
        scores = ctx.enter_context(nc.psum_tensor("scores", [P, 4 * 512], F32))
        bank = [scores[:, b * 512:(b + 1) * 512] for b in range(4)]
        bank += [ctx.enter_context(nc.psum_tensor(f"bank{b}", [P, 512], F32)) for b in range(4, 8)]

        at = 0
        ident, at = carve(arena, at, P)
        ones, at = carve(arena, at, P)
        before, at = carve(arena, at, P)
        iota_e, at = carve(arena, at, NE)
        iota_p, at = carve(arena, at, 1)
        cols, at = carve(arena, at, 80)
        mods, at = carve(arena, at, 48)
        a1, at = carve(arena, at, KD)
        a2, at = carve(arena, at, KD)
        gsub, at = carve(arena, at, 1)
        neg_lam, at = carve(arena, at, 1)
        cos_t, at = carve(arena, at, NT, FM + FD)
        sin_t, at = carve(arena, at, NT, FM + FD)
        small, at = carve(arena, at, 32)
        mhalf, at = carve(arena, at, TOPK)
        base = at
        sh1, sh2, gt2 = mods[:, 0:8], mods[:, 24:32], mods[:, 40:48]

        kT, at = carve(arena, base, HM, S)
        v_m, at = carve(arena, at, NT, HM * DV_M)
        dkT, at = carve(arena, at, HD, S)
        v_d, at = carve(arena, at, NT, HD * 2 * DH)
        work = at
        NRING = 5
        ada = [carve(arena, base + r * KD * 512, KD, 512)[0] for r in range(NRING)]

        NJ, ND = 2 * D // 256, D // 256
        NW = NJ + ND
        w_slot = [carve(arena, base + q * KD * 256, KD, 256)[0] for q in range(NW)]
        NEARLY = (work - base) // (KD * 256)
        s_wd = [sem(f"s_wd{q}") for q in range(NW)]

        def w_piece(e, q):
            e = bass.ds(e, 1) if not isinstance(e, int) else slice(e, e + 1)
            src = (w_gu_v[:, e, :, q * 256:(q + 1) * 256] if q < NJ else
                   w_dn_v[:, e, :, (q - NJ) * 256:(q - NJ + 1) * 256])
            return src.rearrange("p o k n -> p (o k) n")

        win, at = carve(arena, work, KD, NCOL)
        wuq, at = carve(arena, at, KQ, HM * QK)
        wukv, at = carve(arena, at, KKV, HM * (NOPE + DV_M))
        p1 = at
        rows, at = carve(arena, p1, P)
        posi, at = carve(arena, at, P)
        posf, at = carve(arena, at, P)
        pos_c, at = carve(arena, at, NT)
        freq, at = carve(arena, at, FM + FD)
        ang, at = carve(arena, at, NT, FM + FD)
        turns, at = carve(arena, at, NT, FM + FD)
        wide, at = carve(arena, at, NT, FM + FD)
        lam4, at = carve(arena, at, 4, DH)
        brow, at = carve(arena, at, 2, 256)
        drow, at = carve(arena, at, 2, P)
        scb, at = carve(arena, at, KD, P)
        bada_b, at = carve(arena, at, D)
        picked, at = carve(arena, at, 4, P)
        tinit, at = carve(arena, at, 256, 2)
        zero, at = carve(arena, at, D)
        gt1b, at = carve(arena, at, D)
        bias_e, at = carve(arena, at, 3, NE * KD)
        posi = posi.bitcast(I32)
        tinit = tinit.bitcast(I32)
        sig = small[:, 0:8]
        silu = small[:, 8:16]
        lam_s = small[:, 16:24]
        assert at <= 53100

        s_cst, s_rows, s_pos, s_lamld, s_brow, s_bada = map(sem, ("s_cst", "s_rows", "s_pos", "s_lamld", "s_brow", "s_bada"))
        s_ada = [sem(f"s_ada{r}") for r in range(NRING)]
        s_win, s_colT, s_cols, s_sig, s_silu, s_posf, s_posT = map(
            sem, ("s_win", "s_colT", "s_cols", "s_sig", "s_silu", "s_posf", "s_posT"))
        s_adau, s_gt1, s_bT, s_lam, s_lame, s_ang, s_sin, s_v0, s_tab, s_zero = map(
            sem, ("s_adau", "s_gt1", "s_bT", "s_lam", "s_lame", "s_ang", "s_sin", "s_v0", "s_tab", "s_zero"))
        s_keep, s_adae = sem("s_keep"), sem("s_adae")
        NADA = 12

        with nc.Block() as block:
            @block.sync
            def _(sp):
                for row, src, n in ((R_C, c[0], KD), (R_BADA, b_ada[0], 48), (R_G1, g_norm1[0], KD),
                                    (R_G2, g_norm2[0], KD), (R_GQ, g_q_norm[0], KQ), (R_GKV, g_kv_norm[0], KKV),
                                    (R_SUB, g_subln[0], 1)):
                    sp.dma_start(rows[row:row + n, :], src.rearrange("(r p) -> r p", p=P)).then_inc(s_rows, 16)
                sp.dma_start(posi[0:NT, :], positions.rearrange("b (t p) -> (b t) p", p=P)).then_inc(s_pos, 16)
                for q, src in enumerate((lambda_q1, lambda_k1, lambda_q2, lambda_k2)):
                    sp.dma_start(lam4[:, q, :], src.broadcast_to((P, DH))).then_inc(s_lamld, 16)
                sp.dma_start(bada_b, b_ada[0:1, 2 * D:3 * D].broadcast_to((P, D))).then_inc(s_bada, 16)
                for h in range(2):
                    sp.dma_start(brow[:, h, :], b_gate_up[0, 16 * h:16 * h + 16].rearrange(
                        "e (j n) -> (e j) n", j=KD)).then_inc(s_brow, 16)
                    sp.dma_start(drow[:, h, :], b_down[0, 16 * h:16 * h + 16].rearrange(
                        "e (j n) -> (e j) n", j=KD)).then_inc(s_brow, 16)
                for q in range(4):
                    sp.dma_start(ada[q], w_ada_v[:, :, q * 512:(q + 1) * 512]).then_inc(s_ada[q], 16)
                sp.wait_ge(s_cst, 7)
                sp.dma_start(table.rearrange("(p j) w -> p j w", p=P), tinit).then_inc(s_tab, 16)
                for r in range(S, NROW, P):
                    sp.dma_start(x_hat[r:r + P, :], zero).then_inc(s_tab, 16)
                    sp.dma_start(x_acc[r:r + P, :], zero).then_inc(s_tab, 16)
                sp.dma_start(wuq, w_uq[0].rearrange("(k p) n -> p k n", p=P)).then_inc(s_win, 16)
                sp.dma_start(wukv, w_ukv[0].rearrange("(k p) n -> p k n", p=P)).then_inc(s_win, 16)
                for q in range(4, NADA):
                    if q >= NRING:
                        sp.wait_ge(s_adau, q - NRING + 1)
                    sp.dma_start(ada[q % NRING], w_ada_v[:, :, q * 512:(q + 1) * 512]).then_inc(s_ada[q % NRING], 16)
                    sp.dma_start(win[:, q - 4, :], w_in_v[:, q - 4, :]).then_inc(s_win, 16)
                sp.wait_ge(s_adae, 6)
                sp.dma_start(gt1_scr, gt1b).then_inc(s_tab, 16)
                sp.wait_ge(s_keep, 1)
                sp.dma_start(bias_scr, bias_e.rearrange("p a n -> p (a n)")).then_inc(s_tab, 16)
                sp.wait_ge(s_tab, 16 * (3 + 2 * CAP // P))
                sp.wait_ge(s_win, 16 * (2 + KD))

            @block.gpsimd
            def _(pool):
                pool.memset(ident, 0.0).then_inc(s_cst, 1)
                pool.memset(ones, 1.0).then_inc(s_cst, 1)
                pool.wait_ge(s_cst, 2)
                pool.affine_select(out=ident, in_=ident, compare_op=ALU.not_equal, fill=1.0, base=0,
                                   pattern=[[-1, P]], channel_multiplier=1).then_inc(s_cst, 1)
                pool.affine_select(out=before, in_=ones, compare_op=ALU.is_gt, fill=0.0, base=0,
                                   pattern=[[1, P]], channel_multiplier=-1).then_inc(s_cst, 1)
                for f in range(FM + FD):
                    n, half = (f, FM) if f < FM else (f - FM, FD)
                    pool.memset(freq[:, f:f + 1], float(np.float32(THETA ** (-n / half))))
                pool.memset(mhalf, -0.5)
                pool.iota(iota_e, [[1, NE]], 0, 0, allow_small_or_imprecise_dtypes=True)
                pool.iota(iota_p, [[1, 1]], 0, 1, allow_small_or_imprecise_dtypes=True).then_inc(s_cst, 1)
                pool.iota(tinit[:, :, 0], [[1, CAP]], DUMMY, 0).then_inc(s_cst, 1)
                pool.memset(zero, 0.0)
                pool.memset(tinit[:, :, 1], 0).then_inc(s_cst, 1)

            @block.tensor
            def _(pe):
                pe.wait_ge(s_cst, 4)
                pe.wait_ge(s_rows, 16 * 7)
                pe.transpose(bank[0][:, 0:NR], rows[0:NR, :], ident[0:NR, 0:NR]).then_inc(s_colT, 1)
                pe.wait_ge(s_posf, 1)
                pe.transpose(bank[0][:, 128:128 + NT], posf[0:NT, :], ident[0:NT, 0:NT]).then_inc(s_posT, 1)
                pe.wait_ge(s_brow, 64)
                for h in range(2):
                    pe.transpose(bank[4][:, h * P:(h + 1) * P], brow[:, h, 0::2], ident)
                    pe.transpose(bank[4][:, (2 + h) * P:(3 + h) * P], brow[:, h, 1::2], ident)
                    pe.transpose(bank[5][:, h * P:(h + 1) * P], drow[:, h, :], ident).then_inc(s_bT, 1)
                pe.wait_ge(s_silu, 2)
                for q in range(NADA):
                    pe.wait_ge(s_ada[q % NRING], 16 * (q // NRING + 1))
                    if q >= 2:
                        pe.wait_ge(s_adae, q - 1)
                    for k in range(KD):
                        m = pe.matmul(bank[2 + q % 2][:, :], scb[:, k, :], ada[q % NRING][:, k, :],
                                      start=(k == 0), stop=(k == KD - 1))
                    m.then_inc(s_adau, 1)

            @block.scalar
            def _(act):
                act.wait_ge(s_cols, 1)
                act.activation(sig, cols[:, R_C:R_C + KD], ACT.Sigmoid).then_inc(s_sig, 1)
                act.wait_ge(s_lam, 2)
                act.activation(lam_s[:, 2:4], lam_s[:, 0:2], ACT.Exp).then_inc(s_lame, 1)
                act.wait_ge(s_ang, 1)
                act.activation(sin_t, ang, ACT.Sin).then_inc(s_sin, 1)
                act.activation(cos_t, wide, ACT.Sin).then_inc(s_sin, 1)

            @block.vector
            def _(v):
                link = Chain(v, s_v0, 0)

                v.wait_ge(s_colT, 1)
                v.tensor_copy(cols[:, 0:NR], bank[0][:, 0:NR]).then_inc(s_cols, 1)
                v.wait_ge(s_pos, 16)
                v.tensor_copy(posf[0:NT, :], posi[0:NT, :]).then_inc(s_posf, 1)
                v.wait_ge(s_sig, 1)
                v.wait_ge(s_cols, 1)
                v.tensor_tensor(silu, cols[:, R_C:R_C + KD], sig, ALU.mult).then_inc(s_silu, 1)
                v.wait_ge(s_silu, 1)
                v.tensor_copy(scb, silu.rearrange("p (k o) -> p k o", o=1).broadcast_to((P, KD, P))).then_inc(s_silu, 1)
                v.wait_ge(s_lamld, 64)
                for q in range(2):
                    v.tensor_tensor_reduce(lam4[:, 2 * q, :], lam4[:, 2 * q, :], lam4[:, 2 * q + 1, :], 1.0, 0.0,
                                           ALU.mult, ALU.add, lam_s[:, q:q + 1]).then_inc(s_lam, 1)
                v.wait_ge(s_lame, 1)
                link(v.tensor_tensor(lam_s[:, 4:5], lam_s[:, 3:4], lam_s[:, 2:3], ALU.subtract))
                link(v.tensor_scalar(neg_lam, lam_s[:, 4:5], -LAMBDA_INIT, None, ALU.add))
                link(v.tensor_scalar(gsub, cols[:, R_SUB:R_SUB + 1], 1.0 - LAMBDA_INIT, None, ALU.mult))
                v.wait_ge(s_posT, 1)
                link(v.tensor_copy(pos_c, bank[0][:, 128:128 + NT]))
                v.wait_ge(s_cst, 5)
                link(v.tensor_tensor(ang, pos_c.rearrange("p (t o) -> p t o", o=1).broadcast_to((P, NT, FM + FD)),
                                     freq.rearrange("p (o f) -> p o f", o=1).broadcast_to((P, NT, FM + FD)), ALU.mult))
                link(v.tensor_scalar(turns, ang, 1.0 / TWO_PI, MAGIC, ALU.mult, ALU.add))
                link(v.tensor_scalar(turns, turns, MAGIC, None, ALU.subtract))
                for part in (PI_1, PI_2, PI_3):
                    link(v.scalar_tensor_tensor(ang, turns, -part, ang, ALU.mult, ALU.add))
                link(v.tensor_scalar(turns, ang, float(np.pi / 2), -TWO_PI, ALU.is_gt, ALU.mult))
                link(v.scalar_tensor_tensor(wide, ang, float(np.pi / 2), turns, ALU.add, ALU.add))
                link(v.tensor_scalar(wide, wide, PI_IN, -PI_IN, ALU.min, ALU.max))
                v.tensor_scalar(ang, ang, PI_IN, -PI_IN, ALU.min, ALU.max).then_inc(s_ang, 1)
                v.wait_ge(s_bT, 2)
                link(v.tensor_copy(bias_e[:, 0, :], bank[4][:, 0:256]))
                link(v.tensor_scalar(bias_e[:, 1, :], bank[4][:, 256:512], 1.0, None, ALU.add))
                v.tensor_copy(bias_e[:, 2, :], bank[5][:, 0:256]).then_inc(s_keep, 1)
                v.wait_ge(s_bada, 16)
                for q in range(NADA):
                    v.wait_ge(s_adau, q + 1)
                    if q in (4, 5):
                        half = slice((q - 4) * 512, (q - 3) * 512)
                        v.tensor_tensor(gt1b[:, half], bank[2 + q % 2][:, :], bada_b[:, half], ALU.add).then_inc(s_adae, 1)
                    else:
                        v.tensor_tensor(picked, bank[2 + q % 2][:, :].rearrange("p (j n) -> p j n", j=4),
                                        ident.rearrange("p (o n) -> p o n", o=1).broadcast_to((P, 4, P)),
                                        ALU.mult).then_inc(s_adae, 1)
                        v.wait_ge(s_adae, q + 1)
                        link(v.reduce_sum(mods[:, 4 * q:4 * q + 4], picked, AX_X))
                link(v.tensor_tensor(mods[:, 0:16], mods[:, 0:16], cols[:, R_BADA:R_BADA + 16], ALU.add))
                link(v.tensor_tensor(mods[:, 24:48], mods[:, 24:48], cols[:, R_BADA + 24:R_BADA + 48], ALU.add))
                v.scalar_tensor_tensor(a1, mods[:, 8:16], 1.0, cols[:, R_G1:R_G1 + 8], ALU.add, ALU.mult)
                v.scalar_tensor_tensor(a2, mods[:, 32:40], 1.0, cols[:, R_G2:R_G2 + 8], ALU.add, ALU.mult)

        at = p1
        hT, at = carve(arena, at, KD, P)
        xt, at = carve(arena, at, D)
        cqn, at = carve(arena, at, QR)
        ckn, at = carve(arena, at, KVR)
        kpe, at = carve(arena, at, ROPE)
        cT, at = carve(arena, at, KQ + KKV, P)
        qf, at = carve(arena, at, HM, QK)
        kf, at = carve(arena, at, HM, QK)
        dqk_at = at
        dqk, at = carve(arena, at, 16, DH)
        qT_o, at = carve(arena, at, HM, P)
        dqT_o, at = carve(arena, at, HD, P)
        rot, at = carve(arena, at, 512)
        rot_a, rot_b = rot[:, 0:256], rot[:, 256:512]
        cs, at = carve(arena, at, 2, FM + FD)
        st1, at = carve(arena, at, 8)
        assert at <= 53100, at
        junk = carve(arena, dqk_at, QR)[0]

        names = ("pKV pQ pDQ pDK pDV tKV tQ up0 up1 uq0 uq1 tDQ tDK tK0 tK1 tN0 tN1 "
                 "ssKV ssQ eDQ eDK cTk cTq qup0 qup1 dqTo qTo "
                 "ckn cqn vd drot kv0 kv1 qfin dkT kT0 kT1 stored").split()
        ahead = "xn tX0 tX1 hT".split()
        ev = {n: sem("l_" + n) for n in names + ahead}
        s_x, s_qst, s_v1, s_var, s_rstd = map(sem, ("s_x", "s_qst", "s_v1", "s_var", "s_rstd"))

        def now(t):
            return t + 2

        def prev(t):
            return t + 1

        with nc.Block() as block:
            @block.sync
            def _(sp):
                sp.dma_start(xt, x2d[0:P, :]).then_inc(s_x, 16)
                with sp.Fori(0, NT) as t:
                    sp.wait_ge(ev["tX1"], prev(t))
                    sp.dma_start(xt, x2d.rearrange("(t p) d -> t p d", p=P)[bass.ds((t + 1) % NT, 1)]
                                 .rearrange("o p d -> p (o d)")).then_inc(s_x, 16)
                    sp.wait_ge(ev["dqTo"], now(t))
                    sp.dma_start(dq_scr[bass.ds(t, 1)].rearrange("o p n -> p (o n)"),
                                 dqT_o.rearrange("p h n -> p (h n)")).then_inc(s_qst, 16)
                    sp.wait_ge(ev["qTo"], now(t))
                    sp.dma_start(q_scr[bass.ds(t, 1), 0:QK].rearrange("o p n -> p (o n)"),
                                 qT_o[0:QK].rearrange("p h n -> p (h n)")).then_inc(s_qst, 16)
                    sp.wait_ge(s_qst, t * 32 + 32)
                    sp.sem_inc(ev["stored"], 1)
                sp.wait_ge(s_x, 16 * (NT + 1))

            @block.gpsimd
            def _(pool):
                for n in names:
                    pool.sem_inc(ev[n], 1)

                def root(count, col):
                    pool.wait_ge(s_var, count)
                    pool.tensor_tensor(st1[:, col:col + 1], st1[:, col:col + 1], mhalf[:, 0:1], ALU.pow).then_inc(s_rstd, 1)

                root(1, 3)
                with pool.Fori(0, NT) as t:
                    root(t * 3 + 2, 4)
                    root(t * 3 + 3, 5)
                    root(t * 3 + 4, 3)

            @block.tensor
            def _(pe):
                def turn_x():
                    for g in range(2):
                        for k in range(4 * g, 4 * g + 4):
                            m = pe.transpose(bank[5 + g][:, (k % 4) * P:(k % 4 + 1) * P], xt[:, k * P:(k + 1) * P], ident)
                        m.then_inc(ev[f"tX{g}"], 1)

                pe.wait_ge(ev["xn"], 1)
                turn_x()
                with pe.Fori(0, NT) as t:
                    pe.wait_ge(ev["hT"], prev(t))
                    for name, b, lo, n, free in (("pKV", 0, QR, KVR + ROPE, "dqTo"), ("pQ", 1, 0, QR, "dkT"),
                                                 ("pDQ", 2, C_DQ, 512, "qTo"), ("pDK", 3, C_DQ + 512, 512, "qTo"),
                                                 ("pDV", 4, C_DQ + 1024, 512, "qup0")):
                        pe.wait_ge(ev[free], prev(t))
                        for k in range(KD):
                            m = pe.matmul(bank[b][:, 0:n], hT[:, k, :], win[:, k, lo:lo + n],
                                          start=(k == 0), stop=(k == KD - 1))
                        m.then_inc(ev[name], 1)
                    pe.wait_ge(ev["ckn"], now(t))
                    for k in range(KKV):
                        m = pe.transpose(bank[0][:, k * P:(k + 1) * P], ckn[:, k * P:(k + 1) * P], ident)
                    m.then_inc(ev["tKV"], 1)
                    pe.wait_ge(ev["cqn"], now(t))
                    for k in range(KQ):
                        m = pe.transpose(bank[1][:, k * P:(k + 1) * P], cqn[:, k * P:(k + 1) * P], ident)
                    m.then_inc(ev["tQ"], 1)
                    pe.wait_ge(ev["xn"], now(t))
                    pe.wait_ge(ev["kT0"], prev(t))
                    pe.wait_ge(ev["kT1"], prev(t))
                    turn_x()
                    pe.wait_ge(ev["cTk"], now(t))
                    for g, free in ((0, "eDQ"), (1, "eDK")):
                        pe.wait_ge(ev[free], now(t))
                        for k in range(KKV):
                            m = pe.matmul(bank[2 + g][:, :], cT[:, k, :], wukv[:, k, g * 512:(g + 1) * 512],
                                          start=(k == 0), stop=(k == KKV - 1))
                        m.then_inc(ev[f"up{g}"], 1)
                    pe.wait_ge(ev["cTq"], now(t))
                    pe.wait_ge(ev["vd"], now(t))
                    pe.wait_ge(ev["qup1"], prev(t))
                    for g, b in ((0, 4), (1, 7)):
                        for k in range(KQ):
                            m = pe.matmul(bank[b][:, 0:4 * QK], cT[:, KKV + k, :], wuq[:, k, g * 4 * QK:(g + 1) * 4 * QK],
                                          start=(k == 0), stop=(k == KQ - 1))
                        m.then_inc(ev[f"uq{g}"], 1)
                    pe.wait_ge(ev["drot"], now(t))
                    for g, (name, free) in enumerate((("tDQ", "cTk"), ("tDK", "cTq"))):
                        pe.wait_ge(ev[free], now(t))
                        for h in range(HD):
                            m = pe.transpose(bank[g][:, h * P:(h + 1) * P],
                                             dqk[:, 8 * g + 2 * h:8 * g + 2 * h + 2, :].rearrange("p a d -> p (a d)"), ident)
                        m.then_inc(ev[name], 1)
                    pe.wait_ge(ev["kv1"], now(t))
                    pe.wait_ge(ev["hT"], now(t))
                    for g in range(2):
                        for h in range(4):
                            m = pe.transpose(bank[5 + g][0:QK, h * P:(h + 1) * P], kf[:, 4 * g + h, :], ident)
                        m.then_inc(ev[f"tK{g}"], 1)
                    pe.wait_ge(ev["qfin"], now(t))
                    for g in range(2):
                        for h in range(4):
                            m = pe.transpose(bank[2 + g][0:QK, h * P:(h + 1) * P], qf[:, 4 * g + h, :], ident)
                        m.then_inc(ev[f"tN{g}"], 1)

            @block.scalar
            def _(act):
                def modulate():
                    for k in range(KD):
                        m = act.activation(hT[:, k, :], bank[5 + k // 4][:, (k % 4) * P:(k % 4 + 1) * P], ACT.Identity,
                                           bias=sh1[:, k:k + 1], scale=a1[:, k:k + 1])
                    m.then_inc(ev["hT"], 1)

                act.wait_ge(ev["tX0"], 1)
                act.wait_ge(ev["tX1"], 1)
                modulate()
                with act.Fori(0, NT) as t:
                    act.wait_ge(ev["tDK"], prev(t))
                    act.wait_ge(ev["pKV"], now(t))
                    act.activation(junk[:, 0:KVR], bank[0][:, 0:KVR], ACT.Square, accum_out=st1[:, 0:1]).then_inc(ev["ssKV"], 1)
                    act.wait_ge(ev["pQ"], now(t))
                    act.wait_ge(ev["ssKV"], now(t))
                    act.activation(junk, bank[1][:, 0:QR], ACT.Square, accum_out=st1[:, 1:2]).then_inc(ev["ssQ"], 1)
                    act.wait_ge(ev["pDQ"], now(t))
                    act.wait_ge(ev["ssQ"], now(t))
                    act.activation(dqk[:, 0:8, :].rearrange("p a d -> p (a d)"), bank[2][:, :], ACT.Copy).then_inc(ev["eDQ"], 1)
                    act.wait_ge(ev["pDK"], now(t))
                    act.activation(dqk[:, 8:16, :].rearrange("p a d -> p (a d)"), bank[3][:, :], ACT.Copy).then_inc(ev["eDK"], 1)
                    act.wait_ge(ev["tKV"], now(t))
                    for k in range(KKV):
                        m = act.activation(cT[:, k, :], bank[0][:, k * P:(k + 1) * P], ACT.Copy, scale=cols[:, R_GKV + k:R_GKV + k + 1])
                    m.then_inc(ev["cTk"], 1)
                    act.wait_ge(ev["tQ"], now(t))
                    for k in range(KQ):
                        m = act.activation(cT[:, KKV + k, :], bank[1][:, k * P:(k + 1) * P], ACT.Copy, scale=cols[:, R_GQ + k:R_GQ + k + 1])
                    m.then_inc(ev["cTq"], 1)
                    act.wait_ge(ev["tX0"], now(t))
                    act.wait_ge(ev["tX1"], now(t))
                    modulate()
                    act.wait_ge(ev["uq0"], now(t))
                    act.wait_ge(ev["tN1"], prev(t))
                    act.activation(qf[:, 0:4, :].rearrange("p h d -> p (h d)"), bank[4][:, 0:4 * QK], ACT.Copy).then_inc(ev["qup0"], 1)
                    act.wait_ge(ev["uq1"], now(t))
                    act.activation(qf[:, 4:8, :].rearrange("p h d -> p (h d)"), bank[7][:, 0:4 * QK], ACT.Copy).then_inc(ev["qup1"], 1)
                    act.wait_ge(ev["stored"], prev(t))
                    act.wait_ge(ev["tDQ"], now(t))
                    act.activation(dqT_o.rearrange("p h n -> p (h n)"), bank[0][:, :], ACT.Copy,
                                   scale=SCALE_D).then_inc(ev["dqTo"], 1)
                    act.wait_ge(ev["tN0"], now(t))
                    act.activation(qT_o[0:QK, 0:4, :].rearrange("p h n -> p (h n)"), bank[2][0:QK, :], ACT.Copy, scale=SCALE_M)
                    act.wait_ge(ev["tN1"], now(t))
                    act.activation(qT_o[0:QK, 4:8, :].rearrange("p h n -> p (h n)"), bank[3][0:QK, :], ACT.Copy,
                                   scale=SCALE_M).then_inc(ev["qTo"], 1)

            @block.vector
            def _(v):
                def rstd(count, out, ss, n, eps):
                    v.tensor_scalar(out, ss, 1.0 / n, eps, ALU.mult, ALU.add).then_inc(s_var, 1)
                    v.wait_ge(s_rstd, count)

                def norm_x(link, count):
                    for h in range(2):
                        link(v.tensor_tensor_reduce(rot, xt[:, h * 512:(h + 1) * 512], xt[:, h * 512:(h + 1) * 512], 1.0, 0.0,
                                                    ALU.mult, ALU.add, st1[:, 6 + h:7 + h]))
                    link(v.tensor_tensor(st1[:, 2:3], st1[:, 6:7], st1[:, 7:8], ALU.add))
                    rstd(count, st1[:, 3:4], st1[:, 2:3], D, 1e-6)
                    v.tensor_scalar(xt, xt, st1[:, 3:4], None, ALU.mult).then_inc(ev["xn"], 1)

                def rotate(link, z, out, n, F, lo):
                    ra = rot_a[:, 0:2 * n * F].rearrange("p (g a f) -> p g a f", g=n, a=2)
                    rb = rot_b[:, 0:2 * n * F].rearrange("p (g a f) -> p g a f", g=n, a=2)
                    cw = cs[:, 0:1, lo:lo + F].rearrange("p (g a) f -> p g a f", g=1).broadcast_to((P, n, 2, F))
                    sw = cs[:, 1:2, lo:lo + F].rearrange("p (g a) f -> p g a f", g=1).broadcast_to((P, n, 2, F))
                    link(v.tensor_tensor(ra, z, cw, ALU.mult))
                    link(v.tensor_tensor(rb, z, sw, ALU.mult))
                    link(v.tensor_tensor(out[:, :, 0, :], ra[:, :, 0, :], rb[:, :, 1, :], ALU.subtract))
                    return v.tensor_tensor(out[:, :, 1, :], ra[:, :, 1, :], rb[:, :, 0, :], ALU.add)

                PRE, PER = 3, 18
                v.wait_ge(s_x, 16)
                link = Chain(v, s_v1, 0)
                norm_x(link, 1)
                assert link.done == PRE
                with v.Fori(0, NT) as t:
                    link = Chain(v, s_v1, t * PER + PRE)
                    link(v.tensor_scalar(cs[:, 0:1, :], cos_t[:, bass.ds(t, 1), :], 1.0, None, ALU.mult))
                    link(v.tensor_scalar(cs[:, 1:2, :], sin_t[:, bass.ds(t, 1), :], 1.0, None, ALU.mult))
                    v.wait_ge(ev["ssKV"], now(t))
                    rstd(t * 3 + 2, st1[:, 4:5], st1[:, 0:1], KVR, 1e-6)
                    link(v.tensor_scalar(ckn, bank[0][:, 0:KVR], st1[:, 4:5], None, ALU.mult))
                    rotate(link, bank[0][:, KVR:KVR + ROPE].rearrange("p (g a f) -> p g a f", g=1, a=2),
                           kpe.rearrange("p (g a f) -> p g a f", g=1, a=2), 1, FM, 0).then_inc(ev["ckn"], 1)
                    v.wait_ge(ev["ssQ"], now(t))
                    rstd(t * 3 + 3, st1[:, 5:6], st1[:, 1:2], QR, 1e-6)
                    v.tensor_scalar(cqn, bank[1][:, 0:QR], st1[:, 5:6], None, ALU.mult).then_inc(ev["cqn"], 1)
                    v.wait_ge(s_x, t * 16 + 32)
                    norm_x(link, t * 3 + 4)
                    v.wait_ge(ev["pDV"], now(t))
                    v.tensor_scalar(v_d[:, bass.ds(t, 1), :].rearrange("p o n -> p (o n)"), bank[4][:, :], 1.0, None,
                                    ALU.mult).then_inc(ev["vd"], 1)
                    v.wait_ge(ev["eDQ"], now(t))
                    v.wait_ge(ev["eDK"], now(t))
                    z = dqk[:, :, 0:DROPE].rearrange("p g (a f) -> p g a f", a=2)
                    rotate(link, z, z, 16, FD, FM).then_inc(ev["drot"], 1)
                    v.wait_ge(ev["tK1"], prev(t))
                    v.wait_ge(ev["ckn"], now(t))
                    link(v.tensor_copy(kf[:, :, NOPE:QK], kpe.rearrange("p (o f) -> p o f", o=1).broadcast_to((P, HM, ROPE))))
                    for g in range(2):
                        v.wait_ge(ev[f"up{g}"], now(t))
                        kv = bank[2 + g][:, :].rearrange("p (h n) -> p h n", h=4)
                        link(v.tensor_copy(kf[:, 4 * g:4 * g + 4, 0:NOPE], kv[:, :, 0:NOPE]))
                        v.tensor_scalar(v_m[:, bass.ds(t, 1), g * 256:(g + 1) * 256].rearrange("p o (h n) -> p (o h) n", h=4),
                                        kv[:, :, NOPE:NOPE + DV_M], 1.0, None, ALU.mult).then_inc(ev[f"kv{g}"], 1)
                    v.wait_ge(ev["qup0"], now(t))
                    v.wait_ge(ev["qup1"], now(t))
                    z = qf[:, :, NOPE:QK].rearrange("p g (a f) -> p g a f", a=2)
                    rotate(link, z, z, HM, FM, 0).then_inc(ev["qfin"], 1)
                    v.wait_ge(ev["tDK"], now(t))
                    v.tensor_scalar(dkT[:, :, bass.ds(t * P, P)], bank[1][:, :].rearrange("p (h n) -> p h n", h=4), 1.0, None,
                                    ALU.mult).then_inc(ev["dkT"], 1)
                    for g in range(2):
                        v.wait_ge(ev[f"tK{g}"], now(t))
                        v.tensor_scalar(kT[0:QK, 4 * g:4 * g + 4, bass.ds(t * P, P)],
                                        bank[5 + g][0:QK, :].rearrange("p (h n) -> p h n", h=4), 1.0, None,
                                        ALU.mult).then_inc(ev[f"kT{g}"], 1)
                    assert link.done == PER, link.done

        at = work
        wout, at = carve(arena, at, KD, D)
        pbuf, at = carve(arena, at, 8 * 512)
        pT, at = carve(arena, at, 2, KD, P)
        qTb, at = carve(arena, at, 2, HM, P)
        dqTb, at = carve(arena, at, 2, HD, P)
        o_sb, at = carve(arena, at, 2, D)
        oT, at = carve(arena, at, KD, P)
        x2, at = carve(arena, at, D)
        x1, at = carve(arena, at, D)
        xh, at = carve(arena, at, D)
        h2T, at = carve(arena, at, KD, P)
        gt1b, at = carve(arena, at, D)
        wr, at = carve(arena, at, KD, NE)
        br, at = carve(arena, at, NE)
        nmax, at = carve(arena, at, 8)
        sums, at = carve(arena, at, 8)
        inv, at = carve(arena, at, 4)
        fac, at = carve(arena, at, 2, 2)
        st2, at = carve(arena, at, 16)
        lg, at = carve(arena, at, NE)
        v8, at = carve(arena, at, 8)
        i8, at = carve(arena, at, 8)
        i8f, at = carve(arena, at, TOPK)
        hot, at = carve(arena, at, TOPK, NE)
        chosen, at = carve(arena, at, NE)
        earlier, at = carve(arena, at, NE)
        slot_f, at = carve(arena, at, NE)
        pick, at = carve(arena, at, TOPK, NE)
        w4, at = carve(arena, at, 8)
        s4f, at = carve(arena, at, TOPK)
        slots, at = carve(arena, at, 2, TOPK)
        entry, at = carve(arena, at, 2, TOPK, 2)
        ptab, at = carve(arena, at, 4)
        pp, at = carve(arena, at, 10, NE)
        ps, at = carve(arena, at, 8)
        assert at <= 53100, at
        i8 = i8.bitcast(U32)
        slots = slots.bitcast(I32)
        entry_i, entry_f = entry.bitcast(I32), entry
        ptab = ptab.bitcast(I32)

        steps = attention_plan()
        PTB = (4, 5)
        (s_w2, s_x2, s_scores, s_max, s_exp, s_mixw, s_T, s_ev4, s_ev5, s_pv, s_oev, s_on, s_m7, s_m7ev, s_x1, s_xh,
         s_st, s_var2, s_rstd2, s_v2, s_top, s_ew, s_chosen, s_slot, s_cnt, s_ptab) = map(sem, (
             "s_w2 s_x2 s_scores s_max s_exp s_mixw s_T s_ev4 s_ev5 s_pv s_oev s_on s_m7 s_m7ev s_x1 s_xh "
             "s_st s_var2 s_rstd2 s_v2 s_top s_ew s_chosen s_slot s_cnt s_ptab").split())
        s_q = [sem("s_q0"), sem("s_q1")]
        s_scat = [sem("s_scat0"), sem("s_scat1")]
        group_of = {(kind, i, u): g for kind, i, u, g in steps}

        def scores_of(n, lo, hi):
            at_ = 512 * min(slots_of(n, 4))
            return scores[:, at_ + lo:at_ + hi]

        def exps_of(n, lo, hi):
            at_ = 512 * min(slots_of(n, 8))
            return pbuf[:, at_ + lo:at_ + hi]

        def evacuated(eng, g):
            eng.wait_ge((s_ev4, s_ev5)[g % 2], g // 2 + 1)

        with nc.Block() as block:
            @block.sync
            def _(sp):
                sp.dma_start(gt1b, gt1_scr).then_inc(s_w2, 16)
                sp.dma_start(wr, w_router[0].rearrange("(k p) n -> p k n", p=P)).then_inc(s_w2, 16)
                sp.dma_start(br, b_router.broadcast_to((P, NE))).then_inc(s_w2, 16)
                for i in range(NT):
                    if i >= 2:
                        sp.wait_ge(s_scores, item(i - 1, 0))
                    sp.dma_start(qTb[0:QK, i % 2].rearrange("p h n -> p (h n)"), q_scr[i, 0:QK]).then_inc(s_q[i % 2], 16)
                    sp.dma_start(dqTb[:, i % 2].rearrange("p h n -> p (h n)"), dq_scr[i]).then_inc(s_q[i % 2], 16)
                    if i == 0:
                        sp.dma_start(wout, w_out[0].rearrange("(k p) n -> p k n", p=P)).then_inc(s_w2, 16)
                        sp.dma_start(x2, x2d[0:P, :]).then_inc(s_x2, 16)
                    else:
                        sp.wait_ge(s_x1, i)
                        sp.dma_start(x_acc[(i - 1) * P:i * P, :], x1).then_inc(s_st, 16)
                        sp.dma_start(x2, x2d[i * P:(i + 1) * P, :]).then_inc(s_x2, 16)
                        sp.wait_ge(s_xh, i)
                        sp.dma_start(x_hat[(i - 1) * P:i * P, :], xh).then_inc(s_st, 16)
                sp.wait_ge(s_pv, NT * (HM + HD))
                for q in range(NEARLY):
                    sp.dma_start(w_slot[q], w_piece(0, q)).then_inc(s_wd[q], 16)
                sp.wait_ge(s_x1, NT)
                sp.dma_start(x_acc[(NT - 1) * P:S, :], x1).then_inc(s_st, 16)
                sp.wait_ge(s_xh, NT)
                sp.dma_start(x_hat[(NT - 1) * P:S, :], xh).then_inc(s_st, 16)
                sp.wait_ge(s_cnt, 1)
                sp.dma_start(passes, ptab).then_inc(s_ptab, 16)
                sp.wait_ge(s_st, 32 * NT)
                sp.wait_ge(s_ptab, 16)

            @block.gpsimd
            def _(pool):
                for i in range(NT):
                    for q, cut in enumerate((slice(10, 14), slice(15, 16))):
                        pool.wait_ge(s_var2, 2 * i + q + 1)
                        pool.tensor_tensor(st2[:, cut], st2[:, cut], mhalf[:, 0:cut.stop - cut.start], ALU.pow).then_inc(s_rstd2, 1)
                    pool.wait_ge(s_slot, i + 1)
                    for k in range(TOPK):
                        pool.indirect_dma_start(table, bass.IndirectOffsetOnAxis(ap=slots[:, i % 2, k:k + 1], axis=0),
                                                entry_i[:, i % 2, k, :], None).then_inc(s_scat[i % 2], 16)
                for par in range(2):
                    pool.wait_ge(s_scat[par], 16 * TOPK * NT // 2)

            @block.tensor
            def _(pe):
                oT_group = group_of["oT", 0, 0]

                def group_bank(g):
                    if g >= 2:
                        evacuated(pe, g - 2)
                    return bank[PTB[g % 2]]

                def turn(src, g0):
                    for g in range(2):
                        b = group_bank(g0 + g)
                        for k in range(4):
                            m = pe.transpose(b[:, k * P:(k + 1) * P], src[:, (4 * g + k) * P:(4 * g + k + 1) * P], ident)
                        m.then_inc(s_T, 1)

                def misc(n):
                    if n:
                        pe.wait_ge(s_m7ev, n)
                    return bank[7]

                for kind, i, u, g0 in steps:
                    kb = i + 1
                    if kind == "S":
                        n = u
                        _, u = unit_of(n)
                        if n % 16 == 0:
                            pe.wait_ge(s_q[i % 2], 32 * (i // 2 + 1))
                        if last_in_slots(n, 4) is not None:
                            pe.wait_ge(s_exp, last_in_slots(n, 4) + 1)
                        for w in range(0, kb * P, 512):
                            hi = min(w + 512, kb * P)
                            if u < HM:
                                m = pe.matmul(scores_of(n, w, hi), qTb[0:QK, i % 2, u, :], kT[0:QK, u, w:hi],
                                              start=True, stop=True)
                            else:
                                half = n - item(i, u)
                                rows_ = slice(half * DH, half * DH + DH)
                                m = pe.matmul(scores_of(n, w, hi), dqTb[rows_, i % 2, u - HM, :], dkT[rows_, u - HM, w:hi],
                                              start=True, stop=True)
                        m.then_inc(s_scores, 1)
                    elif kind == "T":
                        n = item(i, u)
                        if u < HM:
                            pe.wait_ge(s_exp, n + 1)
                        else:
                            pe.wait_ge(s_mixw, HD * i + u - HM + 1)
                        for g in range(0, kb, 4):
                            b = group_bank(g0 + g // 4)
                            for k in range(g, min(g + 4, kb)):
                                m = pe.transpose(b[:, (k - g) * P:(k - g + 1) * P], exps_of(n, k * P, (k + 1) * P), ident)
                            m.then_inc(s_T, 1)
                    elif kind == "PV":
                        U = (HM + HD) * i + u
                        gs = group_of["T", i, u]
                        for g in range(gs, gs + i // 4 + 1):
                            evacuated(pe, g)
                        if U:
                            pe.wait_ge(s_oev, U)
                        for k in range(kb):
                            if u < HM:
                                m = pe.matmul(bank[6][:, 0:DV_M], pT[:, U % 2, k, :],
                                              v_m[:, k, u * DV_M:(u + 1) * DV_M], start=(k == 0), stop=(k == kb - 1))
                            else:
                                m = pe.matmul(bank[6][:, 0:P], pT[:, U % 2, k, :],
                                              v_d[:, k, (u - HM) * P:(u - HM + 1) * P], start=(k == 0), stop=(k == kb - 1))
                        m.then_inc(s_pv, 1)
                    elif kind == "oT":
                        pe.wait_ge(s_on, i + 1)
                        turn(o_sb[:, i % 2, :], g0)
                    elif kind in ("mix0", "mix1"):
                        h = int(kind[-1])
                        if h == 0:
                            for g in range(2):
                                evacuated(pe, group_of["oT", i, 0] + g)
                            pe.wait_ge(s_w2, 64)
                        b = misc(4 * i + h)
                        for k in range(KD):
                            m = pe.matmul(b[:, :], oT[:, k, :], wout[:, k, h * 512:(h + 1) * 512], start=(k == 0), stop=(k == KD - 1))
                        m.then_inc(s_m7, 1)
                    elif kind == "xT":
                        pe.wait_ge(s_xh, i + 1)
                        turn(xh, g0)
                    elif kind == "router":
                        for g in range(2):
                            evacuated(pe, group_of["xT", i, 0] + g)
                        b = misc(4 * i + 2)
                        for k in range(KD):
                            m = pe.matmul(b[:, 0:NE], h2T[:, k, :], wr[:, k, :], start=(k == 0), stop=(k == KD - 1))
                        m.then_inc(s_m7, 1)
                    elif kind == "rank":
                        pe.wait_ge(s_chosen, i + 1)
                        b = misc(4 * i + 3)
                        m = pe.matmul(b[:, 0:NE], before, chosen, start=True, stop=(i == 0))
                        if i:
                            m = pe.matmul(b[:, 0:NE], ones, earlier, start=False, stop=True)
                        m.then_inc(s_m7, 1)
                pe.wait_ge(s_slot, NT)
                b = misc(4 * NT)
                pe.matmul(b[:, 0:NE], ones, earlier, start=True, stop=True).then_inc(s_m7, 1)

            @block.scalar
            def _(act):
                for kind, i, u, g0 in steps:
                    kw = (i + 1) * P
                    if kind == "S":
                        n = u
                        act.wait_ge(s_max, n + 1)
                        if last_in_slots(n, 8) is not None:
                            un = unit_of(last_in_slots(n, 8))
                            act.wait_ge(s_T, group_of["T", un[0], un[1]] + un[0] // 4 + 1)
                        act.activation(exps_of(n, 0, kw), scores_of(n, 0, kw), ACT.Exp, bias=nmax[:, n % 8:n % 8 + 1],
                                       scale=1.0, accum_out=sums[:, n % 8:n % 8 + 1]).then_inc(s_exp, 1)
                    elif kind == "T":
                        U = (HM + HD) * i + u
                        for g in range(g0, g0 + i // 4 + 1):
                            if g % 2 == 0:
                                continue
                            k0, k1 = 4 * (g - g0), min(4 * (g - g0) + 4, i + 1)
                            act.wait_ge(s_T, g + 1)
                            if U >= 2:
                                act.wait_ge(s_pv, U - 1)
                            act.activation(pT[:, U % 2, k0:k1, :].rearrange("p k n -> p (k n)"),
                                           bank[5][:, 0:(k1 - k0) * P], ACT.Copy).then_inc(s_ev5, 1)
                    elif kind in ("oT", "xT"):
                        g = g0 if g0 % 2 else g0 + 1
                        half = g - g0
                        act.wait_ge(s_T, g + 1)
                        for k in range(4 * half, 4 * half + 4):
                            src = bank[5][:, (k % 4) * P:(k % 4 + 1) * P]
                            if kind == "xT":
                                m = act.activation(h2T[:, k, :], src, ACT.Identity, bias=sh2[:, k:k + 1], scale=a2[:, k:k + 1])
                            else:
                                m = act.activation(oT[:, k, :], src, ACT.Copy, scale=gsub if half else 1.0)
                        m.then_inc(s_ev5, 1)
                    elif kind == "router":
                        act.wait_ge(s_top, i + 1)
                        act.activation(w4[:, 0:TOPK], v8[:, 0:TOPK], ACT.Exp, bias=w4[:, 5:6], scale=1.0,
                                       accum_out=w4[:, 4:5]).then_inc(s_ew, 1)

            @block.vector
            def _(v):
                link = Chain(v, s_v2, 0)
                link(v.memset(earlier, 0.0))

                def rstd(count, out, ss, n, eps):
                    v.tensor_scalar(out, ss, 1.0 / n, eps, ALU.mult, ALU.add).then_inc(s_var2, 1)
                    v.wait_ge(s_rstd2, count)

                def total(n):
                    return sums[:, n % 8:n % 8 + 1]

                for kind, i, u, g0 in steps:
                    kb = i + 1
                    kw = kb * P
                    if kind == "S":
                        n = u
                        v.wait_ge(s_scores, n + 1)
                        link(v.memset(scores_of(n, kw - CHUNK, kw)[0:CHUNK], MASKED))
                        if n >= 8:
                            v.wait_ge(s_exp, n - 7)
                        v.tensor_reduce(nmax[:, n % 8:n % 8 + 1], scores_of(n, 0, kw), AX_X, ALU.max,
                                        negate=True).then_inc(s_max, 1)
                    elif kind == "W":
                        U = (HM + HD) * i + u
                        n = item(i, u)
                        v.wait_ge(s_exp, n + 2)
                        fl, f = fac[:, U % 2, 0:1], fac[:, U % 2, 1:2]
                        link(v.reciprocal(fl, total(n + 1)))
                        link(v.scalar_tensor_tensor(f, fl, neg_lam, total(n), ALU.mult, ALU.mult))
                        v.scalar_tensor_tensor(exps_of(n, 0, kw), exps_of(n + 1, 0, kw), f, exps_of(n, 0, kw),
                                               ALU.mult, ALU.add).then_inc(s_mixw, 1)
                        link(v.reciprocal(inv[:, U % 4:U % 4 + 1], total(n)))
                    elif kind == "T":
                        U = (HM + HD) * i + u
                        n = item(i, u)
                        if u < HM:
                            v.wait_ge(s_exp, n + 1)
                            link(v.reciprocal(inv[:, U % 4:U % 4 + 1], total(n)))
                        for g in range(g0, g0 + i // 4 + 1):
                            if g % 2:
                                continue
                            k0, k1 = 4 * (g - g0), min(4 * (g - g0) + 4, kb)
                            v.wait_ge(s_T, g + 1)
                            if U >= 2:
                                v.wait_ge(s_pv, U - 1)
                            v.tensor_copy(pT[:, U % 2, k0:k1, :].rearrange("p k n -> p (k n)"),
                                          bank[4][:, 0:(k1 - k0) * P]).then_inc(s_ev4, 1)
                    elif kind == "PV":
                        U = (HM + HD) * i + u
                        v.wait_ge(s_pv, U + 1)
                        if u == 0 and i >= 2:
                            v.wait_ge(s_T, group_of["oT", i - 2, 0] + 2)
                        w = DV_M if u < HM else P
                        lo = u * DV_M if u < HM else HM * DV_M + (u - HM) * P
                        ins = v.tensor_scalar(o_sb[:, i % 2, lo:lo + w], bank[6][:, 0:w],
                                              inv[:, U % 4:U % 4 + 1], None, ALU.mult)
                        ins.then_inc(s_oev, 1)
                        if u == HM + HD - 1:
                            v.wait_ge(s_oev, U + 1)
                            od = o_sb[:, i % 2, HM * DV_M:D].rearrange("p (h n) -> p h n", h=HD)
                            sq = xh[:, 0:P]
                            if i:
                                v.wait_ge(s_st, 32 * i)
                            for h in range(HD):
                                link(v.tensor_tensor_reduce(sq, od[:, h, :], od[:, h, :], 1.0, 0.0, ALU.mult, ALU.add,
                                                            st2[:, 10 + h:11 + h]))
                            rstd(2 * i + 1, st2[:, 10:14], st2[:, 10:14], P, 1e-5)
                            v.tensor_tensor(od, od, st2[:, 10:14].rearrange("p (h o) -> p h o", o=1).broadcast_to((P, HD, P)),
                                            ALU.mult).then_inc(s_on, 1)
                    elif kind in ("oT", "xT"):
                        g = g0 + g0 % 2
                        half = g - g0
                        v.wait_ge(s_T, g + 1)
                        for k in range(4 * half, 4 * half + 4):
                            src = bank[4][:, (k % 4) * P:(k % 4 + 1) * P]
                            if kind == "xT":
                                m = v.tensor_scalar(h2T[:, k, :], src, a2[:, k:k + 1], sh2[:, k:k + 1], ALU.mult, ALU.add)
                            elif half:
                                m = v.tensor_scalar(oT[:, k, :], src, gsub, None, ALU.mult)
                            else:
                                m = v.tensor_copy(oT[:, k, :], src)
                        m.then_inc(s_ev4, 1)
                    elif kind in ("mix0", "mix1"):
                        h = int(kind[-1])
                        cut = slice(h * 512, (h + 1) * 512)
                        v.wait_ge(s_m7, 4 * i + h + 1)
                        if h == 0:
                            v.wait_ge(s_w2, 64)
                            v.wait_ge(s_x2, 16 * (i + 1))
                            if i:
                                v.wait_ge(s_st, 32 * i)
                        v.tensor_tensor(x1[:, cut], bank[7][:, :], gt1b[:, cut], ALU.mult).then_inc(s_m7ev, 1)
                        v.wait_ge(s_m7ev, 4 * i + h + 1)
                        ins = v.tensor_tensor(x1[:, cut], x1[:, cut], x2[:, cut], ALU.add)
                        if h == 0:
                            link(ins)
                        else:
                            ins.then_inc(s_x1, 1)
                            v.wait_ge(s_x1, i + 1)
                            link(v.tensor_tensor_reduce(xh, x1, x1, 1.0, 0.0, ALU.mult, ALU.add, st2[:, 14:15]))
                            rstd(2 * i + 2, st2[:, 15:16], st2[:, 14:15], D, 1e-6)
                            v.tensor_scalar(xh, x1, st2[:, 15:16], None, ALU.mult).then_inc(s_xh, 1)
                    elif kind == "router":
                        v.wait_ge(s_m7, 4 * i + 3)
                        v.tensor_tensor(lg, bank[7][:, 0:NE], br, ALU.add).then_inc(s_m7ev, 1)
                        v.wait_ge(s_m7ev, 4 * i + 3)
                        link(v.max(v8, lg))
                        link(v.max_index(i8, v8, lg))
                        v.tensor_scalar(w4[:, 5:6], v8[:, 0:1], -1.0, None, ALU.mult).then_inc(s_top, 1)
                        link(v.tensor_copy(i8f, i8[:, 0:TOPK]))
                        for k in range(TOPK):
                            link(v.tensor_scalar(hot[:, k, :], iota_e, i8f[:, k:k + 1], None, ALU.is_equal))
                        if i >= 2:
                            v.wait_ge(s_scat[i % 2], 16 * TOPK * (i // 2))
                        link(v.tensor_tensor(pick[:, 0, :], hot[:, 0, :], hot[:, 1, :], ALU.add))
                        link(v.tensor_tensor(pick[:, 1, :], hot[:, 2, :], hot[:, 3, :], ALU.add))
                        v.tensor_tensor(chosen, pick[:, 0, :], pick[:, 1, :], ALU.add).then_inc(s_chosen, 1)
                        v.wait_ge(s_ew, i + 1)
                        link(v.reciprocal(w4[:, 6:7], w4[:, 4:5]))
                        link(v.tensor_scalar(entry_f[:, i % 2, :, 1], w4[:, 0:TOPK], w4[:, 6:7], None, ALU.mult))
                        link(v.tensor_scalar(s4f, iota_p.broadcast_to((P, TOPK)), float(i * P), None, ALU.add))
                        link(v.tensor_copy(entry_i[:, i % 2, :, 0], s4f))
                    elif kind == "rank":
                        v.wait_ge(s_m7, 4 * i + 4)
                        v.scalar_tensor_tensor(slot_f, iota_e, float(S), bank[7][:, 0:NE], ALU.mult, ALU.add).then_inc(s_m7ev, 1)
                        v.wait_ge(s_m7ev, 4 * i + 4)
                        v.wait_ge(s_chosen, i + 1)
                        link(v.tensor_tensor(earlier, earlier, chosen, ALU.add))
                        for k in range(TOPK):
                            link(v.tensor_tensor_reduce(pick[:, k, :], hot[:, k, :], slot_f, 1.0, 0.0, ALU.mult, ALU.add,
                                                        s4f[:, k:k + 1]))
                        v.tensor_copy(slots[:, i % 2, :], s4f).then_inc(s_slot, 1)
                cnt, npass, ends, starts, ge, hot_e, tmp = (pp[:, q, :] for q in range(7))
                v.wait_ge(s_m7, 4 * NT + 1)
                link(v.tensor_copy(cnt, bank[7][:, 0:NE]))
                link(v.tensor_scalar(npass, cnt, float(CAP), 1.0, ALU.is_gt, ALU.add))
                for q in range(2, S // CAP):
                    link(v.scalar_tensor_tensor(npass, cnt, float(q * CAP), npass, ALU.is_gt, ALU.add))
                link(v.tensor_tensor_scan(ends, ones[:, 0:NE], npass, 0.0, ALU.mult, ALU.add))
                link(v.tensor_tensor(starts, ends, npass, ALU.subtract))
                link(v.tensor_scalar(ge, starts, iota_p, None, ALU.is_le))
                link(v.reduce_sum(ps[:, 0:1], ge, AX_X))
                link(v.tensor_scalar(ps[:, 0:1], ps[:, 0:1], -1.0, None, ALU.add))
                link(v.tensor_scalar(hot_e, iota_e, ps[:, 0:1], None, ALU.is_equal))
                link(v.tensor_tensor_reduce(tmp, hot_e, starts, 1.0, 0.0, ALU.mult, ALU.add, ps[:, 1:2]))
                link(v.tensor_tensor_reduce(tmp, hot_e, cnt, 1.0, 0.0, ALU.mult, ALU.add, ps[:, 2:3]))
                link(v.tensor_tensor(ps[:, 3:4], iota_p, ps[:, 1:2], ALU.subtract))
                link(v.tensor_scalar(ps[:, 3:4], ps[:, 3:4], float(S // CAP - 1), float(CAP), ALU.min, ALU.mult))
                link(v.tensor_tensor(ps[:, 4:5], ps[:, 2:3], ps[:, 3:4], ALU.subtract))
                link(v.scalar_tensor_tensor(ps[:, 5:6], ps[:, 0:1], float(S), ps[:, 3:4], ALU.mult, ALU.add))
                link(v.tensor_copy(ptab[:, 0:1], ps[:, 0:1]))
                link(v.tensor_copy(ptab[:, 1:2], ps[:, 5:6]))
                link(v.tensor_copy(ptab[:, 2:3], ps[:, 4:5]))
                v.tensor_copy(ptab[:, 3:4], ends[:, NE - 1:NE]).then_inc(s_cnt, 1)

        at = base
        at += NW * KD * 256
        xg, at = carve(arena, at, 2, D)
        xT, at = carve(arena, at, KD, CAP)
        actT, at = carve(arena, at, KD, CAP)
        yT, at = carve(arena, at, KD, CAP)
        y, at = carve(arena, at, 2, D)
        bias_e, at = carve(arena, at, 3, NE * KD)
        bc, at = carve(arena, at, 3, KD)
        gate_t, at = carve(arena, at, CAP)
        up_t, at = carve(arena, at, CAP)
        sig_t, at = carve(arena, at, CAP)
        idx_g, at = carve(arena, at, 2, 2)
        idx_s, at = carve(arena, at, 2, 2)
        prow, at = carve(arena, at, NPASS_ROWS, 4)
        assert at <= 53100, at
        prow = prow.bitcast(I32)
        s_prow = sem("s_prow")
        idx_g, idx_s, wgt = idx_g.bitcast(I32), idx_s.bitcast(I32), idx_s

        (s_gx, s_xte, s_gu, s_gev, s_gate, s_sigd, s_actd, s_yt, s_yev, s_ytr, s_ye, s_yfree,
         s_is, s_ig, s_sc, s_be, s_tr, s_v3, s_go) = map(sem, (
             "s_gx s_xte s_gu s_gev s_gate s_sigd s_actd s_yt s_yev s_ytr s_ye s_yfree "
             "s_is s_ig s_sc s_be s_tr s_v3 s_go").split())
        def pass_value(eng, i, col, hi):
            at_ = prow[0:1, bass.ds(i, 1), col:col + 1] if not isinstance(i, int) else prow[0:1, i:i + 1, col:col + 1]
            return eng.value_load(at_.rearrange("a b c -> a (b c)"), min_val=0, max_val=hi)

        def n_passes(eng):
            eng.wait_ge(s_prow, 16)
            return eng.value_load(prow[0:1, 0, 3:4], min_val=NE, max_val=MAXPASS)

        def by_size(eng, tokens, body, sizes=SIZES):
            if len(sizes) == 1:
                body(sizes[0])
                return
            low, high = sizes[:(len(sizes) + 1) // 2], sizes[(len(sizes) + 1) // 2:]
            with eng.If(tokens <= low[-1]):
                by_size(eng, tokens, body, low)
            with eng.Else():
                by_size(eng, tokens, body, high)

        with nc.Block() as block:
            @block.sync
            def _(sp):
                for q in range(NEARLY, NW):
                    sp.dma_start(w_slot[q], w_piece(0, q)).then_inc(s_wd[q], 16)
                sp.dma_start(prow[0:1].rearrange("o a b -> o (a b)"), passes.rearrange("a b -> (a b)").rearrange("(o n) -> o n", o=1)).then_inc(s_prow, 16)
                sp.dma_start(bias_e.rearrange("p a n -> p (a n)"), bias_scr).then_inc(s_be, 16)
                T = n_passes(sp)
                with sp.Fori(1, T) as i:
                    e = pass_value(sp, i, 0, NE - 1)
                    for q in range(NW):
                        if q < NJ:
                            sp.wait_ge(s_gu, i * 8 + q + 1)
                        else:
                            sp.wait_ge(s_yt, i * 8 + 2 * (q - NJ) + 2)
                        sp.dma_start(w_slot[q], w_piece(e, q)).then_inc(s_wd[q], 16)

            @block.gpsimd
            def _(pool):
                def rows_of(i, dst, sem_):
                    r0 = pass_value(pool, i, 1, NE * S - CAP)
                    pool.dma_start(dst, table[bass.ds(r0, CAP), :].rearrange("(b p) w -> p b w", p=P)).then_inc(sem_, 16)

                def gather():
                    for b in range(2):
                        pool.indirect_dma_start(xg[:, b, :], None, x_hat,
                                                bass.IndirectOffsetOnAxis(ap=idx_g[:, b, 0:1], axis=0)).then_inc(s_gx, 16)

                pool.sem_inc(s_gu, 8)
                pool.sem_inc(s_yt, 8)
                pool.sem_inc(s_gev, 8)
                pool.sem_inc(s_yev, 8)
                pool.sem_inc(s_ye, 4)
                pool.memset(y[:, 1, :], 0.0).then_inc(s_yfree, 1)
                pool.dma_start(idx_g, table[0:CAP, :].rearrange("(b p) w -> p b w", p=P)).then_inc(s_ig, 16)
                T = n_passes(pool)
                pool.wait_ge(s_ig, 16)
                gather()
                with pool.Fori(0, T) as i:
                    rows_of(i, idx_s, s_is)
                    pool.wait_ge(s_gx, i * 32 + 32)
                    pool.sem_inc(s_go, 1)
                    rows_of(i + 1, idx_g, s_ig)
                    pool.wait_ge(s_ig, i * 16 + 32)
                    pool.wait_ge(s_tr, i * 4 + 4)
                    pool.sem_inc(s_go, 1)
                    gather()
                    pool.wait_ge(s_is, i * 16 + 16)
                    pool.wait_ge(s_ye, i * 4 + 8)
                    pool.sem_inc(s_go, 1)
                    for b in range(2):
                        pool.indirect_dma_start(x_acc, bass.IndirectOffsetOnAxis(ap=idx_s[:, b, 0:1], axis=0),
                                                y[:, b, :], None, compute_op=ALU.add).then_inc(s_sc, 16)
                    pool.wait_ge(s_sc, i * 32 + 32)
                    pool.sem_inc(s_yfree, 1)
                pool.wait_ge(s_gx, T * 32 + 32)

            @block.tensor
            def _(pe):
                def load_tokens(reg, i):
                    pe.reg_load(reg, prow[0:1, bass.ds(i, 1) if not isinstance(i, int) else slice(i, i + 1), 2:3]
                                .rearrange("a b c -> a (b c)"))

                def turn_x(g):
                    for kk in range(2):
                        for b in range(2):
                            m = pe.transpose(bank[g][:, (2 * kk + b) * P:(2 * kk + b + 1) * P],
                                             xg[:, b, (2 * g + kk) * P:(2 * g + kk + 1) * P], ident)
                    m.then_inc(s_tr, 1)

                T = n_passes(pe)
                ahead = pe.alloc_register()
                load_tokens(ahead, 0)
                pe.wait_ge(s_gx, 32)
                for g in range(4):
                    turn_x(g)
                with pe.Fori(0, T) as i:
                    tokens = pe.snap(ahead, min_val=0, max_val=S)

                    def body(N):
                        pe.wait_ge(s_xte, i * 4 + 4)
                        for j in range(KD):
                            pe.wait_ge(s_wd[j], i * 16 + 16)
                            if j >= 4:
                                pe.wait_ge(s_gev, i * 8 + j + 5)
                            for half in range(2):
                                for k in range(KD):
                                    m = pe.matmul(bank[j % 4][:, half * 256:half * 256 + N], w_slot[j][:, k, half::2],
                                                  xT[:, k, 0:N], start=(k == 0), stop=(k == KD - 1))
                            m.then_inc(s_gu, 1)
                        pe.wait_ge(s_gx, i * 32 + 64)
                        for g in range(3):
                            pe.wait_ge(s_gev, i * 8 + g + 13)
                            turn_x(g)
                        for m_ in range(KD):
                            q = NJ + m_ // 2
                            pe.wait_ge(s_wd[q], i * 16 + 16)
                            pe.wait_ge(s_yev, i * 8 + m_ + 7)
                            for k in range(KD):
                                if m_ == 0:
                                    pe.wait_ge(s_actd, i * 8 + k + 1)
                                m = pe.matmul(bank[4 + m_ % 2][:, 0:N], w_slot[q][:, k, (m_ % 2) * P:(m_ % 2 + 1) * P],
                                              actT[:, k, 0:N], start=(k == 0), stop=(k == KD - 1))
                            m.then_inc(s_yt, 1)
                            if m_ == 0:
                                pe.wait_ge(s_gev, i * 8 + 16)
                                turn_x(3)
                            if m_ == 5:
                                turn_y(i, 0, N)
                        load_tokens(ahead, i + 1)
                        turn_y(i, 1, N)

                    def turn_y(i, half, N):
                        pe.wait_ge(s_yev, i * 8 + 8 + 4 * half + 4)
                        nb = 2 if N > P else 1
                        for b in range(nb):
                            g = 2 * half + b
                            pe.wait_ge(s_ye, i * 4 + g + 3)
                            for k in range(4):
                                m = pe.transpose(bank[6 + g % 2][:, k * P:(k + 1) * P],
                                                 yT[:, 4 * half + k, b * P:(b + 1) * P], ident)
                            m.then_inc(s_ytr, 2 // nb)

                    by_size(pe, tokens, body)

            @block.scalar
            def _(act):
                def take_x(i, first):
                    for g in range(4):
                        act.wait_ge(s_tr, g + 1 if first else i * 4 + g + 1)
                        for kk in range(2):
                            k = 2 * g + kk
                            m = act.activation(xT[:, k, :], bank[g][:, kk * CAP:(kk + 1) * CAP], ACT.Identity,
                                               bias=sh2[:, k:k + 1], scale=a2[:, k:k + 1])
                        m.then_inc(s_xte, 1)

                take_x(0, True)
                T = n_passes(act)
                with act.Fori(0, T) as i:
                    tokens = pass_value(act, i, 2, S)

                    def body(N):
                        for j in range(KD):
                            act.wait_ge(s_gate, i * 8 + j + 1)
                            act.activation(sig_t[:, 0:N], gate_t[:, 0:N], ACT.Sigmoid, scale=SWISH).then_inc(s_sigd, 1)

                        take_x(i + 1, False)
                        act.wait_ge(s_is, i * 16 + 16)
                        act.wait_ge(s_yfree, i + 1)
                        nb = 2 if N > P else 1
                        for half in range(2):
                            for b in range(nb):
                                act.wait_ge(s_ytr, i * 4 + 2 * half + b + 1)
                                act.activation(y[:, b, half * 512:(half + 1) * 512], bank[6 + b][:, :], ACT.Copy,
                                               scale=wgt[:, b, 1:2]).then_inc(s_ye, 2 // nb)

                    by_size(act, tokens, body)

            @block.vector
            def _(v):
                PER = 1 + KD
                v.memset(yT, 0.0)
                v.wait_ge(s_be, 16)
                T = n_passes(v)
                with v.Fori(0, T) as i:
                    e = pass_value(v, i, 0, NE - 1)
                    tokens = pass_value(v, i, 2, S)
                    link = Chain(v, s_v3, i * PER)
                    v.wait_ge(s_yev, i * 8 + 8)
                    v.tensor_scalar(bc, bias_e[:, :, bass.ds(e * KD, KD)], 1.0, None, ALU.mult).then_inc(s_v3, 1)

                    def body(N):
                        link.done = 1
                        v.wait_ge(s_v3, i * PER + 1)
                        for j in range(KD):
                            v.wait_ge(s_gu, i * 8 + j + 9)
                            b = bank[j % 4]
                            v.tensor_scalar(gate_t[:, 0:N], b[:, 0:N], bc[:, 0, j:j + 1], LIMIT, ALU.add, ALU.min).then_inc(s_gate, 1)
                            v.tensor_scalar(up_t[:, 0:N], b[:, 256:256 + N], bc[:, 1, j:j + 1], 1.0 + LIMIT,
                                            ALU.add, ALU.min).then_inc(s_gev, 1)
                            v.wait_ge(s_gate, i * 8 + j + 1)
                            v.wait_ge(s_gev, i * 8 + j + 9)
                            link(v.scalar_tensor_tensor(up_t[:, 0:N], up_t[:, 0:N], 1.0 - LIMIT, gate_t[:, 0:N], ALU.max, ALU.mult))
                            v.wait_ge(s_sigd, i * 8 + j + 1)
                            v.tensor_tensor(actT[:, j, 0:N], up_t[:, 0:N], sig_t[:, 0:N], ALU.mult).then_inc(s_actd, 1)
                            v.wait_ge(s_actd, i * 8 + j + 1)
                        for m_ in range(KD):
                            v.wait_ge(s_yt, i * 8 + m_ + 9)
                            v.tensor_scalar(yT[:, m_, 0:N], bank[4 + m_ % 2][:, 0:N], bc[:, 2, m_:m_ + 1], gt2[:, m_:m_ + 1],
                                            ALU.add, ALU.mult).then_inc(s_yev, 1)
                        assert link.done == 1 + KD

                    by_size(v, tokens, body)

        at = base
        gfb, at = carve(arena, at, D)
        fin, at = carve(arena, at, NT, D)
        sq, at = carve(arena, at, D)
        fs, at = carve(arena, at, 2, NT)
        s_fin = [sem(f"s_fin{i}") for i in range(NT)]
        s_var4, s_rstd4 = sem("s_var4"), sem("s_rstd4")
        s_gf, s_v4, s_res, s_out = map(sem, ("s_gf", "s_v4", "s_res", "s_out"))

        with nc.Block() as block:
            @block.sync
            def _(sp):
                sp.dma_start(gfb, g_final.rearrange("(o d) -> o d", o=1).broadcast_to((P, D))).then_inc(s_gf, 16)
                for i in range(NT):
                    sp.dma_start(fin[:, i, :], x_acc[i * P:(i + 1) * P, :]).then_inc(s_fin[i], 16)
                for i in range(NT):
                    sp.wait_ge(s_res, i + 1)
                    sp.dma_start(out2d[i * P:(i + 1) * P, :], fin[:, i, :]).then_inc(s_out, 16)
                sp.wait_ge(s_out, 16 * NT)

            @block.gpsimd
            def _(pool):
                for i in range(NT):
                    pool.wait_ge(s_var4, i + 1)
                    pool.tensor_tensor(fs[:, 1, i:i + 1], fs[:, 1, i:i + 1], mhalf[:, 0:1], ALU.pow).then_inc(s_rstd4, 1)

            @block.vector
            def _(v):
                link = Chain(v, s_v4, 0)
                v.wait_ge(s_gf, 16)
                for i in range(NT):
                    v.wait_ge(s_fin[i], 16)
                    link(v.tensor_tensor_reduce(sq, fin[:, i, :], fin[:, i, :], 1.0, 0.0, ALU.mult, ALU.add, fs[:, 0, i:i + 1]))
                    v.tensor_scalar(fs[:, 1, i:i + 1], fs[:, 0, i:i + 1], 1.0 / D, 1e-6, ALU.mult, ALU.add).then_inc(s_var4, 1)
                    v.wait_ge(s_rstd4, i + 1)
                    v.scalar_tensor_tensor(fin[:, i, :], fin[:, i, :], fs[:, 1, i:i + 1], gfb, ALU.mult, ALU.mult).then_inc(s_res, 1)


_INS = ["x", "c", "positions", "w_ada", "b_ada", "g_norm1", "w_in", "g_q_norm", "w_uq", "g_kv_norm", "w_ukv",
        "lambda_q1", "lambda_k1", "lambda_q2", "lambda_k2", "g_subln", "w_out", "g_norm2", "w_router", "b_router",
        "w_gate_up", "b_gate_up", "w_down", "b_down", "g_final"]
_OUTS = [((1, S, D), "float32")]


def kernel(**inputs):
    import numpy as _np
    import concourse.bacc as _bacc
    from concourse import mybir as _mybir
    from concourse.bass_utils import run_bass_kernel_spmd as _run

    nc = _bacc.Bacc("TRN2", target_bir_lowering=False, num_devices=1)
    arrays, args = {}, []
    for name in _INS:
        a = _np.ascontiguousarray(inputs[name])
        arrays[f"in_{name}_dram"] = a
        args.append(nc.dram_tensor(f"in_{name}_dram", a.shape, _mybir.dt.from_np(a.dtype), kind="ExternalInput").ap())
    for i, (shape, dtype) in enumerate(_OUTS):
        dt = _mybir.dt.from_np(_np.dtype(dtype))
        args.append(nc.dram_tensor(f"out_{i}_dram", shape, dt, kind="ExternalOutput").ap())
    hybrid_block(nc, *args)
    r = _run(nc, [arrays], core_ids=[0])
    return r.results[0]["out_0_dram"]
```

```python
from contextlib import ExitStack

import numpy as np
import concourse.bass as bass
from concourse import mybir

F32 = mybir.dt.float32
I32 = mybir.dt.int32
U32 = mybir.dt.uint32
ALU = mybir.AluOpType
ACT = mybir.ActivationFunctionType
AX_X = mybir.AxisListType.X

P = 128
D = 1024
KD = D // P
S = 1024
NT = S // P
HM, NOPE, ROPE, DV_M = 8, 64, 32, 64
QK = NOPE + ROPE
QR, KVR = 384, 256
KQ, KKV = QR // P, KVR // P
HD, DH = 4, 64
DROPE = DH // 4
FM, FD = ROPE // 2, DROPE // 2
THETA = 500000.0
CHUNK = 64
NCOL = QR + KVR + ROPE + 3 * HD * 2 * DH
C_DQ = QR + KVR + ROPE
NE, TOPK = 32, 4
LIMIT, SWISH = 7.0, 1.702
LAMBDA_INIT = 0.8 - 0.6
CAP = 256
SIZES = (*range(P, 176, 8), 176, CAP)
MAXPASS = NE + S * TOPK // CAP
NPASS_ROWS = 128
DUMMY = S
NROW = S + CAP
SCALE_M = float(QK) ** -0.5
SCALE_D = float(DH) ** -0.5
WIDE = 512 // P
ARENA = 53100
MASKED = -1.0e30
MAGIC = 12582912.0
TWO_PI = 2 * np.pi
PI_1 = 6.28125
PI_2 = float(np.float32(round((TWO_PI - PI_1) * 2 ** 21) / 2 ** 21))
PI_3 = float(TWO_PI - PI_1 - PI_2)
PI_IN = 3.1415925

R_C, R_BADA, R_G1, R_G2, R_GQ, R_GKV, R_SUB = 0, 8, 56, 64, 72, 75, 77
NR = 78


def carve(arena, at, *shape):
    n = int(np.prod(shape))
    view = arena[:, at:at + n]
    if len(shape) == 2:
        view = view.rearrange("p (a b) -> p a b", a=shape[0])
    elif len(shape) == 3:
        view = view.rearrange("p (a b c) -> p a b c", a=shape[0], b=shape[1])
    return view, at + n


class Chain:

    def __init__(self, eng, sem, base):
        self.eng, self.sem, self.base, self.done = eng, sem, base, 0

    def __call__(self, ins):
        self.done += 1
        ins.then_inc(self.sem, 1)
        self.eng.wait_ge(self.sem, self.base + self.done)


def attention_plan():
    units = [(i, u) for i in range(NT) for u in range(HM + HD)]
    tail = {0: "sq", 1: "headnorm", 2: "oT", 3: "mix0", 4: "mix1", 6: "norm", 7: "xT", 8: "router", 9: "rank",
            10: "slots"}
    scored = 0
    steps, group = [], 0

    def put(kind, i, u):
        nonlocal group
        steps.append((kind, i, u, group))
        if kind == "T":
            group += i // 4 + 1
        elif kind in ("oT", "xT"):
            group += 2

    for n, (i, u) in enumerate(units):
        last = item(i, u) + (0 if u < HM else 1)
        while scored <= last:
            put("S", scored // 16, scored)
            scored += 1
        if u >= HM:
            put("W", i, u)
        while scored < item(NT, 0) and scored <= last + (3 if scored // 16 < WIDE else 2):
            put("S", scored // 16, scored)
            scored += 1
        put("T", i, u)
        if n:
            put("PV", *units[n - 1])
        if i and u in tail:
            put(tail[u], i - 1, 0)
    put("PV", *units[-1])
    for u in sorted(tail):
        put(tail[u], NT - 1, 0)
    return steps


def item(i, u):
    return 16 * i + (u if u < HM else HM + 2 * (u - HM))


def slots_of(n, narrow):
    return {n % narrow} if n // 16 < WIDE else {2 * (n % (narrow // 2)), 2 * (n % (narrow // 2)) + 1}


def last_in_slots(n, narrow):
    return next((m for m in range(n - 1, -1, -1) if slots_of(m, narrow) & slots_of(n, narrow)), None)


def unit_of(n):
    i, r = divmod(n, 16)
    return i, (r if r < HM else HM + (r - HM) // 2)


def hybrid_block(nc, x, c, positions, w_ada, b_ada, g_norm1, w_in, g_q_norm, w_uq, g_kv_norm, w_ukv,
                 lambda_q1, lambda_k1, lambda_q2, lambda_k2, g_subln, w_out, g_norm2,
                 w_router, b_router, w_gate_up, b_gate_up, w_down, b_down, g_final, out):
    x2d = x.rearrange("b s d -> (b s) d")
    out2d = out.rearrange("b s d -> (b s) d")
    w_ada_v = w_ada[0].rearrange("(k p) n -> p k n", p=P)
    w_in_v = w_in[0].rearrange("(k p) n -> p k n", p=P)
    w_gu_v = w_gate_up.rearrange("l e (k p) n -> p (l e) k n", p=P)
    w_dn_v = w_down.rearrange("l e (k p) n -> p (l e) k n", p=P)

    q_scr = nc.dram_tensor("q_scr", (NT, P, HM * P), F32).ap()
    dq_scr = nc.dram_tensor("dq_scr", (NT, P, HD * P), F32).ap()
    x_hat = nc.dram_tensor("x_hat", (NROW, D), F32).ap()
    x_acc = nc.dram_tensor("x_acc", (NROW, D), F32).ap()
    table = nc.dram_tensor("table", (NE * S, 2), I32).ap()
    bias_scr = nc.dram_tensor("bias_scr", (P, 3 * NE * KD), F32).ap()
    passes = nc.dram_tensor("passes", (NPASS_ROWS, 4), I32).ap()

    with ExitStack() as ctx:
        def sem(name):
            return ctx.enter_context(nc.semaphore(name))

        arena = ctx.enter_context(nc.sbuf_tensor("arena", [P, ARENA], F32))
        scores = ctx.enter_context(nc.psum_tensor("scores", [P, 4 * 512], F32))
        bank = [scores[:, b * 512:(b + 1) * 512] for b in range(4)]
        bank += [ctx.enter_context(nc.psum_tensor(f"bank{b}", [P, 512], F32)) for b in range(4, 8)]

        at = 0
        ident, at = carve(arena, at, P)
        ones, at = carve(arena, at, P)
        before, at = carve(arena, at, P)
        iota_e, at = carve(arena, at, NE)
        iota_p, at = carve(arena, at, 1)
        cols, at = carve(arena, at, 80)
        mods, at = carve(arena, at, 48)
        a1, at = carve(arena, at, KD)
        a2, at = carve(arena, at, KD)
        gsub, at = carve(arena, at, 1)
        neg_lam, at = carve(arena, at, 1)
        cos_t, at = carve(arena, at, NT, FM + FD)
        sin_t, at = carve(arena, at, NT, FM + FD)
        small, at = carve(arena, at, 32)
        mhalf, at = carve(arena, at, TOPK)
        base = at
        sh1, sh2, gt2 = mods[:, 0:8], mods[:, 24:32], mods[:, 40:48]

        kT, at = carve(arena, base, HM, S)
        v_m, at = carve(arena, at, NT, HM * DV_M)
        dkT, at = carve(arena, at, HD, S)
        v_d, at = carve(arena, at, NT, HD * 2 * DH)
        work = at
        NADA = 2 * D // 512
        ada = [carve(arena, base + q * KD * 512, KD, 512)[0] for q in range(NADA)]

        NJ, ND = 2 * D // 256, D // 256
        NW = NJ + ND
        SLOT = KD * 256
        in_kv = (work - base) // SLOT
        w_slot = [carve(arena, base + q * SLOT if q < in_kv else ARENA - (NW - q) * SLOT, KD, 256)[0] for q in range(NW)]
        kept_free = (NW - in_kv) * SLOT
        s_wd = [sem(f"s_wd{q}") for q in range(NW)]

        def w_piece(e, q):
            e = bass.ds(e, 1) if not isinstance(e, int) else slice(e, e + 1)
            src = (w_gu_v[:, e, :, q * 256:(q + 1) * 256] if q < NJ else
                   w_dn_v[:, e, :, (q - NJ) * 256:(q - NJ + 1) * 256])
            return src.rearrange("p o k n -> p (o k) n")

        win, at = carve(arena, work, KD, NCOL)
        wuq, at = carve(arena, at, KQ, HM * QK)
        wukv, at = carve(arena, at, KKV, HM * (NOPE + DV_M))
        p1 = at
        rows, at = carve(arena, p1, P)
        posi, at = carve(arena, at, P)
        posf, at = carve(arena, at, P)
        pos_c, at = carve(arena, at, NT)
        freq, at = carve(arena, at, FM + FD)
        ang, at = carve(arena, at, NT, FM + FD)
        turns, at = carve(arena, at, NT, FM + FD)
        wide, at = carve(arena, at, NT, FM + FD)
        lam4, at = carve(arena, at, 4, DH)
        brow, at = carve(arena, at, 2, 256)
        drow, at = carve(arena, at, 2, P)
        scb, at = carve(arena, at, KD, P)
        picked, at = carve(arena, at, 4, P)
        tinit, at = carve(arena, at, 256, 2)
        bias_e, at = carve(arena, at, 3, NE * KD)
        posi = posi.bitcast(I32)
        tinit = tinit.bitcast(I32)
        sig = small[:, 0:8]
        silu = small[:, 8:16]
        lam_s = small[:, 16:24]
        xt = carve(arena, ARENA - D, D)[0]
        assert at <= ARENA - D, at

        s_cst, s_rows, s_pos, s_lamld, s_brow = map(sem, ("s_cst", "s_rows", "s_pos", "s_lamld", "s_brow"))
        s_ada = [sem(f"s_ada{q}") for q in range(NADA)]
        s_turned, s_colf, s_func, s_silu, s_adau, s_bT, s_arg, s_v0, s_end0 = map(
            sem, ("s_turned", "s_colf", "s_func", "s_silu", "s_adau", "s_bT", "s_arg", "s_v0", "s_end0"))
        WIN_GROUPS = ((0, C_DQ), (C_DQ, 512), (C_DQ + 512, 512), (C_DQ + 1024, 512))
        s_win = [sem(f"s_win{g}") for g in range(len(WIN_GROUPS))]
        s_wu = sem("s_wu")
        s_keep, s_adae, s_x = sem("s_keep"), sem("s_adae"), sem("s_x")

        with nc.Block() as block:
            @block.sync
            def _(sp):
                for row, src, n in ((R_C, c[0], KD), (R_BADA, b_ada[0], 48), (R_G1, g_norm1[0], KD),
                                    (R_G2, g_norm2[0], KD), (R_GQ, g_q_norm[0], KQ), (R_GKV, g_kv_norm[0], KKV),
                                    (R_SUB, g_subln[0], 1)):
                    sp.dma_start(rows[row:row + n, :], src.rearrange("(r p) -> r p", p=P)).then_inc(s_rows, 16)
                sp.dma_start(ada[0], w_ada_v[:, :, 0:512]).then_inc(s_ada[0], 16)
                sp.dma_start(posi[0:NT, :], positions.rearrange("b (t p) -> (b t) p", p=P)).then_inc(s_pos, 16)
                for q, src in enumerate((lambda_q1, lambda_k1, lambda_q2, lambda_k2)):
                    sp.dma_start(lam4[:, q, :], src.broadcast_to((P, DH))).then_inc(s_lamld, 16)
                for h in range(2):
                    sp.dma_start(brow[:, h, :], b_gate_up[0, 16 * h:16 * h + 16].rearrange(
                        "e (j n) -> (e j) n", j=KD)).then_inc(s_brow, 16)
                    sp.dma_start(drow[:, h, :], b_down[0, 16 * h:16 * h + 16].rearrange(
                        "e (j n) -> (e j) n", j=KD)).then_inc(s_brow, 16)
                for q in range(1, NADA):
                    sp.dma_start(ada[q], w_ada_v[:, :, q * 512:(q + 1) * 512]).then_inc(s_ada[q], 16)
                sp.wait_ge(s_cst, 7)
                sp.dma_start(table.rearrange("(p j) w -> p j w", p=P), tinit).then_inc(s_end0, 16)
                sp.wait_ge(s_keep, 1)
                sp.dma_start(bias_scr, bias_e.rearrange("p a n -> p (a n)")).then_inc(s_end0, 16)
                sp.dma_start(xt, x2d[0:P, :]).then_inc(s_x, 16)
                for g, (lo, n) in enumerate(WIN_GROUPS):
                    sp.dma_start(win[:, :, lo:lo + n], w_in_v[:, :, lo:lo + n]).then_inc(s_win[g], 16)
                sp.dma_start(wukv, w_ukv[0].rearrange("(k p) n -> p k n", p=P)).then_inc(s_wu, 16)
                sp.dma_start(wuq, w_uq[0].rearrange("(k p) n -> p k n", p=P)).then_inc(s_wu, 16)
                sp.wait_ge(s_end0, 16 * 2)

            @block.gpsimd
            def _(pool):
                pool.memset(ident, 0.0).then_inc(s_cst, 1)
                pool.memset(ones, 1.0).then_inc(s_cst, 1)
                pool.wait_ge(s_cst, 2)
                pool.affine_select(out=ident, in_=ident, compare_op=ALU.not_equal, fill=1.0, base=0,
                                   pattern=[[-1, P]], channel_multiplier=1).then_inc(s_cst, 1)
                pool.affine_select(out=before, in_=ones, compare_op=ALU.is_gt, fill=0.0, base=0,
                                   pattern=[[1, P]], channel_multiplier=-1).then_inc(s_cst, 1)
                for f in range(FM + FD):
                    n, half = (f, FM) if f < FM else (f - FM, FD)
                    pool.memset(freq[:, f:f + 1], float(np.float32(THETA ** (-n / half))))
                pool.memset(mhalf, -0.5)
                pool.iota(iota_e, [[1, NE]], 0, 0, allow_small_or_imprecise_dtypes=True)
                pool.iota(iota_p, [[1, 1]], 0, 1, allow_small_or_imprecise_dtypes=True).then_inc(s_cst, 1)
                pool.iota(tinit[:, :, 0], [[1, CAP]], DUMMY, 0).then_inc(s_cst, 1)
                pool.memset(tinit[:, :, 1], 0).then_inc(s_cst, 1)

            @block.tensor
            def _(pe):
                pe.wait_ge(s_cst, 4)
                pe.wait_ge(s_rows, 16 * 7)
                pe.transpose(bank[0][:, 0:NR], rows[0:NR, :], ident[0:NR, 0:NR]).then_inc(s_turned, 1)
                pe.wait_ge(s_colf, 2)
                pe.transpose(bank[0][:, 128:128 + NT], posf[0:NT, :], ident[0:NT, 0:NT]).then_inc(s_turned, 1)
                pe.wait_ge(s_brow, 64)
                for h in range(2):
                    pe.transpose(bank[4][:, h * P:(h + 1) * P], brow[:, h, 0::2], ident)
                    pe.transpose(bank[4][:, (2 + h) * P:(3 + h) * P], brow[:, h, 1::2], ident)
                    pe.transpose(bank[5][:, h * P:(h + 1) * P], drow[:, h, :], ident).then_inc(s_bT, 1)
                pe.wait_ge(s_silu, 2)
                for q in range(NADA):
                    pe.wait_ge(s_ada[q], 16)
                    if q >= 2:
                        pe.wait_ge(s_adae, q - 1)
                    for k in range(KD):
                        m = pe.matmul(bank[2 + q % 2][:, :], scb[:, k, :], ada[q][:, k, :],
                                      start=(k == 0), stop=(k == KD - 1))
                    m.then_inc(s_adau, 1)

            @block.scalar
            def _(act):
                act.wait_ge(s_colf, 1)
                act.activation(sig, cols[:, R_C:R_C + KD], ACT.Sigmoid).then_inc(s_func, 1)
                act.wait_ge(s_arg, 2)
                act.activation(lam_s[:, 2:4], lam_s[:, 0:2], ACT.Exp).then_inc(s_func, 1)
                act.wait_ge(s_arg, 3)
                act.activation(sin_t, ang, ACT.Sin).then_inc(s_func, 1)
                act.activation(cos_t, wide, ACT.Sin).then_inc(s_func, 1)

            @block.vector
            def _(v):
                link = Chain(v, s_v0, 0)

                v.wait_ge(s_turned, 1)
                v.tensor_copy(cols[:, 0:NR], bank[0][:, 0:NR]).then_inc(s_colf, 1)
                v.wait_ge(s_pos, 16)
                v.tensor_copy(posf[0:NT, :], posi[0:NT, :]).then_inc(s_colf, 1)
                v.wait_ge(s_func, 1)
                v.wait_ge(s_colf, 1)
                v.tensor_tensor(silu, cols[:, R_C:R_C + KD], sig, ALU.mult).then_inc(s_silu, 1)
                v.wait_ge(s_silu, 1)
                v.tensor_copy(scb, silu.rearrange("p (k o) -> p k o", o=1).broadcast_to((P, KD, P))).then_inc(s_silu, 1)
                v.wait_ge(s_lamld, 64)
                for q in range(2):
                    v.tensor_tensor_reduce(lam4[:, 2 * q, :], lam4[:, 2 * q, :], lam4[:, 2 * q + 1, :], 1.0, 0.0,
                                           ALU.mult, ALU.add, lam_s[:, q:q + 1]).then_inc(s_arg, 1)
                v.wait_ge(s_func, 2)
                link(v.tensor_tensor(lam_s[:, 4:5], lam_s[:, 3:4], lam_s[:, 2:3], ALU.subtract))
                link(v.tensor_scalar(neg_lam, lam_s[:, 4:5], -LAMBDA_INIT, None, ALU.add))
                link(v.tensor_scalar(gsub, cols[:, R_SUB:R_SUB + 1], 1.0 - LAMBDA_INIT, None, ALU.mult))
                v.wait_ge(s_turned, 2)
                link(v.tensor_copy(pos_c, bank[0][:, 128:128 + NT]))
                v.wait_ge(s_cst, 5)
                link(v.tensor_tensor(ang, pos_c.rearrange("p (t o) -> p t o", o=1).broadcast_to((P, NT, FM + FD)),
                                     freq.rearrange("p (o f) -> p o f", o=1).broadcast_to((P, NT, FM + FD)), ALU.mult))
                link(v.tensor_scalar(turns, ang, 1.0 / TWO_PI, MAGIC, ALU.mult, ALU.add))
                link(v.tensor_scalar(turns, turns, MAGIC, None, ALU.subtract))
                for part in (PI_1, PI_2, PI_3):
                    link(v.scalar_tensor_tensor(ang, turns, -part, ang, ALU.mult, ALU.add))
                link(v.tensor_scalar(turns, ang, float(np.pi / 2), -TWO_PI, ALU.is_gt, ALU.mult))
                link(v.scalar_tensor_tensor(wide, ang, float(np.pi / 2), turns, ALU.add, ALU.add))
                link(v.tensor_scalar(wide, wide, PI_IN, -PI_IN, ALU.min, ALU.max))
                v.tensor_scalar(ang, ang, PI_IN, -PI_IN, ALU.min, ALU.max).then_inc(s_arg, 1)
                v.wait_ge(s_bT, 2)
                link(v.tensor_copy(bias_e[:, 0, :], bank[4][:, 0:256]))
                link(v.tensor_scalar(bias_e[:, 1, :], bank[4][:, 256:512], 1.0, None, ALU.add))
                v.tensor_copy(bias_e[:, 2, :], bank[5][:, 0:256]).then_inc(s_keep, 1)
                for q in range(NADA):
                    v.wait_ge(s_adau, q + 1)
                    v.tensor_tensor(picked, bank[2 + q % 2][:, :].rearrange("p (j n) -> p j n", j=4),
                                    ident.rearrange("p (o n) -> p o n", o=1).broadcast_to((P, 4, P)),
                                    ALU.mult).then_inc(s_adae, 1)
                    v.wait_ge(s_adae, q + 1)
                    link(v.reduce_sum(mods[:, 4 * q:4 * q + 4], picked, AX_X))
                link(v.tensor_tensor(mods[:, 0:16], mods[:, 0:16], cols[:, R_BADA:R_BADA + 16], ALU.add))
                v.scalar_tensor_tensor(a1, mods[:, 8:16], 1.0, cols[:, R_G1:R_G1 + 8], ALU.add, ALU.mult)

        at = p1
        hT, at = carve(arena, at, KD, P)
        cqn, at = carve(arena, at, QR)
        ckn, at = carve(arena, at, KVR)
        kpe, at = carve(arena, at, ROPE)
        cT, at = carve(arena, at, KQ + KKV, P)
        qf, at = carve(arena, at, HM, QK)
        kf, at = carve(arena, at, HM, QK)
        dqk_at = at
        dqk, at = carve(arena, at, 16, DH)
        qT_o, at = carve(arena, at, HM, P)
        dqT_o, at = carve(arena, at, HD, P)
        rot, at = carve(arena, at, 512)
        rot_a, rot_b = rot[:, 0:256], rot[:, 256:512]
        cs, at = carve(arena, at, 2, FM + FD)
        st1, at = carve(arena, at, 8)
        NPART = 4
        adac, at = carve(arena, at, KD, P)
        acc, at = carve(arena, at, NPART, P)
        assert NPART * NT * P == 4 * D
        assert at <= ARENA - D, at
        junk = carve(arena, dqk_at, QR)[0]

        names = ("pKV pQ pDQ pDK pDV tKV tQ up0 up1 uq0 uq1 tDQ tDK tK0 tK1 tN0 tN1 "
                 "ssKV ssQ eDQ eDK cTk cTq qup0 qup1 dqTo qTo "
                 "adaM adaR ckn cqn vd drot kv1 qfin dkT kT0 kT1 stored").split()
        ahead = "xn tX0 tX1 hT".split()
        ev = {n: sem("l_" + n) for n in names + ahead}
        s_adac, s_acc, s_qst, s_v1, s_var, s_rstd = map(sem, ("s_adac", "s_acc", "s_qst", "s_v1", "s_var", "s_rstd"))

        def now(t):
            return t + 2

        def prev(t):
            return t + 1

        with nc.Block() as block:
            @block.sync
            def _(sp):
                def load_part(n):
                    cut = bass.ds(n * P + 2 * D, P) if not isinstance(n, int) else slice(n * P + 2 * D, (n + 1) * P + 2 * D)
                    sp.dma_start(adac, w_ada_v[:, :, cut]).then_inc(s_adac, 16)

                load_part(0)
                with sp.Fori(0, NT) as t:
                    sp.wait_ge(ev["tX1"], prev(t))
                    sp.dma_start(xt, x2d.rearrange("(t p) d -> t p d", p=P)[bass.ds((t + 1) % NT, 1)]
                                 .rearrange("o p d -> p (o d)")).then_inc(s_x, 16)
                    for j in range(NPART):
                        sp.wait_ge(s_acc, t * NPART + j + 1)
                        load_part((t * NPART + j + 1) % (NPART * NT))
                    sp.wait_ge(ev["dqTo"], now(t))
                    sp.dma_start(dq_scr[bass.ds(t, 1)].rearrange("o p n -> p (o n)"),
                                 dqT_o.rearrange("p h n -> p (h n)")).then_inc(s_qst, 16)
                    sp.wait_ge(ev["qTo"], now(t))
                    sp.dma_start(q_scr[bass.ds(t, 1), 0:QK].rearrange("o p n -> p (o n)"),
                                 qT_o[0:QK].rearrange("p h n -> p (h n)")).then_inc(s_qst, 16)
                    sp.wait_ge(s_qst, t * 32 + 32)
                    sp.sem_inc(ev["stored"], 1)
                sp.wait_ge(s_x, 16 * (NT + 1))
                sp.wait_ge(s_adac, 16 * (NPART * NT + 1))

            @block.gpsimd
            def _(pool):
                for n in names:
                    pool.sem_inc(ev[n], 1)

                def root(count, col):
                    pool.wait_ge(s_var, count)
                    pool.tensor_tensor(st1[:, col:col + 1], st1[:, col:col + 1], mhalf[:, 0:1], ALU.pow).then_inc(s_rstd, 1)

                root(1, 3)
                with pool.Fori(0, NT) as t:
                    root(t * 3 + 2, 4)
                    root(t * 3 + 3, 5)
                    root(t * 3 + 4, 3)

            @block.tensor
            def _(pe):
                def turn_x():
                    for g in range(2):
                        for k in range(4 * g, 4 * g + 4):
                            m = pe.transpose(bank[5 + g][:, (k % 4) * P:(k % 4 + 1) * P], xt[:, k * P:(k + 1) * P], ident)
                        m.then_inc(ev[f"tX{g}"], 1)

                pe.wait_ge(ev["xn"], 1)
                turn_x()
                with pe.Fori(0, NT) as t:
                    pe.wait_ge(ev["hT"], prev(t))
                    for name, b, lo, n, free in (("pKV", 0, QR, KVR + ROPE, "dqTo"), ("pQ", 1, 0, QR, "dkT"),
                                                 ("pDQ", 2, C_DQ, 512, "qTo"), ("pDK", 3, C_DQ + 512, 512, "qTo"),
                                                 ("pDV", 4, C_DQ + 1024, 512, "qup0")):
                        pe.wait_ge(ev[free], prev(t))
                        pe.wait_ge(s_win[max(0, b - 1)], 16)
                        for k in range(KD):
                            m = pe.matmul(bank[b][:, 0:n], hT[:, k, :], win[:, k, lo:lo + n],
                                          start=(k == 0), stop=(k == KD - 1))
                        m.then_inc(ev[name], 1)
                    pe.wait_ge(ev["ckn"], now(t))
                    for k in range(KKV):
                        m = pe.transpose(bank[0][:, k * P:(k + 1) * P], ckn[:, k * P:(k + 1) * P], ident)
                    m.then_inc(ev["tKV"], 1)
                    pe.wait_ge(ev["cqn"], now(t))
                    for k in range(KQ):
                        m = pe.transpose(bank[1][:, k * P:(k + 1) * P], cqn[:, k * P:(k + 1) * P], ident)
                    m.then_inc(ev["tQ"], 1)
                    pe.wait_ge(ev["xn"], now(t))
                    pe.wait_ge(ev["kT0"], prev(t))
                    pe.wait_ge(ev["kT1"], prev(t))
                    turn_x()
                    pe.wait_ge(ev["cTk"], now(t))
                    pe.wait_ge(s_wu, 32)
                    for g, free in ((0, "eDQ"), (1, "eDK")):
                        pe.wait_ge(ev[free], now(t))
                        for k in range(KKV):
                            m = pe.matmul(bank[2 + g][:, :], cT[:, k, :], wukv[:, k, g * 512:(g + 1) * 512],
                                          start=(k == 0), stop=(k == KKV - 1))
                        m.then_inc(ev[f"up{g}"], 1)
                    pe.wait_ge(ev["cTq"], now(t))
                    pe.wait_ge(ev["vd"], now(t))
                    pe.wait_ge(ev["qup1"], prev(t))
                    pe.wait_ge(s_acc, t * NPART + NPART)
                    for j in range(NPART):
                        m = pe.matmul(bank[7][:, 4 * QK + j:4 * QK + j + 1], acc[:, j, :], ones[:, 0:1], start=True, stop=True)
                    m.then_inc(ev["adaM"], 1)
                    for g, b in ((0, 4), (1, 7)):
                        if g:
                            pe.wait_ge(ev["adaR"], now(t))
                        for k in range(KQ):
                            m = pe.matmul(bank[b][:, 0:4 * QK], cT[:, KKV + k, :], wuq[:, k, g * 4 * QK:(g + 1) * 4 * QK],
                                          start=(k == 0), stop=(k == KQ - 1))
                        m.then_inc(ev[f"uq{g}"], 1)
                    pe.wait_ge(ev["drot"], now(t))
                    for g, (name, free) in enumerate((("tDQ", "cTk"), ("tDK", "cTq"))):
                        pe.wait_ge(ev[free], now(t))
                        for h in range(HD):
                            m = pe.transpose(bank[g][:, h * P:(h + 1) * P],
                                             dqk[:, 8 * g + 2 * h:8 * g + 2 * h + 2, :].rearrange("p a d -> p (a d)"), ident)
                        m.then_inc(ev[name], 1)
                    pe.wait_ge(ev["kv1"], now(t))
                    pe.wait_ge(ev["hT"], now(t))
                    for g in range(2):
                        for h in range(4):
                            m = pe.transpose(bank[5 + g][0:QK, h * P:(h + 1) * P], kf[:, 4 * g + h, :], ident)
                        m.then_inc(ev[f"tK{g}"], 1)
                    pe.wait_ge(ev["qfin"], now(t))
                    for g in range(2):
                        for h in range(4):
                            m = pe.transpose(bank[2 + g][0:QK, h * P:(h + 1) * P], qf[:, 4 * g + h, :], ident)
                        m.then_inc(ev[f"tN{g}"], 1)

            @block.scalar
            def _(act):
                def modulate():
                    for k in range(KD):
                        m = act.activation(hT[:, k, :], bank[5 + k // 4][:, (k % 4) * P:(k % 4 + 1) * P], ACT.Identity,
                                           bias=sh1[:, k:k + 1], scale=a1[:, k:k + 1])
                    m.then_inc(ev["hT"], 1)

                act.wait_ge(ev["tX0"], 1)
                act.wait_ge(ev["tX1"], 1)
                modulate()
                with act.Fori(0, NT) as t:
                    act.wait_ge(ev["tDK"], prev(t))
                    act.wait_ge(ev["pKV"], now(t))
                    act.activation(junk[:, 0:KVR], bank[0][:, 0:KVR], ACT.Square, accum_out=st1[:, 0:1]).then_inc(ev["ssKV"], 1)
                    act.wait_ge(ev["pQ"], now(t))
                    act.wait_ge(ev["ssKV"], now(t))
                    act.activation(junk, bank[1][:, 0:QR], ACT.Square, accum_out=st1[:, 1:2]).then_inc(ev["ssQ"], 1)
                    act.wait_ge(ev["pDQ"], now(t))
                    act.wait_ge(ev["ssQ"], now(t))
                    act.activation(dqk[:, 0:8, :].rearrange("p a d -> p (a d)"), bank[2][:, :], ACT.Copy).then_inc(ev["eDQ"], 1)
                    act.wait_ge(ev["pDK"], now(t))
                    act.activation(dqk[:, 8:16, :].rearrange("p a d -> p (a d)"), bank[3][:, :], ACT.Copy).then_inc(ev["eDK"], 1)
                    act.wait_ge(ev["tKV"], now(t))
                    for k in range(KKV):
                        m = act.activation(cT[:, k, :], bank[0][:, k * P:(k + 1) * P], ACT.Copy, scale=cols[:, R_GKV + k:R_GKV + k + 1])
                    m.then_inc(ev["cTk"], 1)
                    act.wait_ge(ev["tQ"], now(t))
                    for k in range(KQ):
                        m = act.activation(cT[:, KKV + k, :], bank[1][:, k * P:(k + 1) * P], ACT.Copy, scale=cols[:, R_GQ + k:R_GQ + k + 1])
                    m.then_inc(ev["cTq"], 1)
                    act.wait_ge(ev["tX0"], now(t))
                    act.wait_ge(ev["tX1"], now(t))
                    modulate()
                    act.wait_ge(ev["uq0"], now(t))
                    act.wait_ge(ev["tN1"], prev(t))
                    act.activation(qf[:, 0:4, :].rearrange("p h d -> p (h d)"), bank[4][:, 0:4 * QK], ACT.Copy).then_inc(ev["qup0"], 1)
                    act.wait_ge(ev["uq1"], now(t))
                    act.activation(qf[:, 4:8, :].rearrange("p h d -> p (h d)"), bank[7][:, 0:4 * QK], ACT.Copy).then_inc(ev["qup1"], 1)
                    act.wait_ge(ev["stored"], prev(t))
                    act.wait_ge(ev["tDQ"], now(t))
                    act.activation(dqT_o.rearrange("p h n -> p (h n)"), bank[0][:, :], ACT.Copy,
                                   scale=SCALE_D).then_inc(ev["dqTo"], 1)
                    act.wait_ge(ev["tN0"], now(t))
                    act.activation(qT_o[0:QK, 0:4, :].rearrange("p h n -> p (h n)"), bank[2][0:QK, :], ACT.Copy, scale=SCALE_M)
                    act.wait_ge(ev["tN1"], now(t))
                    act.activation(qT_o[0:QK, 4:8, :].rearrange("p h n -> p (h n)"), bank[3][0:QK, :], ACT.Copy,
                                   scale=SCALE_M).then_inc(ev["qTo"], 1)

            @block.vector
            def _(v):
                def rstd(count, out, ss, n, eps):
                    v.tensor_scalar(out, ss, 1.0 / n, eps, ALU.mult, ALU.add).then_inc(s_var, 1)
                    v.wait_ge(s_rstd, count)

                def norm_x(link, count):
                    for h in range(2):
                        link(v.tensor_tensor_reduce(rot, xt[:, h * 512:(h + 1) * 512], xt[:, h * 512:(h + 1) * 512], 1.0, 0.0,
                                                    ALU.mult, ALU.add, st1[:, 6 + h:7 + h]))
                    link(v.tensor_tensor(st1[:, 2:3], st1[:, 6:7], st1[:, 7:8], ALU.add))
                    rstd(count, st1[:, 3:4], st1[:, 2:3], D, 1e-6)
                    v.tensor_scalar(xt, xt, st1[:, 3:4], None, ALU.mult).then_inc(ev["xn"], 1)

                def rotate(link, z, out, n, F, lo):
                    ra = rot_a[:, 0:2 * n * F].rearrange("p (g a f) -> p g a f", g=n, a=2)
                    rb = rot_b[:, 0:2 * n * F].rearrange("p (g a f) -> p g a f", g=n, a=2)
                    cw = cs[:, 0:1, lo:lo + F].rearrange("p (g a) f -> p g a f", g=1).broadcast_to((P, n, 2, F))
                    sw = cs[:, 1:2, lo:lo + F].rearrange("p (g a) f -> p g a f", g=1).broadcast_to((P, n, 2, F))
                    link(v.tensor_tensor(ra, z, cw, ALU.mult))
                    link(v.tensor_tensor(rb, z, sw, ALU.mult))
                    link(v.tensor_tensor(out[:, :, 0, :], ra[:, :, 0, :], rb[:, :, 1, :], ALU.subtract))
                    return v.tensor_tensor(out[:, :, 1, :], ra[:, :, 1, :], rb[:, :, 0, :], ALU.add)

                def add_up(link, t, j):
                    v.wait_ge(s_adac, t * (16 * NPART) + 16 * (j + 1))
                    link(v.tensor_scalar(acc[:, j, :], adac[:, 0, :], silu[:, 0:1], None, ALU.mult))
                    for k in range(1, KD):
                        m = v.scalar_tensor_tensor(acc[:, j, :], adac[:, k, :], silu[:, k:k + 1], acc[:, j, :], ALU.mult, ALU.add)
                        if k < KD - 1:
                            link(m)
                    m.then_inc(s_acc, 1)

                PRE, PER = 3, 18 + NPART * (KD - 1)
                v.wait_ge(s_x, 16)
                link = Chain(v, s_v1, 0)
                norm_x(link, 1)
                assert link.done == PRE
                with v.Fori(0, NT) as t:
                    link = Chain(v, s_v1, t * PER + PRE)
                    link(v.tensor_scalar(cs[:, 0:1, :], cos_t[:, bass.ds(t, 1), :], 1.0, None, ALU.mult))
                    link(v.tensor_scalar(cs[:, 1:2, :], sin_t[:, bass.ds(t, 1), :], 1.0, None, ALU.mult))
                    add_up(link, t, 0)
                    v.wait_ge(ev["ssKV"], now(t))
                    rstd(t * 3 + 2, st1[:, 4:5], st1[:, 0:1], KVR, 1e-6)
                    link(v.tensor_scalar(ckn, bank[0][:, 0:KVR], st1[:, 4:5], None, ALU.mult))
                    rotate(link, bank[0][:, KVR:KVR + ROPE].rearrange("p (g a f) -> p g a f", g=1, a=2),
                           kpe.rearrange("p (g a f) -> p g a f", g=1, a=2), 1, FM, 0).then_inc(ev["ckn"], 1)
                    add_up(link, t, 1)
                    v.wait_ge(ev["ssQ"], now(t))
                    rstd(t * 3 + 3, st1[:, 5:6], st1[:, 1:2], QR, 1e-6)
                    v.tensor_scalar(cqn, bank[1][:, 0:QR], st1[:, 5:6], None, ALU.mult).then_inc(ev["cqn"], 1)
                    add_up(link, t, 2)
                    v.wait_ge(s_x, t * 16 + 32)
                    norm_x(link, t * 3 + 4)
                    add_up(link, t, 3)
                    v.wait_ge(ev["pDV"], now(t))
                    v.tensor_scalar(v_d[:, bass.ds(t, 1), :].rearrange("p o n -> p (o n)"), bank[4][:, :], 1.0, None,
                                    ALU.mult).then_inc(ev["vd"], 1)
                    v.wait_ge(ev["eDQ"], now(t))
                    v.wait_ge(ev["eDK"], now(t))
                    z = dqk[:, :, 0:DROPE].rearrange("p g (a f) -> p g a f", a=2)
                    rotate(link, z, z, 16, FD, FM).then_inc(ev["drot"], 1)
                    v.wait_ge(ev["tK1"], prev(t))
                    v.wait_ge(ev["ckn"], now(t))
                    link(v.tensor_copy(kf[:, :, NOPE:QK], kpe.rearrange("p (o f) -> p o f", o=1).broadcast_to((P, HM, ROPE))))
                    for g in range(2):
                        v.wait_ge(ev[f"up{g}"], now(t))
                        kv = bank[2 + g][:, :].rearrange("p (h n) -> p h n", h=4)
                        link(v.tensor_copy(kf[:, 4 * g:4 * g + 4, 0:NOPE], kv[:, :, 0:NOPE]))
                        m = v.tensor_scalar(v_m[:, bass.ds(t, 1), g * 256:(g + 1) * 256].rearrange("p o (h n) -> p (o h) n", h=4),
                                            kv[:, :, NOPE:NOPE + DV_M], 1.0, None, ALU.mult)
                    m.then_inc(ev["kv1"], 1)
                    v.wait_ge(ev["adaM"], now(t))
                    v.tensor_tensor(mods[:, bass.ds(t * NPART + 16, NPART)], bank[7][:, 4 * QK:4 * QK + NPART],
                                    cols[:, bass.ds(t * NPART + (R_BADA + 16), NPART)], ALU.add).then_inc(ev["adaR"], 1)
                    v.wait_ge(ev["qup0"], now(t))
                    v.wait_ge(ev["qup1"], now(t))
                    z = qf[:, :, NOPE:QK].rearrange("p g (a f) -> p g a f", a=2)
                    rotate(link, z, z, HM, FM, 0).then_inc(ev["qfin"], 1)
                    v.wait_ge(ev["tDK"], now(t))
                    v.tensor_scalar(dkT[:, :, bass.ds(t * P, P)], bank[1][:, :].rearrange("p (h n) -> p h n", h=4), 1.0, None,
                                    ALU.mult).then_inc(ev["dkT"], 1)
                    for g in range(2):
                        v.wait_ge(ev[f"tK{g}"], now(t))
                        v.tensor_scalar(kT[0:QK, 4 * g:4 * g + 4, bass.ds(t * P, P)],
                                        bank[5 + g][0:QK, :].rearrange("p (h n) -> p h n", h=4), 1.0, None,
                                        ALU.mult).then_inc(ev[f"kT{g}"], 1)
                    assert link.done == PER, link.done

        at = work
        wout, at = carve(arena, at, KD, D)
        pbuf, at = carve(arena, at, 8 * 512)
        pT, at = carve(arena, at, 2, KD, P)
        qTb, at = carve(arena, at, 2, HM, P)
        dqTb, at = carve(arena, at, 2, HD, P)
        o_sb, at = carve(arena, at, 2, D)
        oT, at = carve(arena, at, KD, P)
        x2, at = carve(arena, at, D)
        x1, at = carve(arena, at, D)
        xh, at = carve(arena, at, D)
        h2T, at = carve(arena, at, KD, P)
        gt1b, at = carve(arena, at, D)
        wr, at = carve(arena, at, KD, NE)
        br, at = carve(arena, at, NE)
        nmax, at = carve(arena, at, 8)
        sums, at = carve(arena, at, 8)
        inv, at = carve(arena, at, 4)
        fac, at = carve(arena, at, 2, 2)
        st2, at = carve(arena, at, 16)
        lg, at = carve(arena, at, NE)
        v8, at = carve(arena, at, 8)
        i8, at = carve(arena, at, 8)
        i8f, at = carve(arena, at, TOPK)
        sq, at = carve(arena, at, HD, P)
        hot, at = carve(arena, at, TOPK, NE)
        chosen, at = carve(arena, at, NE)
        earlier, at = carve(arena, at, NE)
        slot_f, at = carve(arena, at, NE)
        pick, at = carve(arena, at, TOPK, NE)
        w4, at = carve(arena, at, 8)
        s4f, at = carve(arena, at, TOPK)
        slots, at = carve(arena, at, 2, TOPK)
        entry, at = carve(arena, at, 2, TOPK, 2)
        ptab, at = carve(arena, at, 4)
        pp, at = carve(arena, at, 10, NE)
        ps, at = carve(arena, at, 8)
        assert at <= ARENA - kept_free, at
        i8 = i8.bitcast(U32)
        slots = slots.bitcast(I32)
        entry_i, entry_f = entry.bitcast(I32), entry
        ptab = ptab.bitcast(I32)

        steps = attention_plan()
        s_xsq, s_gt1, s_gt1T, s_gt1ev = map(sem, ("s_xsq", "s_gt1", "s_gt1T", "s_gt1ev"))
        PTB = (4, 5)
        (s_w2, s_x2, s_scores, s_max, s_exp, s_mixw, s_T, s_ev4, s_ev5, s_pv, s_oev, s_on, s_m7, s_m7ev, s_x1, s_xh,
         s_st, s_var2, s_rstd2, s_v2, s_top, s_ew, s_chosen, s_slot, s_cnt) = map(sem, (
             "s_w2 s_x2 s_scores s_max s_exp s_mixw s_T s_ev4 s_ev5 s_pv s_oev s_on s_m7 s_m7ev s_x1 s_xh "
             "s_st s_var2 s_rstd2 s_v2 s_top s_ew s_chosen s_slot s_cnt").split())
        s_q = [sem("s_q0"), sem("s_q1")]
        s_scat = [sem("s_scat0"), sem("s_scat1")]
        group_of = {(kind, i, u): g for kind, i, u, g in steps}

        def scores_of(n, lo, hi):
            at_ = 512 * min(slots_of(n, 4))
            return scores[:, at_ + lo:at_ + hi]

        def exps_of(n, lo, hi):
            at_ = 512 * min(slots_of(n, 8))
            return pbuf[:, at_ + lo:at_ + hi]

        def evacuated(eng, g):
            eng.wait_ge((s_ev4, s_ev5)[g % 2], g // 2 + 1)

        with nc.Block() as block:
            @block.sync
            def _(sp):
                for i in range(NT):
                    if i >= 2:
                        sp.wait_ge(s_scores, item(i - 1, 0))
                    sp.dma_start(qTb[0:QK, i % 2].rearrange("p h n -> p (h n)"), q_scr[i, 0:QK]).then_inc(s_q[i % 2], 16)
                    sp.dma_start(dqTb[:, i % 2].rearrange("p h n -> p (h n)"), dq_scr[i]).then_inc(s_q[i % 2], 16)
                    if i == 0:
                        sp.dma_start(wr, w_router[0].rearrange("(k p) n -> p k n", p=P)).then_inc(s_w2, 16)
                        sp.dma_start(br, b_router.broadcast_to((P, NE))).then_inc(s_w2, 16)
                        sp.dma_start(wout, w_out[0].rearrange("(k p) n -> p k n", p=P)).then_inc(s_w2, 16)
                        sp.dma_start(x2, x2d[0:P, :]).then_inc(s_x2, 16)
                    else:
                        sp.wait_ge(s_x1, i)
                        sp.dma_start(x_acc[(i - 1) * P:i * P, :], x1).then_inc(s_st, 16)
                        sp.dma_start(x2, x2d[i * P:(i + 1) * P, :]).then_inc(s_x2, 16)
                        sp.wait_ge(s_xh, i)
                        sp.dma_start(x_hat[(i - 1) * P:i * P, :], xh).then_inc(s_st, 16)
                sp.wait_ge(s_pv, NT * (HM + HD))
                for q in range(NW):
                    sp.dma_start(w_slot[q], w_piece(0, q)).then_inc(s_wd[q], 16)
                sp.wait_ge(s_x1, NT)
                sp.dma_start(x_acc[(NT - 1) * P:S, :], x1).then_inc(s_st, 16)
                sp.wait_ge(s_xh, NT)
                sp.dma_start(x_hat[(NT - 1) * P:S, :], xh).then_inc(s_st, 16)
                for r in range(S, NROW, P):
                    sp.dma_start(x_hat[r:r + P, :], xh).then_inc(s_st, 16)
                    sp.dma_start(x_acc[r:r + P, :], x1).then_inc(s_st, 16)
                sp.wait_ge(s_cnt, 1)
                sp.dma_start(passes, ptab).then_inc(s_st, 16)
                sp.wait_ge(s_st, 32 * (NT + CAP // P) + 16)

            @block.gpsimd
            def _(pool):
                for i in range(NT):
                    for q, cut in enumerate((slice(10, 14), slice(15, 16))):
                        pool.wait_ge(s_var2, 2 * i + q + 1)
                        pool.tensor_tensor(st2[:, cut], st2[:, cut], mhalf[:, 0:cut.stop - cut.start], ALU.pow).then_inc(s_rstd2, 1)
                    pool.wait_ge(s_slot, i + 1)
                    for k in range(TOPK):
                        pool.indirect_dma_start(table, bass.IndirectOffsetOnAxis(ap=slots[:, i % 2, k:k + 1], axis=0),
                                                entry_i[:, i % 2, k, :], None).then_inc(s_scat[i % 2], 16)
                for par in range(2):
                    pool.wait_ge(s_scat[par], 16 * TOPK * NT // 2)

            @block.tensor
            def _(pe):
                oT_group = group_of["oT", 0, 0]

                def group_bank(g):
                    if g >= 2:
                        evacuated(pe, g - 2)
                    return bank[PTB[g % 2]]

                def turn(src, g0):
                    for g in range(2):
                        b = group_bank(g0 + g)
                        for k in range(4):
                            m = pe.transpose(b[:, k * P:(k + 1) * P], src[:, (4 * g + k) * P:(4 * g + k + 1) * P], ident)
                        m.then_inc(s_T, 1)

                def misc(n):
                    if n:
                        pe.wait_ge(s_m7ev, n)
                    return bank[7]

                pe.wait_ge(s_gt1, 1 + KD)
                for h in range(2):
                    m = pe.matmul(bank[6 + h][:, :], ones, x1[:, h * 512:(h + 1) * 512], start=True, stop=True)
                m.then_inc(s_gt1T, 1)
                pe.wait_ge(s_gt1ev, 2)
                for kind, i, u, g0 in steps:
                    kb = i + 1
                    if kind == "S":
                        n = u
                        _, u = unit_of(n)
                        if n % 16 == 0:
                            pe.wait_ge(s_q[i % 2], 32 * (i // 2 + 1))
                        if last_in_slots(n, 4) is not None:
                            pe.wait_ge(s_exp, last_in_slots(n, 4) + 1)
                        for w in range(0, kb * P, 512):
                            hi = min(w + 512, kb * P)
                            if u < HM:
                                m = pe.matmul(scores_of(n, w, hi), qTb[0:QK, i % 2, u, :], kT[0:QK, u, w:hi],
                                              start=True, stop=True)
                            else:
                                half = n - item(i, u)
                                rows_ = slice(half * DH, half * DH + DH)
                                m = pe.matmul(scores_of(n, w, hi), dqTb[rows_, i % 2, u - HM, :], dkT[rows_, u - HM, w:hi],
                                              start=True, stop=True)
                        m.then_inc(s_scores, 1)
                    elif kind == "T":
                        n = item(i, u)
                        if u < HM:
                            pe.wait_ge(s_exp, n + 1)
                        else:
                            pe.wait_ge(s_mixw, HD * i + u - HM + 1)
                        for g in range(0, kb, 4):
                            b = group_bank(g0 + g // 4)
                            for k in range(g, min(g + 4, kb)):
                                m = pe.transpose(b[:, (k - g) * P:(k - g + 1) * P], exps_of(n, k * P, (k + 1) * P), ident)
                            m.then_inc(s_T, 1)
                    elif kind == "PV":
                        U = (HM + HD) * i + u
                        gs = group_of["T", i, u]
                        for g in range(gs, gs + i // 4 + 1):
                            evacuated(pe, g)
                        if U:
                            pe.wait_ge(s_oev, U)
                        for k in range(kb):
                            if u < HM:
                                m = pe.matmul(bank[6][:, 0:DV_M], pT[:, U % 2, k, :],
                                              v_m[:, k, u * DV_M:(u + 1) * DV_M], start=(k == 0), stop=(k == kb - 1))
                            else:
                                m = pe.matmul(bank[6][:, 0:P], pT[:, U % 2, k, :],
                                              v_d[:, k, (u - HM) * P:(u - HM + 1) * P], start=(k == 0), stop=(k == kb - 1))
                        m.then_inc(s_pv, 1)
                    elif kind == "oT":
                        pe.wait_ge(s_on, i + 1)
                        turn(o_sb[:, i % 2, :], g0)
                    elif kind in ("mix0", "mix1"):
                        h = int(kind[-1])
                        if h == 0:
                            for g in range(2):
                                evacuated(pe, group_of["oT", i, 0] + g)
                            pe.wait_ge(s_w2, 48)
                        b = misc(4 * i + h)
                        for k in range(KD):
                            m = pe.matmul(b[:, :], oT[:, k, :], wout[:, k, h * 512:(h + 1) * 512], start=(k == 0), stop=(k == KD - 1))
                        m.then_inc(s_m7, 1)
                    elif kind == "xT":
                        pe.wait_ge(s_xh, i + 1)
                        turn(xh, g0)
                    elif kind == "router":
                        for g in range(2):
                            evacuated(pe, group_of["xT", i, 0] + g)
                        b = misc(4 * i + 2)
                        for k in range(KD):
                            m = pe.matmul(b[:, 0:NE], h2T[:, k, :], wr[:, k, :], start=(k == 0), stop=(k == KD - 1))
                        m.then_inc(s_m7, 1)
                    elif kind == "rank":
                        pe.wait_ge(s_chosen, i + 1)
                        b = misc(4 * i + 3)
                        m = pe.matmul(b[:, 0:NE], before, chosen, start=True, stop=(i == 0))
                        if i:
                            m = pe.matmul(b[:, 0:NE], ones, earlier, start=False, stop=True)
                        m.then_inc(s_m7, 1)
                pe.wait_ge(s_slot, NT)
                b = misc(4 * NT)
                pe.matmul(b[:, 0:NE], ones, earlier, start=True, stop=True).then_inc(s_m7, 1)

            @block.scalar
            def _(act):
                for kind, i, u, g0 in steps:
                    kw = (i + 1) * P
                    if kind == "S":
                        n = u
                        act.wait_ge(s_max, n + 1)
                        if last_in_slots(n, 8) is not None:
                            un = unit_of(last_in_slots(n, 8))
                            act.wait_ge(s_T, group_of["T", un[0], un[1]] + un[0] // 4 + 1)
                        act.activation(exps_of(n, 0, kw), scores_of(n, 0, kw), ACT.Exp, bias=nmax[:, n % 8:n % 8 + 1],
                                       scale=1.0, accum_out=sums[:, n % 8:n % 8 + 1]).then_inc(s_exp, 1)
                    elif kind == "T":
                        U = (HM + HD) * i + u
                        for g in range(g0, g0 + i // 4 + 1):
                            if g % 2 == 0:
                                continue
                            k0, k1 = 4 * (g - g0), min(4 * (g - g0) + 4, i + 1)
                            act.wait_ge(s_T, g + 1)
                            if U >= 2:
                                act.wait_ge(s_pv, U - 1)
                            act.activation(pT[:, U % 2, k0:k1, :].rearrange("p k n -> p (k n)"),
                                           bank[5][:, 0:(k1 - k0) * P], ACT.Copy).then_inc(s_ev5, 1)
                    elif kind in ("oT", "xT"):
                        g = g0 if g0 % 2 else g0 + 1
                        half = g - g0
                        act.wait_ge(s_T, g + 1)
                        for k in range(4 * half, 4 * half + 4):
                            src = bank[5][:, (k % 4) * P:(k % 4 + 1) * P]
                            if kind == "xT":
                                m = act.activation(h2T[:, k, :], src, ACT.Identity, bias=sh2[:, k:k + 1], scale=a2[:, k:k + 1])
                            else:
                                m = act.activation(oT[:, k, :], src, ACT.Copy, scale=gsub if half else 1.0)
                        m.then_inc(s_ev5, 1)
                    elif kind == "mix1":
                        act.wait_ge(s_x1, i + 1)
                        if i:
                            act.wait_ge(s_st, 32 * i)
                        act.activation(xh, x1, ACT.Square, accum_out=st2[:, 14:15]).then_inc(s_xsq, 1)
                    elif kind == "router":
                        act.wait_ge(s_top, i + 1)
                        act.activation(w4[:, 0:TOPK], v8[:, 0:TOPK], ACT.Exp, bias=w4[:, 5:6], scale=1.0,
                                       accum_out=w4[:, 4:5]).then_inc(s_ew, 1)

            @block.vector
            def _(v):
                link = Chain(v, s_v2, 0)
                link(v.memset(earlier, 0.0))
                v.scalar_tensor_tensor(a2, mods[:, 32:40], 1.0, cols[:, R_G2:R_G2 + KD], ALU.add, ALU.mult).then_inc(s_gt1, 1)
                for k in range(KD):
                    v.tensor_scalar(x1[:, k * P:(k + 1) * P], ident, mods[:, 16 + k:17 + k], None, ALU.mult).then_inc(s_gt1, 1)
                v.wait_ge(s_gt1T, 1)
                for h in range(2):
                    v.tensor_copy(gt1b[:, h * 512:(h + 1) * 512], bank[6 + h][:, :]).then_inc(s_gt1ev, 1)
                v.wait_ge(s_gt1ev, 2)

                def mean(out, ss, n, eps):
                    v.tensor_scalar(out, ss, 1.0 / n, eps, ALU.mult, ALU.add).then_inc(s_var2, 1)

                def total(n):
                    return sums[:, n % 8:n % 8 + 1]

                for kind, i, u, g0 in steps:
                    kb = i + 1
                    kw = kb * P
                    if kind == "S":
                        n = u
                        v.wait_ge(s_scores, n + 1)
                        link(v.memset(scores_of(n, kw - CHUNK, kw)[0:CHUNK], MASKED))
                        if n >= 8:
                            v.wait_ge(s_exp, n - 7)
                        v.tensor_reduce(nmax[:, n % 8:n % 8 + 1], scores_of(n, 0, kw), AX_X, ALU.max,
                                        negate=True).then_inc(s_max, 1)
                    elif kind == "W":
                        U = (HM + HD) * i + u
                        n = item(i, u)
                        v.wait_ge(s_exp, n + 2)
                        fl, f = fac[:, U % 2, 0:1], fac[:, U % 2, 1:2]
                        link(v.reciprocal(fl, total(n + 1)))
                        link(v.scalar_tensor_tensor(f, fl, neg_lam, total(n), ALU.mult, ALU.mult))
                        v.scalar_tensor_tensor(exps_of(n, 0, kw), exps_of(n + 1, 0, kw), f, exps_of(n, 0, kw),
                                               ALU.mult, ALU.add).then_inc(s_mixw, 1)
                        link(v.reciprocal(inv[:, U % 4:U % 4 + 1], total(n)))
                    elif kind == "T":
                        U = (HM + HD) * i + u
                        n = item(i, u)
                        if u < HM:
                            v.wait_ge(s_exp, n + 1)
                            link(v.reciprocal(inv[:, U % 4:U % 4 + 1], total(n)))
                        for g in range(g0, g0 + i // 4 + 1):
                            if g % 2:
                                continue
                            k0, k1 = 4 * (g - g0), min(4 * (g - g0) + 4, kb)
                            v.wait_ge(s_T, g + 1)
                            if U >= 2:
                                v.wait_ge(s_pv, U - 1)
                            v.tensor_copy(pT[:, U % 2, k0:k1, :].rearrange("p k n -> p (k n)"),
                                          bank[4][:, 0:(k1 - k0) * P]).then_inc(s_ev4, 1)
                    elif kind == "PV":
                        U = (HM + HD) * i + u
                        v.wait_ge(s_pv, U + 1)
                        if u == 0 and i >= 2:
                            v.wait_ge(s_T, group_of["oT", i - 2, 0] + 2)
                        w = DV_M if u < HM else P
                        lo = u * DV_M if u < HM else HM * DV_M + (u - HM) * P
                        ins = v.tensor_scalar(o_sb[:, i % 2, lo:lo + w], bank[6][:, 0:w],
                                              inv[:, U % 4:U % 4 + 1], None, ALU.mult)
                        ins.then_inc(s_oev, 1)
                    elif kind == "sq":
                        v.wait_ge(s_oev, (HM + HD) * (i + 1))
                        od = o_sb[:, i % 2, HM * DV_M:D].rearrange("p (h n) -> p h n", h=HD)
                        link(v.tensor_tensor(sq, od, od, ALU.mult))
                        link(v.reduce_sum(st2[:, 10:14], sq, AX_X))
                        mean(st2[:, 10:14], st2[:, 10:14], P, 1e-5)
                    elif kind == "headnorm":
                        v.wait_ge(s_rstd2, 2 * i + 1)
                        od = o_sb[:, i % 2, HM * DV_M:D].rearrange("p (h n) -> p h n", h=HD)
                        v.tensor_tensor(od, od, st2[:, 10:14].rearrange("p (h o) -> p h o", o=1).broadcast_to((P, HD, P)),
                                        ALU.mult).then_inc(s_on, 1)
                    elif kind in ("oT", "xT"):
                        g = g0 + g0 % 2
                        half = g - g0
                        v.wait_ge(s_T, g + 1)
                        for k in range(4 * half, 4 * half + 4):
                            src = bank[4][:, (k % 4) * P:(k % 4 + 1) * P]
                            if kind == "xT":
                                m = v.tensor_scalar(h2T[:, k, :], src, a2[:, k:k + 1], sh2[:, k:k + 1], ALU.mult, ALU.add)
                            elif half:
                                m = v.tensor_scalar(oT[:, k, :], src, gsub, None, ALU.mult)
                            else:
                                m = v.tensor_copy(oT[:, k, :], src)
                        m.then_inc(s_ev4, 1)
                    elif kind in ("mix0", "mix1"):
                        h = int(kind[-1])
                        cut = slice(h * 512, (h + 1) * 512)
                        v.wait_ge(s_m7, 4 * i + h + 1)
                        if h == 0:
                            v.wait_ge(s_w2, 48)
                            v.wait_ge(s_x2, 16 * (i + 1))
                            if i:
                                v.wait_ge(s_st, 32 * i)
                        v.tensor_tensor(x1[:, cut], bank[7][:, :], gt1b[:, cut], ALU.mult).then_inc(s_m7ev, 1)
                        v.wait_ge(s_m7ev, 4 * i + h + 1)
                        ins = v.tensor_tensor(x1[:, cut], x1[:, cut], x2[:, cut], ALU.add)
                        if h == 0:
                            link(ins)
                        else:
                            ins.then_inc(s_x1, 1)
                            v.wait_ge(s_xsq, i + 1)
                            mean(st2[:, 15:16], st2[:, 14:15], D, 1e-6)
                    elif kind == "norm":
                        v.wait_ge(s_rstd2, 2 * i + 2)
                        v.tensor_scalar(xh, x1, st2[:, 15:16], None, ALU.mult).then_inc(s_xh, 1)
                    elif kind == "router":
                        v.wait_ge(s_m7, 4 * i + 3)
                        v.tensor_tensor(lg, bank[7][:, 0:NE], br, ALU.add).then_inc(s_m7ev, 1)
                        v.wait_ge(s_m7ev, 4 * i + 3)
                        link(v.max(v8, lg))
                        link(v.max_index(i8, v8, lg))
                        v.tensor_scalar(w4[:, 5:6], v8[:, 0:1], -1.0, None, ALU.mult).then_inc(s_top, 1)
                        link(v.tensor_copy(i8f, i8[:, 0:TOPK]))
                        link(v.tensor_tensor(hot, iota_e.rearrange("p (o n) -> p o n", o=1).broadcast_to((P, TOPK, NE)),
                                             i8f.rearrange("p (k o) -> p k o", o=1).broadcast_to((P, TOPK, NE)), ALU.is_equal))
                        v.reduce_sum(chosen, hot.rearrange("p k n -> p n k"), AX_X).then_inc(s_chosen, 1)
                    elif kind == "rank":
                        v.wait_ge(s_ew, i + 1)
                        if i >= 2:
                            v.wait_ge(s_scat[i % 2], 16 * TOPK * (i // 2))
                        link(v.reciprocal(w4[:, 6:7], w4[:, 4:5]))
                        link(v.tensor_scalar(entry_f[:, i % 2, :, 1], w4[:, 0:TOPK], w4[:, 6:7], None, ALU.mult))
                        link(v.tensor_scalar(s4f, iota_p.broadcast_to((P, TOPK)), float(i * P), None, ALU.add))
                        link(v.tensor_copy(entry_i[:, i % 2, :, 0], s4f))
                    elif kind == "slots":
                        v.wait_ge(s_m7, 4 * i + 4)
                        v.scalar_tensor_tensor(slot_f, iota_e, float(S), bank[7][:, 0:NE], ALU.mult, ALU.add).then_inc(s_m7ev, 1)
                        v.wait_ge(s_m7ev, 4 * i + 4)
                        v.wait_ge(s_chosen, i + 1)
                        link(v.tensor_tensor(earlier, earlier, chosen, ALU.add))
                        link(v.tensor_tensor(pick, hot, slot_f.rearrange("p (o n) -> p o n", o=1).broadcast_to((P, TOPK, NE)),
                                             ALU.mult))
                        link(v.reduce_sum(s4f, pick, AX_X))
                        v.tensor_copy(slots[:, i % 2, :], s4f).then_inc(s_slot, 1)
                cnt, npass, ends, starts, ge, hot_e, tmp = (pp[:, q, :] for q in range(7))
                v.wait_ge(s_m7, 4 * NT + 1)
                link(v.tensor_copy(cnt, bank[7][:, 0:NE]))
                link(v.tensor_scalar(npass, cnt, float(CAP), 1.0, ALU.is_gt, ALU.add))
                for q in range(2, S // CAP):
                    link(v.scalar_tensor_tensor(npass, cnt, float(q * CAP), npass, ALU.is_gt, ALU.add))
                link(v.tensor_tensor_scan(ends, ones[:, 0:NE], npass, 0.0, ALU.mult, ALU.add))
                link(v.tensor_tensor(starts, ends, npass, ALU.subtract))
                link(v.tensor_scalar(ge, starts, iota_p, None, ALU.is_le))
                link(v.reduce_sum(ps[:, 0:1], ge, AX_X))
                link(v.tensor_scalar(ps[:, 0:1], ps[:, 0:1], -1.0, None, ALU.add))
                link(v.tensor_scalar(hot_e, iota_e, ps[:, 0:1], None, ALU.is_equal))
                link(v.tensor_tensor_reduce(tmp, hot_e, starts, 1.0, 0.0, ALU.mult, ALU.add, ps[:, 1:2]))
                link(v.tensor_tensor_reduce(tmp, hot_e, cnt, 1.0, 0.0, ALU.mult, ALU.add, ps[:, 2:3]))
                link(v.tensor_tensor(ps[:, 3:4], iota_p, ps[:, 1:2], ALU.subtract))
                link(v.tensor_scalar(ps[:, 3:4], ps[:, 3:4], float(S // CAP - 1), float(CAP), ALU.min, ALU.mult))
                link(v.tensor_tensor(ps[:, 4:5], ps[:, 2:3], ps[:, 3:4], ALU.subtract))
                link(v.scalar_tensor_tensor(ps[:, 5:6], ps[:, 0:1], float(S), ps[:, 3:4], ALU.mult, ALU.add))
                link(v.tensor_copy(ptab[:, 0:1], ps[:, 0:1]))
                link(v.tensor_copy(ptab[:, 1:2], ps[:, 5:6]))
                link(v.tensor_copy(ptab[:, 2:3], ps[:, 4:5]))
                v.tensor_copy(ptab[:, 3:4], ends[:, NE - 1:NE]).then_inc(s_cnt, 1)

        at = work
        xg, at = carve(arena, at, 2, D)
        xT, at = carve(arena, at, KD, CAP)
        actT, at = carve(arena, at, KD, CAP)
        yT, at = carve(arena, at, KD, CAP)
        y, at = carve(arena, at, 2, D)
        bias_e, at = carve(arena, at, 3, NE * KD)
        bc, at = carve(arena, at, 3, KD)
        gate_t, at = carve(arena, at, CAP)
        up_t, at = carve(arena, at, CAP)
        sig_t, at = carve(arena, at, CAP)
        idx_g, at = carve(arena, at, 2, 2)
        idx_s, at = carve(arena, at, 2, 2)
        prow, at = carve(arena, at, NPASS_ROWS, 4)
        assert at <= ARENA - kept_free, at
        prow = prow.bitcast(I32)
        s_prow = sem("s_prow")
        idx_g, idx_s, wgt = idx_g.bitcast(I32), idx_s.bitcast(I32), idx_s

        (s_gx, s_xte, s_gu, s_gev, s_gate, s_sigd, s_actd, s_yt, s_yev, s_ytr, s_ye, s_yfree,
         s_is, s_ig, s_sc, s_be, s_tr, s_v3, s_go) = map(sem, (
             "s_gx s_xte s_gu s_gev s_gate s_sigd s_actd s_yt s_yev s_ytr s_ye s_yfree "
             "s_is s_ig s_sc s_be s_tr s_v3 s_go").split())

        def pass_value(eng, i, col, hi):
            at_ = prow[0:1, bass.ds(i, 1), col:col + 1] if not isinstance(i, int) else prow[0:1, i:i + 1, col:col + 1]
            return eng.value_load(at_.rearrange("a b c -> a (b c)"), min_val=0, max_val=hi)

        def n_passes(eng):
            eng.wait_ge(s_prow, 16)
            return eng.value_load(prow[0:1, 0, 3:4], min_val=NE, max_val=MAXPASS)

        def by_size(eng, tokens, body, sizes=SIZES):
            if len(sizes) == 1:
                body(sizes[0])
                return
            low, high = sizes[:(len(sizes) + 1) // 2], sizes[(len(sizes) + 1) // 2:]
            with eng.If(tokens <= low[-1]):
                by_size(eng, tokens, body, low)
            with eng.Else():
                by_size(eng, tokens, body, high)

        with nc.Block() as block:
            @block.sync
            def _(sp):
                sp.dma_start(prow[0:1].rearrange("o a b -> o (a b)"),
                             passes.rearrange("a b -> (a b)").rearrange("(o n) -> o n", o=1)).then_inc(s_prow, 16)
                sp.dma_start(bias_e.rearrange("p a n -> p (a n)"), bias_scr).then_inc(s_be, 16)
                T = n_passes(sp)
                with sp.Fori(1, T) as i:
                    e = pass_value(sp, i, 0, NE - 1)
                    for q in range(NW):
                        if q < NJ:
                            sp.wait_ge(s_gu, i * 8 + q + 1)
                        else:
                            sp.wait_ge(s_yt, i * 8 + 2 * (q - NJ) + 2)
                        sp.dma_start(w_slot[q], w_piece(e, q)).then_inc(s_wd[q], 16)

            @block.gpsimd
            def _(pool):
                def rows_of(i, dst, sem_):
                    r0 = pass_value(pool, i, 1, NE * S - CAP)
                    pool.dma_start(dst, table[bass.ds(r0, CAP), :].rearrange("(b p) w -> p b w", p=P)).then_inc(sem_, 16)

                def gather():
                    for b in range(2):
                        pool.indirect_dma_start(xg[:, b, :], None, x_hat,
                                                bass.IndirectOffsetOnAxis(ap=idx_g[:, b, 0:1], axis=0)).then_inc(s_gx, 16)

                pool.sem_inc(s_gu, 8)
                pool.sem_inc(s_yt, 8)
                pool.sem_inc(s_gev, 8)
                pool.sem_inc(s_yev, 8)
                pool.sem_inc(s_ye, 4)
                pool.dma_start(idx_g, table[0:CAP, :].rearrange("(b p) w -> p b w", p=P)).then_inc(s_ig, 16)
                T = n_passes(pool)
                pool.wait_ge(s_ig, 16)
                gather()
                with pool.Fori(0, T) as i:
                    rows_of(i, idx_s, s_is)
                    pool.wait_ge(s_gx, i * 32 + 32)
                    pool.sem_inc(s_go, 1)
                    rows_of(i + 1, idx_g, s_ig)
                    pool.wait_ge(s_ig, i * 16 + 32)
                    pool.wait_ge(s_tr, i * 4 + 4)
                    pool.sem_inc(s_go, 1)
                    gather()
                    pool.wait_ge(s_is, i * 16 + 16)
                    pool.wait_ge(s_ye, i * 4 + 8)
                    pool.sem_inc(s_go, 1)
                    for b in range(2):
                        pool.indirect_dma_start(x_acc, bass.IndirectOffsetOnAxis(ap=idx_s[:, b, 0:1], axis=0),
                                                y[:, b, :], None, compute_op=ALU.add).then_inc(s_sc, 16)
                    pool.wait_ge(s_sc, i * 32 + 32)
                    pool.sem_inc(s_yfree, 1)
                pool.wait_ge(s_gx, T * 32 + 32)

            @block.tensor
            def _(pe):
                def load_tokens(reg, i):
                    pe.reg_load(reg, prow[0:1, bass.ds(i, 1) if not isinstance(i, int) else slice(i, i + 1), 2:3]
                                .rearrange("a b c -> a (b c)"))

                def turn_x(g):
                    for kk in range(2):
                        for b in range(2):
                            m = pe.transpose(bank[g][:, (2 * kk + b) * P:(2 * kk + b + 1) * P],
                                             xg[:, b, (2 * g + kk) * P:(2 * g + kk + 1) * P], ident)
                    m.then_inc(s_tr, 1)

                T = n_passes(pe)
                ahead = pe.alloc_register()
                load_tokens(ahead, 0)
                pe.wait_ge(s_gx, 32)
                for g in range(4):
                    turn_x(g)
                with pe.Fori(0, T) as i:
                    tokens = pe.snap(ahead, min_val=0, max_val=S)

                    def body(N):
                        for j in range(KD):
                            pe.wait_ge(s_wd[j], i * 16 + 16)
                            if j >= 4:
                                pe.wait_ge(s_gev, i * 8 + j + 5)
                            for half in range(2):
                                for k in range(KD):
                                    if j == 0 and half == 0 and k % 2 == 0:
                                        pe.wait_ge(s_xte, i * 4 + k // 2 + 1)
                                    m = pe.matmul(bank[j % 4][:, half * 256:half * 256 + N], w_slot[j][:, k, half::2],
                                                  xT[:, k, 0:N], start=(k == 0), stop=(k == KD - 1))
                            m.then_inc(s_gu, 1)
                        pe.wait_ge(s_gx, i * 32 + 64)
                        for g in range(3):
                            pe.wait_ge(s_gev, i * 8 + g + 13)
                            turn_x(g)
                        for m_ in range(KD):
                            q = NJ + m_ // 2
                            pe.wait_ge(s_wd[q], i * 16 + 16)
                            pe.wait_ge(s_yev, i * 8 + m_ + 7)
                            for k in range(KD):
                                if m_ == 0:
                                    pe.wait_ge(s_actd, i * 8 + k + 1)
                                m = pe.matmul(bank[4 + m_ % 2][:, 0:N], w_slot[q][:, k, (m_ % 2) * P:(m_ % 2 + 1) * P],
                                              actT[:, k, 0:N], start=(k == 0), stop=(k == KD - 1))
                            m.then_inc(s_yt, 1)
                            if m_ == 5:
                                turn_y(i, 0, N)
                        load_tokens(ahead, i + 1)
                        pe.wait_ge(s_gev, i * 8 + 16)
                        turn_x(3)
                        turn_y(i, 1, N)

                    def turn_y(i, half, N):
                        pe.wait_ge(s_yev, i * 8 + 8 + 4 * half + 4)
                        nb = 2 if N > P else 1
                        for b in range(nb):
                            g = 2 * half + b
                            pe.wait_ge(s_ye, i * 4 + g + 3)
                            for k in range(4):
                                m = pe.transpose(bank[6 + g % 2][:, k * P:(k + 1) * P],
                                                 yT[:, 4 * half + k, b * P:(b + 1) * P], ident)
                            m.then_inc(s_ytr, 2 // nb)

                    by_size(pe, tokens, body)

            @block.scalar
            def _(act):
                def take_x(i, first, groups):
                    for g in groups:
                        act.wait_ge(s_tr, g + 1 if first else i * 4 + g + 1)
                        for kk in range(2):
                            k = 2 * g + kk
                            m = act.activation(xT[:, k, :], bank[g][:, kk * CAP:(kk + 1) * CAP], ACT.Identity,
                                               bias=sh2[:, k:k + 1], scale=a2[:, k:k + 1])
                        m.then_inc(s_xte, 1)

                take_x(0, True, range(4))
                T = n_passes(act)
                with act.Fori(0, T) as i:
                    tokens = pass_value(act, i, 2, S)

                    def body(N):
                        for j in range(KD):
                            act.wait_ge(s_gate, i * 8 + j + 1)
                            act.activation(sig_t[:, 0:N], gate_t[:, 0:N], ACT.Sigmoid, scale=SWISH).then_inc(s_sigd, 1)

                        take_x(i + 1, False, range(3))
                        act.wait_ge(s_is, i * 16 + 16)
                        act.wait_ge(s_yfree, i + 1)
                        nb = 2 if N > P else 1
                        for half in range(2):
                            if half:
                                take_x(i + 1, False, (3,))
                            for b in range(nb):
                                act.wait_ge(s_ytr, i * 4 + 2 * half + b + 1)
                                act.activation(y[:, b, half * 512:(half + 1) * 512], bank[6 + b][:, :], ACT.Copy,
                                               scale=wgt[:, b, 1:2]).then_inc(s_ye, 2 // nb)

                    by_size(act, tokens, body)

            @block.vector
            def _(v):
                PER = 1 + KD
                v.memset(yT, 0.0)
                v.memset(y[:, 1, :], 0.0).then_inc(s_yfree, 1)
                v.wait_ge(s_be, 16)
                T = n_passes(v)
                with v.Fori(0, T) as i:
                    e = pass_value(v, i, 0, NE - 1)
                    tokens = pass_value(v, i, 2, S)
                    link = Chain(v, s_v3, i * PER)
                    v.wait_ge(s_yev, i * 8 + 8)
                    v.tensor_scalar(bc, bias_e[:, :, bass.ds(e * KD, KD)], 1.0, None, ALU.mult).then_inc(s_v3, 1)

                    def body(N):
                        link.done = 1
                        v.wait_ge(s_v3, i * PER + 1)
                        for j in range(KD):
                            v.wait_ge(s_gu, i * 8 + j + 9)
                            b = bank[j % 4]
                            v.tensor_scalar(gate_t[:, 0:N], b[:, 0:N], bc[:, 0, j:j + 1], LIMIT, ALU.add, ALU.min).then_inc(s_gate, 1)
                            v.tensor_scalar(up_t[:, 0:N], b[:, 256:256 + N], bc[:, 1, j:j + 1], 1.0 + LIMIT,
                                            ALU.add, ALU.min).then_inc(s_gev, 1)
                            v.wait_ge(s_gate, i * 8 + j + 1)
                            v.wait_ge(s_gev, i * 8 + j + 9)
                            link(v.scalar_tensor_tensor(up_t[:, 0:N], up_t[:, 0:N], 1.0 - LIMIT, gate_t[:, 0:N], ALU.max, ALU.mult))
                            v.wait_ge(s_sigd, i * 8 + j + 1)
                            v.tensor_tensor(actT[:, j, 0:N], up_t[:, 0:N], sig_t[:, 0:N], ALU.mult).then_inc(s_actd, 1)
                            v.wait_ge(s_actd, i * 8 + j + 1)
                        for m_ in range(KD):
                            v.wait_ge(s_yt, i * 8 + m_ + 9)
                            v.tensor_scalar(yT[:, m_, 0:N], bank[4 + m_ % 2][:, 0:N], bc[:, 2, m_:m_ + 1], gt2[:, m_:m_ + 1],
                                            ALU.add, ALU.mult).then_inc(s_yev, 1)
                        assert link.done == 1 + KD

                    by_size(v, tokens, body)

        at = base
        gfb, at = carve(arena, at, D)
        fin, at = carve(arena, at, NT, D)
        sq, at = carve(arena, at, D)
        fs, at = carve(arena, at, 2, NT)
        s_fin = [sem(f"s_fin{i}") for i in range(NT)]
        s_var4, s_rstd4 = sem("s_var4"), sem("s_rstd4")
        s_gf, s_sq4, s_res, s_out = map(sem, ("s_gf", "s_sq4", "s_res", "s_out"))

        with nc.Block() as block:
            @block.sync
            def _(sp):
                sp.dma_start(gfb, g_final.rearrange("(o d) -> o d", o=1).broadcast_to((P, D))).then_inc(s_gf, 16)
                for i in range(NT):
                    sp.dma_start(fin[:, i, :], x_acc[i * P:(i + 1) * P, :]).then_inc(s_fin[i], 16)
                for i in range(NT):
                    sp.wait_ge(s_res, i + 1)
                    sp.dma_start(out2d[i * P:(i + 1) * P, :], fin[:, i, :]).then_inc(s_out, 16)
                sp.wait_ge(s_out, 16 * NT)

            @block.gpsimd
            def _(pool):
                for i in range(NT):
                    pool.wait_ge(s_var4, i + 1)
                    pool.tensor_tensor(fs[:, 1, i:i + 1], fs[:, 1, i:i + 1], mhalf[:, 0:1], ALU.pow).then_inc(s_rstd4, 1)

            @block.scalar
            def _(act):
                for i in range(NT):
                    act.wait_ge(s_fin[i], 16)
                    if i:
                        act.wait_ge(s_sq4, i)
                    act.activation(sq, fin[:, i, :], ACT.Square, accum_out=fs[:, 0, i:i + 1]).then_inc(s_sq4, 1)

            @block.vector
            def _(v):
                def mean(i):
                    v.wait_ge(s_sq4, i + 1)
                    v.tensor_scalar(fs[:, 1, i:i + 1], fs[:, 0, i:i + 1], 1.0 / D, 1e-6, ALU.mult, ALU.add).then_inc(s_var4, 1)

                v.wait_ge(s_gf, 16)
                mean(0)
                for i in range(NT):
                    if i + 1 < NT:
                        mean(i + 1)
                    v.wait_ge(s_rstd4, i + 1)
                    v.scalar_tensor_tensor(fin[:, i, :], fin[:, i, :], fs[:, 1, i:i + 1], gfb, ALU.mult, ALU.mult).then_inc(s_res, 1)


_INS = ["x", "c", "positions", "w_ada", "b_ada", "g_norm1", "w_in", "g_q_norm", "w_uq", "g_kv_norm", "w_ukv",
        "lambda_q1", "lambda_k1", "lambda_q2", "lambda_k2", "g_subln", "w_out", "g_norm2", "w_router", "b_router",
        "w_gate_up", "b_gate_up", "w_down", "b_down", "g_final"]
_OUTS = [((1, S, D), "float32")]


def kernel(**inputs):
    import numpy as _np
    import concourse.bacc as _bacc
    from concourse import mybir as _mybir
    from concourse.bass_utils import run_bass_kernel_spmd as _run

    nc = _bacc.Bacc("TRN2", target_bir_lowering=False, num_devices=1)
    arrays, args = {}, []
    for name in _INS:
        a = _np.ascontiguousarray(inputs[name])
        arrays[f"in_{name}_dram"] = a
        args.append(nc.dram_tensor(f"in_{name}_dram", a.shape, _mybir.dt.from_np(a.dtype), kind="ExternalInput").ap())
    for i, (shape, dtype) in enumerate(_OUTS):
        dt = _mybir.dt.from_np(_np.dtype(dtype))
        args.append(nc.dram_tensor(f"out_{i}_dram", shape, dt, kind="ExternalOutput").ap())
    hybrid_block(nc, *args)
    r = _run(nc, [arrays], core_ids=[0])
    return r.results[0]["out_0_dram"]
```
